# Optimizing a Trainium2 kernel written in Bass

```python
import jax, jax.numpy as jnp
from jax import lax
import numpy as np

D_MODEL = 1024
BATCH = 1
SEQ = 1024
DEPTH = 1
DEC_BATCH = 8
DEC_SEQ = 8
PAST_LEN = 2048
PAGE_SIZE = 128

N_HEADS = 8
QK_NOPE = 64
QK_ROPE = 32
V_HEAD = 64
Q_LORA = 384
KV_LORA = 256
D_ATTN = N_HEADS * V_HEAD
D_CONV = D_MODEL // 2
CONV_WIDTH = 31
D_MIX = D_ATTN + D_CONV
D_IN = Q_LORA + KV_LORA + QK_ROPE + 2 * D_CONV
N_MEM = 256
X_HEADS = 4
X_HEAD_DIM = D_MODEL // X_HEADS
D_FF = 2816
FFN_CONV_WIDTH = 3

ROPE_THETA = 10000.0
EPS = 1e-6
Q_BLOCK = 128
NEG_INF = -1e30
ATTN_SCALE = (QK_NOPE + QK_ROPE) ** -0.5
X_SCALE = X_HEAD_DIM ** -0.5

kernel_name = 'hymba_mla_conformer_memxattn_convglu_step'

def rms_norm(x, g):
    xf = x.astype(jnp.float32)
    y = xf * lax.rsqrt(jnp.mean(xf * xf, axis=-1, keepdims=True) + EPS)
    return (y * g.astype(jnp.float32)).astype(x.dtype)

def layer_norm(x, g, b):
    xf = x.astype(jnp.float32)
    xc = xf - jnp.mean(xf, axis=-1, keepdims=True)
    var = jnp.mean(xc * xc, axis=-1, keepdims=True)
    return (xc * lax.rsqrt(var + EPS) * g.astype(jnp.float32) + b.astype(jnp.float32)).astype(x.dtype)

def rope(x, pos):
    half = x.shape[-1] // 2
    inv = ROPE_THETA ** (-jnp.arange(half, dtype=jnp.float32) / half)
    ang = pos.astype(jnp.float32)[:, None] * inv[None, :]
    ang = ang.reshape(ang.shape[:1] + (1,) * (x.ndim - 3) + (half,))
    cos, sin = jnp.cos(ang), jnp.sin(ang)
    xf = x.astype(jnp.float32)
    x1, x2 = xf[..., :half], xf[..., half:]
    return jnp.concatenate([x1 * cos - x2 * sin, x2 * cos + x1 * sin], axis=-1).astype(x.dtype)

def causal_dwconv(u, buf, w, b):
    full = jnp.concatenate([buf, u], axis=1)
    y = lax.conv_general_dilated(full, w[:, None, :], window_strides=(1,), padding='VALID',
                                 dimension_numbers=('NWC', 'WIO', 'NWC'),
                                 feature_group_count=u.shape[-1]) + b
    return y, full[:, full.shape[1] - buf.shape[1]:]

def mla_attend(q_lat, q_pe, c_keys, pe_keys, q_pos):
    B, S, H, L = q_lat.shape
    T = c_keys.shape[1]
    qb = Q_BLOCK if S % Q_BLOCK == 0 else S
    nb = S // qb
    k_pos = jnp.arange(T, dtype=jnp.int32)

    def block(args):
        ql, qp, pos = args
        s = (jnp.einsum('bqhl,btl->bhqt', ql, c_keys, preferred_element_type=jnp.float32)
             + jnp.einsum('bqhr,btr->bhqt', qp, pe_keys, preferred_element_type=jnp.float32)) * ATTN_SCALE
        s = jnp.where(pos[:, None] >= k_pos[None, :], s, NEG_INF)
        pr = jax.nn.softmax(s, axis=-1).astype(c_keys.dtype)
        return jnp.einsum('bhqt,btl->bqhl', pr, c_keys)

    to_blocks = lambda a: jnp.swapaxes(a.reshape((B, nb, qb) + a.shape[2:]), 0, 1)
    out = lax.map(block, (to_blocks(q_lat), to_blocks(q_pe), q_pos.reshape(nb, qb)))
    return jnp.swapaxes(out, 0, 1).reshape(B, S, H, L)

def token_mixer(h, pos, past_c, past_pe, conv_buf, p):
    B, S, _ = h.shape
    proj = h @ p['w_in']
    cuts = [Q_LORA, Q_LORA + KV_LORA, Q_LORA + KV_LORA + QK_ROPE, Q_LORA + KV_LORA + QK_ROPE + D_CONV]
    q_a, c_raw, pe_raw, glu_a, glu_b = jnp.split(proj, cuts, axis=-1)
    q = (rms_norm(q_a, p['g_q_a']) @ p['w_q_b']).reshape(B, S, N_HEADS, QK_NOPE + QK_ROPE)
    q_nope, q_pe = q[..., :QK_NOPE], rope(q[..., QK_NOPE:], pos)
    c_new = rms_norm(c_raw, p['g_kv_a'])
    pe_new = rope(pe_raw, pos)
    q_lat = jnp.einsum('bshn,lhn->bshl', q_nope, p['w_uk'])
    if past_c is None:
        c_keys, pe_keys = c_new, pe_new
    else:
        c_keys = jnp.concatenate([past_c, c_new], axis=1)
        pe_keys = jnp.concatenate([past_pe, pe_new], axis=1)
    o_lat = mla_attend(q_lat, q_pe, c_keys, pe_keys, pos)
    attn = jnp.einsum('bshl,lhv->bshv', o_lat, p['w_uv']).reshape(B, S, D_ATTN)
    u = glu_a * jax.nn.sigmoid(glu_b)
    cv, new_buf = causal_dwconv(u, conv_buf, p['w_dw'], p['b_dw'])
    cv = jax.nn.silu(layer_norm(cv, p['g_cln'], p['b_cln']))
    out = jnp.concatenate([attn, cv], axis=-1) @ p['w_out']
    return out, c_new, pe_new, new_buf

def mem_kv(mem, p):
    B, N, _ = mem.shape
    m = rms_norm(mem, p['g_mem'])
    k = (m @ p['w_xk']).reshape(B, N, X_HEADS, X_HEAD_DIM)
    v = (m @ p['w_xv']).reshape(B, N, X_HEADS, X_HEAD_DIM)
    return k, v

def cross_attend(h, mem_k, mem_v, p):
    B, S, _ = h.shape
    q = (h @ p['w_xq']).reshape(B, S, X_HEADS, X_HEAD_DIM)
    s = jnp.einsum('bshd,bnhd->bhsn', q, mem_k, preferred_element_type=jnp.float32) * X_SCALE
    pr = jax.nn.softmax(s, axis=-1).astype(mem_v.dtype)
    o = jnp.einsum('bhsn,bnhd->bshd', pr, mem_v).reshape(B, S, X_HEADS * X_HEAD_DIM)
    return o @ p['w_xo']

def conv_glu_ffn(h, buf, p):
    val, gate = jnp.split(h @ p['w_up'], 2, axis=-1)
    gate, new_buf = causal_dwconv(gate, buf, p['w_fdw'], p['b_fdw'])
    return (jax.nn.silu(gate) * val) @ p['w_down'], new_buf

def layer(x, pos, past_c, past_pe, conv_buf, ffn_buf, mem_k, mem_v, p):
    m, c_new, pe_new, conv_new = token_mixer(rms_norm(x, p['g_pre_mix']), pos, past_c, past_pe, conv_buf, p)
    x = x + rms_norm(m, p['g_post_mix'])
    xa = cross_attend(rms_norm(x, p['g_pre_x']), mem_k, mem_v, p)
    x = x + rms_norm(xa, p['g_post_x'])
    f, ffn_new = conv_glu_ffn(rms_norm(x, p['g_pre_ffn']), ffn_buf, p)
    x = x + rms_norm(f, p['g_post_ffn'])
    return x, c_new, pe_new, conv_new, ffn_new

def setup_inputs(seed: int = 0) -> dict:
    key = jax.random.key(seed)
    keys = iter(jax.random.split(key, 48))
    nk = lambda: next(keys)
    normal = lambda shape, scale: jax.random.normal(nk(), shape, jnp.float32) * scale
    w = lambda shape, fan_in: normal((DEPTH,) + shape, fan_in ** -0.5)
    gain = lambda n: 1.0 + normal((DEPTH, n), 0.05)
    bias = lambda n: normal((DEPTH, n), 0.01)

    n_pages = PAST_LEN // PAGE_SIZE
    n_used = DEC_BATCH * n_pages
    n_phys = n_used + n_used // 4
    perm = jax.random.permutation(nk(), n_phys)
    page_table = perm[:n_used].reshape(DEC_BATCH, n_pages).astype(jnp.int32)

    return {
        'x_prompt': normal((BATCH, SEQ, D_MODEL), 1.0),
        'x_sample': normal((DEC_BATCH, DEC_SEQ, D_MODEL), 1.0),
        'cache_kv_latent': normal((DEPTH, n_phys, PAGE_SIZE, KV_LORA), 1.0),
        'cache_k_rope': normal((DEPTH, n_phys, PAGE_SIZE, QK_ROPE), 1.0),
        'cache_mem_k': normal((DEPTH, DEC_BATCH, N_MEM, X_HEADS, X_HEAD_DIM), 1.0),
        'cache_mem_v': normal((DEPTH, DEC_BATCH, N_MEM, X_HEADS, X_HEAD_DIM), 1.0),
        'state_conv': normal((DEPTH, DEC_BATCH, CONV_WIDTH - 1, D_CONV), 0.5),
        'state_ffn_conv': normal((DEPTH, DEC_BATCH, FFN_CONV_WIDTH - 1, D_FF), 1.0),
        'page_table': page_table,
        'mem_prompt': normal((BATCH, N_MEM, D_MODEL), 1.0),
        'w_in': w((D_MODEL, D_IN), D_MODEL),
        'g_q_a': gain(Q_LORA),
        'w_q_b': w((Q_LORA, N_HEADS * (QK_NOPE + QK_ROPE)), Q_LORA),
        'g_kv_a': gain(KV_LORA),
        'w_uk': w((KV_LORA, N_HEADS, QK_NOPE), KV_LORA),
        'w_uv': w((KV_LORA, N_HEADS, V_HEAD), KV_LORA),
        'w_dw': w((CONV_WIDTH, D_CONV), CONV_WIDTH),
        'b_dw': bias(D_CONV),
        'g_cln': gain(D_CONV),
        'b_cln': bias(D_CONV),
        'w_out': w((D_MIX, D_MODEL), D_MIX),
        'g_mem': gain(D_MODEL),
        'w_xq': w((D_MODEL, X_HEADS * X_HEAD_DIM), D_MODEL),
        'w_xk': w((D_MODEL, X_HEADS * X_HEAD_DIM), D_MODEL),
        'w_xv': w((D_MODEL, X_HEADS * X_HEAD_DIM), D_MODEL),
        'w_xo': w((X_HEADS * X_HEAD_DIM, D_MODEL), X_HEADS * X_HEAD_DIM),
        'w_up': w((D_MODEL, 2 * D_FF), D_MODEL),
        'w_fdw': w((FFN_CONV_WIDTH, D_FF), FFN_CONV_WIDTH),
        'b_fdw': bias(D_FF),
        'w_down': w((D_FF, D_MODEL), D_FF),
        'g_pre_mix': gain(D_MODEL),
        'g_post_mix': gain(D_MODEL),
        'g_pre_x': gain(D_MODEL),
        'g_post_x': gain(D_MODEL),
        'g_pre_ffn': gain(D_MODEL),
        'g_post_ffn': gain(D_MODEL),
    }

def reference(x_prompt, x_sample, cache_kv_latent, cache_k_rope, cache_mem_k, cache_mem_v,
              state_conv, state_ffn_conv, page_table, mem_prompt,
              w_in, g_q_a, w_q_b, g_kv_a, w_uk, w_uv, w_dw, b_dw, g_cln, b_cln, w_out,
              g_mem, w_xq, w_xk, w_xv, w_xo, w_up, w_fdw, b_fdw, w_down,
              g_pre_mix, g_post_mix, g_pre_x, g_post_x, g_pre_ffn, g_post_ffn):
    B, S = x_prompt.shape[0], x_prompt.shape[1]
    DB, DS = x_sample.shape[0], x_sample.shape[1]
    n_past = page_table.shape[1] * PAGE_SIZE
    pos_p = jnp.arange(S, dtype=jnp.int32)
    pos_s = PAST_LEN + jnp.arange(DS, dtype=jnp.int32)
    yp, ys = x_prompt, x_sample
    c_p_l, pe_p_l, cb_p_l, fb_p_l, mk_p_l, mv_p_l = [], [], [], [], [], []
    c_s_l, pe_s_l, cb_s_l, fb_s_l = [], [], [], []
    for l in range(DEPTH):
        p = {
            'w_in': w_in[l], 'g_q_a': g_q_a[l], 'w_q_b': w_q_b[l], 'g_kv_a': g_kv_a[l],
            'w_uk': w_uk[l], 'w_uv': w_uv[l], 'w_dw': w_dw[l], 'b_dw': b_dw[l],
            'g_cln': g_cln[l], 'b_cln': b_cln[l], 'w_out': w_out[l],
            'g_mem': g_mem[l], 'w_xq': w_xq[l], 'w_xk': w_xk[l], 'w_xv': w_xv[l], 'w_xo': w_xo[l],
            'w_up': w_up[l], 'w_fdw': w_fdw[l], 'b_fdw': b_fdw[l], 'w_down': w_down[l],
            'g_pre_mix': g_pre_mix[l], 'g_post_mix': g_post_mix[l],
            'g_pre_x': g_pre_x[l], 'g_post_x': g_post_x[l],
            'g_pre_ffn': g_pre_ffn[l], 'g_post_ffn': g_post_ffn[l],
        }
        mk_p, mv_p = mem_kv(mem_prompt, p)
        yp, c_p, pe_p, cb_p, fb_p = layer(
            yp, pos_p, None, None,
            jnp.zeros((B, CONV_WIDTH - 1, D_CONV), yp.dtype),
            jnp.zeros((B, FFN_CONV_WIDTH - 1, D_FF), yp.dtype),
            mk_p, mv_p, p)
        past_c = cache_kv_latent[l][page_table].reshape(DB, n_past, KV_LORA)
        past_pe = cache_k_rope[l][page_table].reshape(DB, n_past, QK_ROPE)
        ys, c_s, pe_s, cb_s, fb_s = layer(
            ys, pos_s, past_c, past_pe, state_conv[l], state_ffn_conv[l],
            cache_mem_k[l], cache_mem_v[l], p)
        c_p_l.append(c_p); pe_p_l.append(pe_p); cb_p_l.append(cb_p); fb_p_l.append(fb_p)
        mk_p_l.append(mk_p); mv_p_l.append(mv_p)
        c_s_l.append(c_s); pe_s_l.append(pe_s); cb_s_l.append(cb_s); fb_s_l.append(fb_s)
    kv_latent_prompt = jnp.stack(c_p_l)
    k_rope_prompt = jnp.stack(pe_p_l)
    conv_state_prompt = jnp.stack(cb_p_l)
    ffn_state_prompt = jnp.stack(fb_p_l)
    mem_k_prompt = jnp.stack(mk_p_l)
    mem_v_prompt = jnp.stack(mv_p_l)
    kv_latent_sample = jnp.stack(c_s_l)
    k_rope_sample = jnp.stack(pe_s_l)
    conv_state_sample = jnp.stack(cb_s_l)
    ffn_state_sample = jnp.stack(fb_s_l)
    return (yp, ys, kv_latent_prompt, k_rope_prompt, conv_state_prompt, ffn_state_prompt,
            mem_k_prompt, mem_v_prompt, kv_latent_sample, k_rope_sample, conv_state_sample,
            ffn_state_sample)


_drawn_inputs = setup_inputs


def setup_inputs(seed=0):
    import zlib

    import numpy as np

    out = dict(_drawn_inputs(seed))
    spreads = {}
    factors = {'g_q_a': 7.628, 'b_dw': 3.581, 'b_cln': 7.366, 'b_fdw': 8.0}
    for name, (base, spread) in spreads.items():
        noise = np.random.default_rng([zlib.crc32(name.encode()), seed]).standard_normal(out[name].shape)
        drawn = base * np.exp(spread * noise) if base else spread * noise
        out[name] = __import__('jax').numpy.asarray(drawn.astype(out[name].dtype))
    for name, factor in factors.items():
        out[name] = (out[name] * factor).astype(out[name].dtype)
    return out
```

```python
from contextlib import ExitStack

import concourse.bass as bass
from concourse import mybir

P = 128
F32 = mybir.dt.float32
I32 = mybir.dt.int32
ALU = mybir.AluOpType
ACT = mybir.ActivationFunctionType
AX_X = mybir.AxisListType.X

D_MODEL, SEQ, DEC_B, DEC_S = 1024, 1024, 8, 8
PAST, PAGE = 2048, 128
HEADS, NOPE, ROPE, VH = 8, 64, 32, 64
Q_LORA, KV_LORA, D_CONV, CONV_W = 384, 256, 512, 31
XH, XD, N_MEM = 4, 256, 256
D_FF, FFN_W = 2816, 3
EPS = 1e-6
SAMPLE = DEC_B * DEC_S
T = SEQ + SAMPLE
KD = D_MODEL // P
KQ, KC, KU, KF = Q_LORA // P, KV_LORA // P, D_CONV // P, D_FF // P
PAGES = PAST // PAGE
KEYS = PAST + DEC_S
QT = SEQ // P
SCALE = float(NOPE + ROPE) ** -0.5
X_SCALE = float(XD) ** -0.5
CHUNKS = [(0, 512), (512, 512), (1024, SAMPLE)]
CPAD, FPAD = CONV_W - 1, FFN_W - 1
DOWN_KT = [8, 8, 6]

VEC_SIZES = [("g_pre_mix", KD), ("g_post_mix", KD), ("g_pre_x", KD), ("g_post_x", KD),
             ("g_pre_ffn", KD), ("g_post_ffn", KD), ("g_mem", KD), ("g_q_a", KQ), ("g_kv_a", KC),
             ("b_dw", KU), ("g_cln", KU), ("b_cln", KU), ("b_fdw", KF),
             ("w_dw", KU * CONV_W), ("w_fdw", KF * FFN_W)]
VEC_AT, _n = {}, 0
for _name, _size in VEC_SIZES:
    VEC_AT[_name] = _n
    _n += _size
N_VEC = _n


def region(ps, s):
    return ps[:, 3 * s:3 * s + 3, :].rearrange("p a b -> p (a b)")[:, 0:T]


def vec(K, name, j):
    a = VEC_AT[name] + j
    return K.vecs[:, a:a + 1]


class Names:
    pass


def semaphores(nc, ctx, stage):
    made = []
    ctx.callback(lambda: [nc.gpsimd.sem_clear(s) for s in made])

    def sem(what):
        made.append(ctx.enter_context(nc.semaphore(f"{stage}_{what}")))
        return made[-1]

    return sem


def load_stage(nc, K, A):
    with nc.Block() as block:
        @block.sync
        def _(sp):
            sp.dma_start(K.x[:, :, :], A.x_t).then_inc(K.s_load, 16)
            sp.dma_start(K.vecs[:, :], A.vecs).then_inc(K.s_load, 16)
            sp.dma_start(K.ident[:, :], A.ident).then_inc(K.s_load, 16)
            sp.dma_start(K.rope[64:128, :], A.rope).then_inc(K.s_load, 16)
            sp.dma_start(K.causal[:, :], A.causal).then_inc(K.s_load, 16)
            sp.dma_start(K.new_mask[:, :], A.new_mask).then_inc(K.s_load, 16)
            sp.wait_ge(K.s_load, 96)

        @block.vector
        def _(dve):
            nc.vector.memset(K.ones[:, :], 1.0)
            nc.vector.memset(K.eps[:, :], EPS)


def norm_stage(nc, K, name, src, n_k, width, gain, dst, dim, add_to=None, center=False, bias=None, func=None,
               store=None):
    chunks = CHUNKS if width == T else [(0, width)]
    with ExitStack() as ctx:
        sq = ctx.enter_context(nc.sbuf_tensor(f"{name}_sq", [P, 2, width], F32))
        acc = ctx.enter_context(nc.sbuf_tensor(f"{name}_acc", [P, width], F32))
        rstd = ctx.enter_context(nc.sbuf_tensor(f"{name}_rstd", [P, width], F32))

        sem = semaphores(nc, ctx, name)

        summed, mean_ready, centered = sem("summed"), sem("mean_ready"), sem("centered")
        squared, sq_added, total_ready, rooted = sem("squared"), sem("sq_added"), sem("total_ready"), sem("rooted")
        rstd_ready, scaled, done, stored = sem("rstd_ready"), sem("scaled"), sem("done"), sem("stored")
        block = ctx.enter_context(nc.Block())
        total = region(K.ps, 0)[:, 0:width]
        mean_total = region(K.ps, 1)[:, 0:width]

        @block.scalar
        def _(act):
            if center:
                act.wait_ge(centered, n_k)
            for k in range(n_k):
                if k >= 2:
                    act.wait_ge(sq_added, k - 1)
                nc.scalar.activation(sq[:, k % 2, :], src[:, k, :], ACT.Square).then_inc(squared, 1)
            act.wait_ge(total_ready, 1)
            nc.scalar.activation(rstd[:, :], total, ACT.Sqrt, bias=K.eps[:, :], scale=1.0 / dim).then_inc(rooted, 1)
            if func is not None:
                for k in range(n_k):
                    act.wait_ge(scaled, k + 1)
                    nc.scalar.activation(dst[:, k, :], dst[:, k, :], func, bias=vec(K, bias, k)).then_inc(done, 1)

        @block.tensor
        def _(pe):
            if center:
                pe.wait_ge(summed, n_k)
                for at, n in chunks:
                    mm = nc.tensor.matmul(mean_total[:, at:at + n], K.ones[:, :], acc[:, at:at + n],
                                          start=True, stop=True)
                mm.then_inc(mean_ready, 1)
            pe.wait_ge(sq_added, n_k)
            for at, n in chunks:
                mm = nc.tensor.matmul(total[:, at:at + n], K.ones[:, :], acc[:, at:at + n], start=True, stop=True)
            mm.then_inc(total_ready, 1)

        @block.vector
        def _(dve):
            if center:
                nc.vector.tensor_copy(acc[:, :], src[:, 0, :]).then_inc(summed, 1)
                for k in range(1, n_k):
                    dve.wait_ge(summed, k)
                    nc.vector.tensor_tensor(acc[:, :], acc[:, :], src[:, k, :], ALU.add).then_inc(summed, 1)
                dve.wait_ge(mean_ready, 1)
                for k in range(n_k):
                    nc.vector.scalar_tensor_tensor(src[:, k, :], mean_total, -1.0 / dim, src[:, k, :],
                                                   ALU.mult, ALU.add).then_inc(centered, 1)
            dve.wait_ge(squared, 1)
            nc.vector.tensor_copy(acc[:, :], sq[:, 0, :]).then_inc(sq_added, 1)
            for k in range(1, n_k):
                dve.wait_ge(squared, k + 1)
                dve.wait_ge(sq_added, k)
                nc.vector.tensor_tensor(acc[:, :], acc[:, :], sq[:, k % 2, :], ALU.add).then_inc(sq_added, 1)
            dve.wait_ge(rooted, 1)
            nc.vector.reciprocal(rstd[:, :], rstd[:, :]).then_inc(rstd_ready, 1)
            dve.wait_ge(rstd_ready, 1)
            for k in range(n_k):
                if add_to is None:
                    nc.vector.scalar_tensor_tensor(dst[:, k, :], src[:, k, :], vec(K, gain, k), rstd[:, :],
                                                   ALU.mult, ALU.mult).then_inc(done if func is None else scaled, 1)
                else:
                    nc.vector.scalar_tensor_tensor(src[:, k, :], src[:, k, :], vec(K, gain, k), rstd[:, :],
                                                   ALU.mult, ALU.mult).then_inc(scaled, 1)
                    dve.wait_ge(scaled, k + 1)
                    nc.vector.tensor_tensor(dst[:, k, :], add_to[:, k, :], src[:, k, :], ALU.add).then_inc(done, 1)

        @block.sync
        def _(sp):
            if store is not None:
                sp.wait_ge(done, n_k)
                sp.wait_ge(stored, 16 * store(sp, stored))


def stream_weights(sp, K, name_sems, tiles, n_bodies, units):
    full, used = name_sems
    with sp.Fori(0, n_bodies) as i:
        for q, kt in enumerate(units):
            slot, turn = q % 2, i * (len(units) // 2) + q // 2
            sp.wait_ge(used[slot], turn)
            sp.dma_start(K.ring[:, slot, 0:kt, :].rearrange("p k f -> p (k f)"),
                         tiles[bass.ds(i * len(units) + q, 1), :, 0:kt * P].rearrange("a p c -> p (a c)")
                         ).then_inc(full[slot], 16)


def accumulate(nc, K, out, slot, kt, rhs, first, last):
    for k in range(kt):
        for at, n in CHUNKS:
            mm = nc.tensor.matmul(out[:, at:at + n], K.ring[:, slot, k, :], rhs(k, at, n),
                                  start=first and k == 0, stop=last and k == kt - 1)
    return mm


def linear_stage(nc, K, name, tiles, src, dst, n_f, units=(KD,), src_at=None):
    n_u = len(units)
    with ExitStack() as ctx:
        sem = semaphores(nc, ctx, name)
        full = [sem(f"full{s}") for s in range(2)]
        used = [sem(f"used{s}") for s in range(2)]
        copied = [sem(f"copied{s}") for s in range(2)]
        block = ctx.enter_context(nc.Block())

        def last_unit(s, i):
            q = s * n_u + n_u - 1
            return used[q % 2], i * n_u + q // 2 + 1

        @block.sync
        def _(sp):
            stream_weights(sp, K, (full, used), tiles, n_f // 2, list(units) * 2)

        @block.tensor
        def _(pe):
            with pe.Fori(0, n_f // 2) as i:
                for s in range(2):
                    pe.wait_ge(copied[s], i)
                    for u, kt in enumerate(units):
                        q = s * n_u + u
                        pe.wait_ge(full[q % 2], i * (16 * n_u) + 16 * (q // 2 + 1))
                        k0 = sum(units[:u])
                        accumulate(nc, K, region(K.ps, s), q % 2, kt, lambda k, at, n: src[:, k0 + k, at:at + n],
                                   u == 0, u == n_u - 1).then_inc(used[q % 2], 1)

        @block.scalar
        def _(act):
            with act.Fori(0, n_f // 2) as i:
                act.wait_ge(*last_unit(0, i))
                nc.scalar.activation(dst[:, bass.ds(2 * i, 1), :], region(K.ps, 0), ACT.Identity
                                     ).then_inc(copied[0], 1)

        @block.vector
        def _(dve):
            with dve.Fori(0, n_f // 2) as i:
                dve.wait_ge(*last_unit(1, i))
                nc.vector.tensor_copy(dst[:, bass.ds(2 * i + 1, 1), :], region(K.ps, 1)).then_inc(copied[1], 1)


def glu_stage(nc, K):
    with ExitStack() as ctx:
        sem = semaphores(nc, ctx, "glu")
        gate = ctx.enter_context(nc.sbuf_tensor("glu_gate", [P, T], F32))
        full = [sem(f"full{s}") for s in range(2)]
        used = [sem(f"used{s}") for s in range(2)]
        gated, multiplied = (sem(w) for w in ("gated", "multiplied"))
        hist = sem("hist")
        block = ctx.enter_context(nc.Block())

        @block.sync
        def _(sp):
            for k in range(KU):
                sp.dma_start(K.u_sample[:, k, :, 0:CPAD], K.A.state_conv_t[k]).then_inc(hist, 16)
            stream_weights(sp, K, (full, used), K.A.w_in_t[2 * 3:], KU, [KD, KD])
            sp.wait_ge(hist, 16 * KU)

        @block.tensor
        def _(pe):
            with pe.Fori(0, KU) as i:
                for s in range(2):
                    pe.wait_ge(gated if s == 0 else multiplied, i if s == 0 else 2 * i)
                    pe.wait_ge(full[s], i * 16 + 16)
                    accumulate(nc, K, region(K.ps, s), s, KD, lambda k, at, n: K.h[:, k, at:at + n],
                               True, True).then_inc(used[s], 1)

        @block.scalar
        def _(act):
            with act.Fori(0, KU) as i:
                act.wait_ge(used[0], i + 1)
                act.wait_ge(multiplied, 2 * i)
                nc.scalar.activation(gate[:, :], region(K.ps, 0), ACT.Sigmoid).then_inc(gated, 1)

        @block.vector
        def _(dve):
            nc.vector.memset(K.u_prompt[:, :, 0:CPAD], 0.0)
            with dve.Fori(0, KU) as i:
                dve.wait_ge(used[1], i + 1)
                dve.wait_ge(gated, i + 1)
                a = region(K.ps, 1)
                nc.vector.tensor_tensor(K.u_prompt[:, bass.ds(i, 1), CPAD:CPAD + SEQ], a[:, 0:SEQ], gate[:, 0:SEQ],
                                        ALU.mult).then_inc(multiplied, 1)
                nc.vector.tensor_tensor(K.u_sample[:, bass.ds(i, 1), :, CPAD:].rearrange("p a b s -> p (a b) s"),
                                        a[:, SEQ:T].rearrange("p (b s) -> p b s", b=DEC_B),
                                        gate[:, SEQ:T].rearrange("p (b s) -> p b s", b=DEC_B),
                                        ALU.mult).then_inc(multiplied, 1)


def rope_k_stage(nc, K):
    with ExitStack() as ctx:
        sem = semaphores(nc, ctx, "rope")
        part = ctx.enter_context(nc.sbuf_tensor("rope_part", [P, 2, T], F32))
        products, rotated = (sem(w) for w in ("products", "rotated"))
        stored = sem("stored")
        block = ctx.enter_context(nc.Block())

        @block.vector
        def _(dve):
            nc.vector.tensor_tensor(part[64:96, 0, :], K.lat[64:96, 5, :], K.rope[64:96, :], ALU.mult
                                    ).then_inc(products, 1)
            nc.vector.tensor_tensor(part[64:96, 1, :], K.lat[96:128, 5, :], K.rope[96:128, :], ALU.mult
                                    ).then_inc(products, 1)
            dve.wait_ge(products, 2)
            nc.vector.tensor_tensor(K.kh[64:96, :], part[64:96, 0, :], part[64:96, 1, :], ALU.add
                                    ).then_inc(rotated, 1)

        @block.sync
        def _(sp):
            sp.wait_ge(rotated, 1)
            sp.dma_start(K.A.k_rope_t, K.kh[64:96, :]).then_inc(stored, 16)
            for k in range(KU):
                sp.dma_start(K.A.conv_prompt_t[k], K.u_prompt[:, k, SEQ:]).then_inc(stored, 16)
                sp.dma_start(K.A.conv_sample_t[k], K.u_sample[:, k, :, DEC_S:]).then_inc(stored, 16)
            sp.wait_ge(stored, 16 + 32 * KU)


def conv_stage(nc, K):
    with ExitStack() as ctx:
        sem = semaphores(nc, ctx, "conv")
        tap_done = sem("tap_done")
        block = ctx.enter_context(nc.Block())

        @block.vector
        def _(dve):
            for k in range(KU):
                for w in range(CONV_W):
                    n = (k * CONV_W + w) * 2
                    scale = vec(K, "w_dw", k * CONV_W + w)
                    out_p = K.mix[:, KU + k, 0:SEQ]
                    out_s = K.mix[:, KU + k, SEQ:T].rearrange("p (b s) -> p b s", b=DEC_B)
                    in_p, in_s = K.u_prompt[:, k, w:w + SEQ], K.u_sample[:, k, :, w:w + DEC_S]
                    if w == 0:
                        nc.vector.tensor_scalar(out_p, in_p, scale, vec(K, "b_dw", k), ALU.mult, ALU.add
                                                ).then_inc(tap_done, 1)
                        nc.vector.tensor_scalar(out_s, in_s, scale, vec(K, "b_dw", k), ALU.mult, ALU.add
                                                ).then_inc(tap_done, 1)
                        continue
                    dve.wait_ge(tap_done, n - 1)
                    nc.vector.scalar_tensor_tensor(out_p, in_p, scale, out_p, ALU.mult, ALU.add
                                                   ).then_inc(tap_done, 1)
                    dve.wait_ge(tap_done, n)
                    nc.vector.scalar_tensor_tensor(out_s, in_s, scale, out_s, ALU.mult, ALU.add
                                                   ).then_inc(tap_done, 1)


def value_stage(nc, K):
    with ExitStack() as ctx:
        sem = semaphores(nc, ctx, "value")
        wuv_full, summed, copied = (sem(w)
                                    for w in ("wuv_full", "summed", "copied"))
        block = ctx.enter_context(nc.Block())

        @block.sync
        def _(sp):
            sp.dma_start(K.wuv[:, :, :], K.A.w_uv_t).then_inc(wuv_full, 16)

        @block.tensor
        def _(pe):
            pe.wait_ge(wuv_full, 16)
            for t in range(QT):
                if t >= 4:
                    pe.wait_ge(copied, t - 3)
                for l in range(KC):
                    mm = nc.tensor.matmul(K.ps[:, t % 4, :], K.c[:, l, t * P:(t + 1) * P], K.wuv[:, l, :],
                                          start=l == 0, stop=l == KC - 1)
                mm.then_inc(summed, 1)

        @block.scalar
        def _(act):
            for t in range(QT):
                act.wait_ge(summed, t + 1)
                nc.scalar.activation(K.v[:, t, :], K.ps[:, t % 4, :], ACT.Identity).then_inc(copied, 1)


def prompt_attention_stage(nc, K):
    with ExitStack() as ctx:
        def sb(what, shape):
            return ctx.enter_context(nc.sbuf_tensor(f"mla_{what}", shape, F32))

        sem = semaphores(nc, ctx, "mla")

        wh = sb("wh", [P, KQ * P + KC * NOPE + KV_LORA])
        wq = wh[:, 0:KQ * P].rearrange("p (k f) -> p k f", k=KQ)
        wuk = wh[:, KQ * P:KQ * P + KC * NOPE].rearrange("p (k f) -> p k f", k=KC)
        wuk_t = wh[0:NOPE, KQ * P + KC * NOPE:]
        qh = sb("qh", [P, T])
        part = sb("part", [P, 2, T])
        prob = sb("prob", [P, 2, SEQ])
        prob_t = sb("prob_t", [P, 2, SEQ])
        top = sb("top", [P, QT])
        neg_top = sb("neg_top", [P, QT])
        den = sb("den", [P, QT])
        inv = sb("inv", [P, QT])
        w_full, proj_done, nope_ready, rope_parts, q_ready, ql_done, ql_copied = (
            sem(x) for x in ("w_full", "proj_done", "nope_ready", "rope_parts", "q_ready", "ql_done", "ql_copied"))
        scored, masked, top_found, top_ready, exped, turned, turned_copied, summed, inv_ready, normed = (
            sem(x) for x in ("scored", "masked", "top_found", "top_ready", "exped", "turned", "turned_copied",
                             "summed", "inv_ready", "normed"))
        block = ctx.enter_context(nc.Block())
        q_acc = region(K.ps, 0)
        k_acc = K.ps[0:NOPE, 4:6, :].rearrange("p a b -> p (a b)")
        turn = K.ps[:, 4:6, :].rearrange("p a b -> p (a b)")
        ql_acc = K.ps[:, 6, 0:KC * SAMPLE].rearrange("p (l t) -> p l t", l=KC)

        def score(i):
            return K.ps[:, 2 * (i % 2):2 * (i % 2) + 2, :].rearrange("p a b -> p (a b)")[:, 0:(i + 1) * P]

        @block.sync
        def _(sp):
            with sp.Fori(0, HEADS) as h:
                sp.wait_ge(ql_done, h)
                sp.dma_start(wh[:, :], K.A.w_head_t[bass.ds(h, 1)].rearrange("a p c -> p (a c)")
                             ).then_inc(w_full, 16)

        @block.tensor
        def _(pe):
            with pe.Fori(0, HEADS) as h:
                def scores(i):
                    if i >= 2:
                        pe.wait_ge(exped, h * QT + i - 1)
                    for at in range(0, (i + 1) * P, 512):
                        n = min(512, (i + 1) * P - at)
                        mm = nc.tensor.matmul(score(i)[:, at:at + n], qh[0:96, i * P:(i + 1) * P],
                                              K.kh[0:96, at:at + n], start=True, stop=True)
                    mm.then_inc(scored, 1)

                pe.wait_ge(w_full, h * 16 + 16)
                pe.wait_ge(exped, h * QT)
                pe.wait_ge(turned_copied, h * QT)
                for k in range(KQ):
                    for at, n in CHUNKS:
                        nc.tensor.matmul(q_acc[:, at:at + n], wq[:, k, :], K.lat[:, k, at:at + n],
                                         start=k == 0, stop=k == KQ - 1)
                for l in range(KC):
                    for at, n in CHUNKS[:2]:
                        mm = nc.tensor.matmul(k_acc[:, at:at + n], wuk[:, l, :], K.c[:, l, at:at + n],
                                              start=l == 0, stop=l == KC - 1)
                mm.then_inc(proj_done, 1)
                pe.wait_ge(nope_ready, h * 2 + 2)
                pe.wait_ge(q_ready, h + 1)
                pe.wait_ge(normed, h * QT)
                for l in range(KC):
                    mm = nc.tensor.matmul(ql_acc[:, l, :], wuk_t[:, l * P:(l + 1) * P], qh[0:NOPE, SEQ:T],
                                          start=True, stop=True)
                mm.then_inc(ql_done, 1)
                scores(0)
                scores(1)
                pe.wait_ge(ql_copied, h + 1)
                for i in range(QT):
                    pe.wait_ge(exped, h * QT + i + 1)
                    if i >= 1:
                        pe.wait_ge(turned_copied, h * QT + i)
                    for j in range(i + 1):
                        mm = nc.tensor.transpose(turn[:, j * P:(j + 1) * P], prob[:, i % 2, j * P:(j + 1) * P],
                                                 K.ident[:, :])
                    mm.then_inc(turned, 1)
                    if i + 2 < QT:
                        scores(i + 2)
                    pe.wait_ge(turned_copied, h * QT + i + 1)
                    if i >= 2:
                        pe.wait_ge(normed, h * QT + i - 1)
                    for j in range(i + 1):
                        mm = nc.tensor.matmul(K.ps[:, 6 + i % 2, 0:VH], prob_t[:, i % 2, j * P:(j + 1) * P],
                                              K.v[:, j, bass.ds(h * VH, VH)], start=j == 0, stop=j == i)
                    mm.then_inc(summed, 1)

        @block.scalar
        def _(act):
            with act.Fori(0, HEADS) as h:
                def exp(i):
                    act.wait_ge(top_ready, h * QT + i + 1)
                    nc.scalar.activation(prob[:, i % 2, 0:(i + 1) * P], score(i), ACT.Exp, bias=neg_top[:, i:i + 1],
                                         scale=SCALE, accum_out=den[:, i:i + 1]).then_inc(exped, 1)

                act.wait_ge(proj_done, h + 1)
                nc.scalar.activation(qh[0:NOPE, :], q_acc[0:NOPE, :], ACT.Identity).then_inc(nope_ready, 1)
                nc.scalar.activation(K.kh[0:NOPE, 0:SEQ], k_acc, ACT.Identity).then_inc(nope_ready, 1)
                exp(0)
                exp(1)
                for i in range(QT):
                    act.wait_ge(turned, h * QT + i + 1)
                    if i >= 2:
                        act.wait_ge(summed, h * QT + i - 1)
                    nc.scalar.activation(prob_t[:, i % 2, 0:(i + 1) * P], turn[:, 0:(i + 1) * P], ACT.Identity
                                         ).then_inc(turned_copied, 1)
                    if i + 2 < QT:
                        exp(i + 2)

        @block.vector
        def _(dve):
            with dve.Fori(0, HEADS) as h:
                def find_top(i):
                    n = h * QT + i + 1
                    diag = score(i)[:, i * P:(i + 1) * P]
                    dve.wait_ge(scored, n)
                    nc.vector.tensor_tensor(diag, diag, K.causal[:, :], ALU.add).then_inc(masked, 1)
                    dve.wait_ge(masked, n)
                    nc.vector.tensor_reduce(top[:, i:i + 1], score(i), AX_X, ALU.max).then_inc(top_found, 1)
                    dve.wait_ge(top_found, n)
                    nc.vector.tensor_scalar(neg_top[:, i:i + 1], top[:, i:i + 1], -SCALE, None, ALU.mult
                                            ).then_inc(top_ready, 1)

                dve.wait_ge(proj_done, h + 1)
                nc.vector.tensor_tensor(part[64:96, 0, :], q_acc[64:96, :], K.rope[64:96, :], ALU.mult
                                        ).then_inc(rope_parts, 1)
                nc.vector.tensor_tensor(part[64:96, 1, :], q_acc[96:128, :], K.rope[96:128, :], ALU.mult
                                        ).then_inc(rope_parts, 1)
                dve.wait_ge(rope_parts, h * 2 + 2)
                nc.vector.tensor_tensor(qh[64:96, :], part[64:96, 0, :], part[64:96, 1, :], ALU.add
                                        ).then_inc(q_ready, 1)
                dve.wait_ge(q_ready, h + 1)
                nc.vector.tensor_copy(K.qpe[64:96, :, bass.ds(h, 1), :].rearrange("p b a s -> p b (a s)"),
                                      qh[64:96, SEQ:T].rearrange("p (b s) -> p b s", b=DEC_B))
                dve.wait_ge(ql_done, h + 1)
                for l in range(KC):
                    ins = nc.vector.tensor_copy(
                        K.qlat[:, l, :, bass.ds(h, 1), :].rearrange("p b a s -> p b (a s)"),
                        ql_acc[:, l, :].rearrange("p (b s) -> p b s", b=DEC_B))
                ins.then_inc(ql_copied, 1)
                find_top(0)
                find_top(1)
                for i in range(QT):
                    if i + 2 < QT:
                        find_top(i + 2)
                    dve.wait_ge(exped, h * QT + i + 1)
                    nc.vector.reciprocal(inv[:, i:i + 1], den[:, i:i + 1]).then_inc(inv_ready, 1)
                    dve.wait_ge(inv_ready, h * QT + i + 1)
                    dve.wait_ge(summed, h * QT + i + 1)
                    nc.vector.tensor_scalar(K.attn[:, i, bass.ds(h * VH, VH)], K.ps[:, 6 + i % 2, 0:VH],
                                            inv[:, i:i + 1], None, ALU.mult).then_inc(normed, 1)


def turn_attention_stage(nc, K):
    with ExitStack() as ctx:
        sem = semaphores(nc, ctx, "turn")
        turned, copied = (sem(w) for w in ("turned", "copied"))
        block = ctx.enter_context(nc.Block())

        @block.tensor
        def _(pe):
            for t in range(QT):
                if t >= 4:
                    pe.wait_ge(copied, t - 3)
                for f in range(4):
                    mm = nc.tensor.transpose(K.ps[:, t % 4, f * P:(f + 1) * P], K.attn[:, t, f * P:(f + 1) * P],
                                             K.ident[:, :])
                mm.then_inc(turned, 1)

        @block.vector
        def _(dve):
            for t in range(QT):
                dve.wait_ge(turned, t + 1)
                nc.vector.tensor_copy(K.mix[:, 0:4, t * P:(t + 1) * P],
                                      K.ps[:, t % 4, :].rearrange("p (f q) -> p f q", f=4)).then_inc(copied, 1)


def paged_attention_stage(nc, K):
    with ExitStack() as ctx:
        def sb(what, shape, dt=F32):
            return ctx.enter_context(nc.sbuf_tensor(f"paged_{what}", shape, dt))

        sem = semaphores(nc, ctx, "paged")

        R = HEADS * DEC_S
        table = sb("table", [1, DEC_B * PAGES], I32)
        lat_t = [sb(f"lat_t{s}", [P, KC, PAST]) for s in range(2)]
        pe_t = [sb(f"pe_t{s}", [P, PAST]) for s in range(2)]
        lat = [sb(f"lat{s}", [P, PAGES, KV_LORA]) for s in range(2)]
        ql = sb("ql", [P, 2, KC, R])
        qp = sb("qp", [P, 2, R])
        new_t = sb("new_t", [P, 2, KC, DEC_S])
        new_pe = sb("new_pe", [P, 2, DEC_S])
        new = sb("new", [DEC_S, 2, KV_LORA])
        prob = sb("prob", [R, KEYS])
        prob_t = sb("prob_t", [P, PAGES * R])
        prob_new = sb("prob_new", [DEC_S, R])
        o = sb("o", [R, KV_LORA])
        stats = sb("stats", [R, 4])
        table_in, may_turn = sem("table_in"), sem("may_turn")
        paged = [sem(f"paged{s}") for s in range(2)]
        staged, new_turned, new_copied, scored, masked, top_found, top_ready, exped = (
            sem(x) for x in ("staged", "new_turned", "new_copied", "scored", "masked", "top_found", "top_ready",
                             "exped"))
        turned, half_copied, other_copied, summed, inv_ready, normed, o_turned, o_copied = (
            sem(x) for x in ("turned", "half_copied", "other_copied", "summed", "inv_ready", "normed", "o_turned",
                             "o_copied"))
        block = ctx.enter_context(nc.Block())
        score = K.ps[0:R, 0:5, :].rearrange("p a b -> p (a b)")[:, 0:KEYS]
        turn = K.ps[:, 5:7, :].rearrange("p a b -> p (a b)")
        new_acc = K.ps[0:DEC_S, 7, 256:512]
        turn_new = K.ps[0:DEC_S, 7, 256:256 + R]
        o_acc = K.ps[0:R, 7, 0:KV_LORA]
        o_turn = K.ps[:, 7, 256:256 + KC * R]
        half = PAGES * R // 2

        @block.sync
        def _(sp):
            sp.dma_start(table[:, :], K.A.page_table).then_inc(table_in, 16)
            sp.wait_ge(table_in, 16)
            with sp.Fori(0, DEC_B // 2) as i:
                for s in range(2):
                    b = 2 * i + s
                    sp.wait_ge(summed, b - s if s == 0 else 2 * i)
                    if s == 1:
                        sp.wait_ge(summed, 2 * i)
                    for j in range(PAGES):
                        page = sp.value_load(table[0:1, bass.ds(b * PAGES + j, 1)], min_val=0,
                                             max_val=K.A.lat_t.shape[0] - 1)
                        sp.dma_start(lat_t[s][:, :, j * PAGE:(j + 1) * PAGE],
                                     K.A.lat_t[bass.ds(page, 1)].rearrange("a l p t -> p (a l) t")
                                     ).then_inc(paged[s], 16)
                        sp.dma_start(pe_t[s][64:96, j * PAGE:(j + 1) * PAGE],
                                     K.A.pe_t[bass.ds(page, 1)].rearrange("a p t -> p (a t)")
                                     ).then_inc(paged[s], 16)
                        sp.dma_start(lat[s][:, j, :], K.A.lat[bass.ds(page, 1)].rearrange("a p l -> p (a l)")
                                     ).then_inc(paged[s], 16)

        @block.tensor
        def _(pe):
            with pe.Fori(0, DEC_B // 2) as i:
                for s in range(2):
                    b = 2 * i + s
                    pe.wait_ge(staged, 4 * b + 4)
                    pe.wait_ge(o_copied, b)
                    for l in range(KC):
                        mm = nc.tensor.transpose(new_acc[:, l * P:(l + 1) * P], new_t[:, s, l, :], K.ident[:, :])
                    mm.then_inc(new_turned, 1)
                    pe.wait_ge(paged[s], i * (16 * 3 * PAGES) + 16 * 3 * PAGES)
                    pe.wait_ge(exped, b)
                    for c in range(PAST // 512):
                        at = slice(c * 512, (c + 1) * 512)
                        for l in range(KC):
                            nc.tensor.matmul(score[:, at], ql[:, s, l, :], lat_t[s][:, l, at], start=l == 0,
                                             stop=False)
                        nc.tensor.matmul(score[:, at], qp[64:96, s, :], pe_t[s][64:96, at], start=False, stop=True)
                    for l in range(KC):
                        nc.tensor.matmul(score[:, PAST:], ql[:, s, l, :], new_t[:, s, l, :], start=l == 0,
                                         stop=False)
                    nc.tensor.matmul(score[:, PAST:], qp[64:96, s, :], new_pe[64:96, s, :], start=False,
                                     stop=True).then_inc(scored, 1)
                    pe.wait_ge(exped, b + 1)
                    pe.wait_ge(new_copied, b + 1)
                    pe.sem_inc(may_turn, 1)
                    for j in range(PAGES):
                        nc.tensor.transpose(turn[:, j * R:(j + 1) * R], prob[:, j * PAGE:(j + 1) * PAGE],
                                            K.ident[0:R, 0:R])
                    nc.tensor.transpose(turn_new, prob[:, PAST:], K.ident[0:R, 0:R]).then_inc(turned, 1)
                    pe.wait_ge(half_copied, b + 1)
                    pe.wait_ge(other_copied, b + 1)
                    for j in range(PAGES):
                        nc.tensor.matmul(o_acc, prob_t[:, j * R:(j + 1) * R], lat[s][:, j, :], start=j == 0,
                                         stop=False)
                    nc.tensor.matmul(o_acc, prob_new[:, :], new[:, s, :], start=False, stop=True
                                     ).then_inc(summed, 1)
                    pe.wait_ge(normed, b + 1)
                    pe.sem_inc(may_turn, 1)
                    for l in range(KC):
                        mm = nc.tensor.transpose(o_turn[:, l * R:(l + 1) * R], o[:, l * P:(l + 1) * P],
                                                 K.ident[0:R, 0:R])
                    mm.then_inc(o_turned, 1)

        @block.scalar
        def _(act):
            with act.Fori(0, DEC_B // 2) as i:
                for s in range(2):
                    b = 2 * i + s
                    act.wait_ge(summed, 2 * i)
                    nc.scalar.activation(ql[:, s, :, :], K.qlat[:, :, bass.ds(b, 1), :, :].rearrange(
                        "p l a h s -> p l (a h s)"), ACT.Identity).then_inc(staged, 1)
                    nc.scalar.activation(qp[64:96, s, :], K.qpe[64:96, bass.ds(b, 1), :, :].rearrange(
                        "p a h s -> p (a h s)"), ACT.Identity).then_inc(staged, 1)
                    nc.scalar.activation(new_t[:, s, :, :], K.c[:, :, bass.ds(SEQ + b * DEC_S, DEC_S)],
                                         ACT.Identity).then_inc(staged, 1)
                    nc.scalar.activation(new_pe[64:96, s, :], K.kh[64:96, bass.ds(SEQ + b * DEC_S, DEC_S)],
                                         ACT.Identity).then_inc(staged, 1)
                    act.wait_ge(top_ready, b + 1)
                    act.wait_ge(turned, b)
                    nc.scalar.activation(prob[:, :], score, ACT.Exp, bias=stats[:, 1:2], scale=SCALE,
                                         accum_out=stats[:, 2:3]).then_inc(exped, 1)
                    act.wait_ge(turned, b + 1)
                    act.wait_ge(summed, b)
                    nc.scalar.activation(prob_t[:, 0:half], turn[:, 0:half], ACT.Identity).then_inc(half_copied, 1)

        @block.vector
        def _(dve):
            with dve.Fori(0, DEC_B // 2) as i:
                for s in range(2):
                    b = 2 * i + s
                    dve.wait_ge(new_turned, b + 1)
                    nc.vector.tensor_copy(new[:, s, :], new_acc).then_inc(new_copied, 1)
                    dve.wait_ge(scored, b + 1)
                    nc.vector.tensor_tensor(score[:, PAST:], score[:, PAST:], K.new_mask[:, :], ALU.add
                                            ).then_inc(masked, 1)
                    dve.wait_ge(masked, b + 1)
                    nc.vector.tensor_reduce(stats[:, 0:1], score, AX_X, ALU.max).then_inc(top_found, 1)
                    dve.wait_ge(top_found, b + 1)
                    nc.vector.tensor_scalar(stats[:, 1:2], stats[:, 0:1], -SCALE, None, ALU.mult
                                            ).then_inc(top_ready, 1)
                    dve.wait_ge(exped, b + 1)
                    nc.vector.reciprocal(stats[:, 3:4], stats[:, 2:3]).then_inc(inv_ready, 1)
                    dve.wait_ge(turned, b + 1)
                    nc.vector.tensor_copy(prob_new[:, :], turn_new)
                    nc.vector.tensor_copy(prob_t[:, half:], turn[:, half:]).then_inc(other_copied, 1)
                    dve.wait_ge(summed, b + 1)
                    dve.wait_ge(inv_ready, b + 1)
                    nc.vector.tensor_scalar(o[:, :], o_acc, stats[:, 3:4], None, ALU.mult).then_inc(normed, 1)
                    dve.wait_ge(o_turned, b + 1)
                    for l in range(KC):
                        ins = nc.vector.tensor_copy(
                            K.olat[:, l, :, bass.ds(b * DEC_S, DEC_S)],
                            o_turn[:, l * R:(l + 1) * R].rearrange("p (h s) -> p h s", h=HEADS))
                    ins.then_inc(o_copied, 1)


def sample_value_stage(nc, K):
    with ExitStack() as ctx:
        sem = semaphores(nc, ctx, "sv")
        summed, copied = (sem(w) for w in ("summed", "copied"))
        block = ctx.enter_context(nc.Block())

        @block.tensor
        def _(pe):
            for j in range(HEADS // 2):
                for par in range(2):
                    for l in range(KC):
                        mm = nc.tensor.matmul(K.ps[:, j, par * SAMPLE:(par + 1) * SAMPLE],
                                              K.wuv[:, l, j * P:(j + 1) * P], K.olat[:, l, 2 * j + par, :],
                                              start=l == 0, stop=l == KC - 1)
                mm.then_inc(summed, 1)

        @block.vector
        def _(dve):
            for j in range(HEADS // 2):
                dve.wait_ge(summed, j + 1)
                for par in range(2):
                    rows = slice(par * VH, (par + 1) * VH)
                    nc.vector.tensor_copy(K.mix[rows, j, SEQ:T], K.ps[rows, j, par * SAMPLE:(par + 1) * SAMPLE])


def memory_stage(nc, K, mem, mem_k, mem_v):
    with ExitStack() as ctx:
        sem = semaphores(nc, ctx, "mem")
        full = [sem(f"full{s}") for s in range(2)]
        used = [sem(f"used{s}") for s in range(2)]
        copied = [sem(f"copied{s}") for s in range(2)]
        stored = sem("stored")
        block = ctx.enter_context(nc.Block())

        @block.sync
        def _(sp):
            with sp.Fori(0, KD) as f:
                for s, tiles in enumerate((K.A.w_xk_t, K.A.w_xv_t)):
                    sp.wait_ge(used[s], f)
                    sp.dma_start(K.ring[:, s, :, :].rearrange("p k f -> p (k f)"),
                                 tiles[bass.ds(f, 1)].rearrange("a p c -> p (a c)")).then_inc(full[s], 16)
            sp.wait_ge(copied[0], KD)
            sp.dma_start(K.A.mem_k_t, mem_k[:, :, :]).then_inc(stored, 16)
            sp.wait_ge(copied[1], KD)
            sp.dma_start(K.A.mem_v_t, mem_v[:, :, :]).then_inc(stored, 16)
            sp.wait_ge(stored, 32)

        @block.tensor
        def _(pe):
            with pe.Fori(0, KD) as f:
                pe.wait_ge(full[0], f * 16 + 16)
                pe.wait_ge(copied[0], f)
                for k in range(KD):
                    mm = nc.tensor.matmul(K.ps[:, 0, 0:N_MEM], K.ring[:, 0, k, :], mem[:, k, :], start=k == 0,
                                          stop=k == KD - 1)
                mm.then_inc(used[0], 1)
                pe.wait_ge(full[1], f * 16 + 16)
                pe.wait_ge(copied[1], f)
                for n in range(N_MEM // P):
                    for k in range(KD):
                        mm = nc.tensor.matmul(K.ps[:, 1 + n, 0:P], mem[:, k, n * P:(n + 1) * P], K.ring[:, 1, k, :],
                                              start=k == 0, stop=k == KD - 1)
                mm.then_inc(used[1], 1)

        @block.scalar
        def _(act):
            with act.Fori(0, KD) as f:
                act.wait_ge(used[0], f + 1)
                nc.scalar.activation(mem_k[:, bass.ds(f, 1), :], K.ps[:, 0, 0:N_MEM], ACT.Identity
                                     ).then_inc(copied[0], 1)

        @block.vector
        def _(dve):
            with dve.Fori(0, KD) as f:
                dve.wait_ge(used[1], f + 1)
                nc.vector.tensor_copy(mem_v[:, :, bass.ds(f * P, P)], K.ps[:, 1:3, 0:P]).then_inc(copied[1], 1)


def prompt_cross_stage(nc, K, mem_k, mem_v, xo, xq_sample):
    with ExitStack() as ctx:
        def sb(what, shape):
            return ctx.enter_context(nc.sbuf_tensor(f"xp_{what}", shape, F32))

        sem = semaphores(nc, ctx, "xp")

        G = QT // 2
        q = sb("q", [P, 2, T])
        vh = sb("vh", [P, 2, XD])
        prob = sb("prob", [P, 2, N_MEM])
        prob_t = sb("prob_t", [P, 2, 2, 512])
        top, neg_top, den, inv = (sb(x, [P, QT]) for x in ("top", "neg_top", "den", "inv"))
        full = [sem(f"full{s}") for s in range(2)]
        used = [sem(f"used{s}") for s in range(2)]
        q_copied, kept, scored, top_found, top_ready, exped, inv_ready, normed, turned, turned_copied, summed, out = (
            sem(x) for x in ("q_copied", "kept", "scored", "top_found", "top_ready", "exped", "inv_ready", "normed",
                             "turned", "turned_copied", "summed", "out"))
        block = ctx.enter_context(nc.Block())

        def turn(g):
            return K.ps[:, 2 * g:2 * g + 2, :]

        @block.sync
        def _(sp):
            stream_weights(sp, K, (full, used), K.A.w_xq_t, XH, [KD, KD])

        @block.tensor
        def _(pe):
            with pe.Fori(0, XH) as h:
                def scores(i):
                    if i >= 2:
                        pe.wait_ge(exped, h * QT + i - 1)
                    for k in range(2):
                        mm = nc.tensor.matmul(K.ps[:, 6 + i % 2, 0:N_MEM], q[:, k, i * P:(i + 1) * P],
                                              mem_k[:, bass.ds(2 * h + k, 1), :].rearrange("p a n -> p (a n)"),
                                              start=k == 0, stop=k == 1)
                    mm.then_inc(scored, 1)

                pe.wait_ge(turned_copied, h * 2)
                pe.wait_ge(out, h * 4)
                for s in range(2):
                    pe.wait_ge(full[s], h * 16 + 16)
                    accumulate(nc, K, region(K.ps, s), s, KD, lambda k, at, n: K.h[:, k, at:at + n],
                               True, True).then_inc(used[s], 1)
                pe.wait_ge(q_copied, h * 3 + 3)
                scores(0)
                scores(1)
                for i in range(QT):
                    g = i // G
                    pe.wait_ge(normed, h * QT + i + 1)
                    for n in range(2):
                        mm = nc.tensor.transpose(turn(g)[:, n, (i % G) * P:(i % G + 1) * P],
                                                 prob[:, i % 2, n * P:(n + 1) * P], K.ident[:, :])
                    mm.then_inc(turned, 1)
                    if i + 2 < QT:
                        scores(i + 2)
                    if i % G == G - 1:
                        pe.wait_ge(turned_copied, h * 2 + g + 1)
                        for f in range(2):
                            if g == 1:
                                pe.wait_ge(out, h * 4 + f + 1)
                            for n in range(2):
                                mm = nc.tensor.matmul(K.ps[:, 4 + f, :], vh[:, n, f * P:(f + 1) * P],
                                                      prob_t[:, g, n, :], start=n == 0, stop=n == 1)
                            mm.then_inc(summed, 1)

        @block.scalar
        def _(act):
            with act.Fori(0, XH) as h:
                def exp(i):
                    act.wait_ge(top_ready, h * QT + i + 1)
                    if i >= 2:
                        act.wait_ge(turned, h * QT + i - 1)
                    nc.scalar.activation(prob[:, i % 2, :], K.ps[:, 6 + i % 2, 0:N_MEM], ACT.Exp,
                                         bias=neg_top[:, i:i + 1], scale=X_SCALE, accum_out=den[:, i:i + 1]
                                         ).then_inc(exped, 1)

                act.wait_ge(used[0], h + 1)
                nc.scalar.activation(q[:, 0, :], region(K.ps, 0), ACT.Identity).then_inc(q_copied, 1)
                nc.scalar.activation(vh[:, :, :], mem_v[:, :, bass.ds(h * XD, XD)], ACT.Identity
                                     ).then_inc(q_copied, 1)
                exp(0)
                exp(1)
                for i in range(QT):
                    if i % G == G - 1:
                        act.wait_ge(turned, h * QT + i + 1)
                        g = i // G
                        nc.scalar.activation(prob_t[:, g, :, :], turn(g), ACT.Identity).then_inc(turned_copied, 1)
                    if i + 2 < QT:
                        exp(i + 2)

        @block.vector
        def _(dve):
            with dve.Fori(0, XH) as h:
                def find_top(i):
                    n = h * QT + i + 1
                    dve.wait_ge(scored, n)
                    nc.vector.tensor_reduce(top[:, i:i + 1], K.ps[:, 6 + i % 2, 0:N_MEM], AX_X, ALU.max
                                            ).then_inc(top_found, 1)
                    dve.wait_ge(top_found, n)
                    nc.vector.tensor_scalar(neg_top[:, i:i + 1], top[:, i:i + 1], -X_SCALE, None, ALU.mult
                                            ).then_inc(top_ready, 1)

                dve.wait_ge(used[1], h + 1)
                nc.vector.tensor_copy(q[:, 1, :], region(K.ps, 1)).then_inc(q_copied, 1)
                dve.wait_ge(q_copied, h * 3 + 3)
                nc.vector.tensor_copy(xq_sample[:, bass.ds(2 * h, 2), :], q[:, :, SEQ:T])
                find_top(0)
                find_top(1)
                for i in range(QT):
                    dve.wait_ge(exped, h * QT + i + 1)
                    nc.vector.reciprocal(inv[:, i:i + 1], den[:, i:i + 1]).then_inc(inv_ready, 1)
                    dve.wait_ge(inv_ready, h * QT + i + 1)
                    nc.vector.tensor_scalar(prob[:, i % 2, :], prob[:, i % 2, :], inv[:, i:i + 1], None, ALU.mult
                                            ).then_inc(normed, 1)
                    if i + 2 < QT:
                        find_top(i + 2)
                    if i % G == G - 1:
                        g = i // G
                        for f in range(2):
                            dve.wait_ge(summed, h * 4 + 2 * g + f + 1)
                            nc.vector.tensor_copy(xo[:, bass.ds(2 * h + f, 1), g * 512:(g + 1) * 512],
                                                  K.ps[:, 4 + f, :]).then_inc(out, 1)


def sample_cross_stage(nc, K, xo, xq_sample):
    with ExitStack() as ctx:
        def sb(what, shape):
            return ctx.enter_context(nc.sbuf_tensor(f"xs_{what}", shape, F32))

        sem = semaphores(nc, ctx, "xs")

        R = XH * DEC_S
        may_turn = sem("may_turn")
        keys = sb("keys", [P, 2, KD, N_MEM])
        vals = sb("vals", [P, 2, 2, D_MODEL])
        qd = sb("qd", [P, 2, KD, R])
        prob = sb("prob", [R, 2, N_MEM])
        prob_t = sb("prob_t", [P, 2, 2, R])
        stats = sb("stats", [R, 2, 4])
        loaded = [sem(f"loaded{s}") for s in range(2)]
        cleared, staged, scored, top_found, top_ready, exped, inv_ready, normed, turned, turned_copied, summed, out = (
            sem(x) for x in ("cleared", "staged", "scored", "top_found", "top_ready", "exped", "inv_ready", "normed",
                             "turned", "turned_copied", "summed", "out"))
        block = ctx.enter_context(nc.Block())

        @block.sync
        def _(sp):
            with sp.Fori(0, DEC_B // 2) as i:
                for s in range(2):
                    sp.wait_ge(summed, 2 * i)
                    sp.dma_start(keys[:, s, :, :], K.A.cache_k_t[bass.ds(2 * i + s, 1)].rearrange(
                        "a p k n -> p (a k) n")).then_inc(loaded[s], 16)
                    sp.dma_start(vals[:, s, :, :], K.A.cache_v_t[bass.ds(2 * i + s, 1)].rearrange(
                        "a p k n -> p (a k) n")).then_inc(loaded[s], 16)

        @block.tensor
        def _(pe):
            with pe.Fori(0, DEC_B // 2) as i:
                for s in range(2):
                    b = 2 * i + s
                    pe.wait_ge(loaded[s], i * 32 + 32)
                    pe.wait_ge(staged, b * 4 + 4)
                    pe.wait_ge(exped, b)
                    for k in range(KD):
                        mm = nc.tensor.matmul(K.ps[0:R, 4 * s, 0:N_MEM], qd[:, s, k, :], keys[:, s, k, :],
                                              start=k == 0, stop=k == KD - 1)
                    mm.then_inc(scored, 1)
                    pe.wait_ge(normed, b + 1)
                    pe.sem_inc(may_turn, 1)
                    for n in range(2):
                        mm = nc.tensor.transpose(K.ps[:, 4 * s + 1, n * R:(n + 1) * R],
                                                 prob[:, s, n * P:(n + 1) * P], K.ident[0:R, 0:R])
                    mm.then_inc(turned, 1)
                    pe.wait_ge(turned_copied, b + 1)
                    for f in range(KD):
                        for n in range(2):
                            mm = nc.tensor.matmul(K.ps[:, 4 * s + 2, f * DEC_S:(f + 1) * DEC_S],
                                                  vals[:, s, n, f * P:(f + 1) * P],
                                                  prob_t[:, s, n, (f // 2) * DEC_S:(f // 2 + 1) * DEC_S],
                                                  start=n == 0, stop=n == 1)
                    mm.then_inc(summed, 1)

        @block.scalar
        def _(act):
            act.wait_ge(cleared, 1)
            with act.Fori(0, DEC_B // 2) as i:
                for s in range(2):
                    b = 2 * i + s
                    act.wait_ge(scored, 2 * i)
                    for h in range(XH):
                        nc.scalar.activation(qd[:, s, 2 * h:2 * h + 2, h * DEC_S:(h + 1) * DEC_S],
                                             xq_sample[:, 2 * h:2 * h + 2, bass.ds(b * DEC_S, DEC_S)], ACT.Identity
                                             ).then_inc(staged, 1)
                    act.wait_ge(top_ready, b + 1)
                    act.wait_ge(turned, 2 * i)
                    nc.scalar.activation(prob[:, s, :], K.ps[0:R, 4 * s, 0:N_MEM], ACT.Exp, bias=stats[:, s, 1:2],
                                         scale=X_SCALE, accum_out=stats[:, s, 2:3]).then_inc(exped, 1)

        @block.vector
        def _(dve):
            nc.vector.memset(qd[:, :, :, :], 0.0).then_inc(cleared, 1)
            with dve.Fori(0, DEC_B // 2) as i:
                for s in range(2):
                    b = 2 * i + s
                    dve.wait_ge(scored, b + 1)
                    nc.vector.tensor_reduce(stats[:, s, 0:1], K.ps[0:R, 4 * s, 0:N_MEM], AX_X, ALU.max
                                            ).then_inc(top_found, 1)
                    dve.wait_ge(top_found, b + 1)
                    nc.vector.tensor_scalar(stats[:, s, 1:2], stats[:, s, 0:1], -X_SCALE, None, ALU.mult
                                            ).then_inc(top_ready, 1)
                    dve.wait_ge(exped, b + 1)
                    nc.vector.reciprocal(stats[:, s, 3:4], stats[:, s, 2:3]).then_inc(inv_ready, 1)
                    dve.wait_ge(inv_ready, b + 1)
                    nc.vector.tensor_scalar(prob[:, s, :], prob[:, s, :], stats[:, s, 3:4], None, ALU.mult
                                            ).then_inc(normed, 1)
                    dve.wait_ge(turned, b + 1)
                    nc.vector.tensor_copy(prob_t[:, s, :, :].rearrange("p n r -> p (n r)"),
                                          K.ps[:, 4 * s + 1, 0:2 * R]).then_inc(turned_copied, 1)
                    dve.wait_ge(summed, b + 1)
                    nc.vector.tensor_copy(xo[:, :, bass.ds(SEQ + b * DEC_S, DEC_S)],
                                          K.ps[:, 4 * s + 2, 0:KD * DEC_S].rearrange("p (f s) -> p f s", f=KD)
                                          ).then_inc(out, 1)


def ffn_up_stage(nc, K, hid):
    with ExitStack() as ctx:
        def sb(what, shape):
            return ctx.enter_context(nc.sbuf_tensor(f"up_{what}", shape, F32))

        sem = semaphores(nc, ctx, "up")

        g_prompt = sb("g_prompt", [P, FPAD + SEQ])
        g_sample = sb("g_sample", [P, DEC_B, FPAD + DEC_S])
        hist = sb("hist", [P, KF, DEC_B, FPAD])
        last = sb("last", [P, KF, 1 + DEC_B, FPAD])
        conv = sb("conv", [P, T])
        full = [sem(f"full{s}") for s in range(2)]
        used = [sem(f"used{s}") for s in range(2)]
        padded = sem("padded")
        hist_in, g_copied, tap_done, kept, acted, multiplied, stored = (
            sem(x) for x in ("hist_in", "g_copied", "tap_done", "kept", "acted", "multiplied", "stored"))
        block = ctx.enter_context(nc.Block())
        conv_s = conv[:, SEQ:T].rearrange("p (b s) -> p b s", b=DEC_B)
        gate, value = region(K.ps, 0), region(K.ps, 1)

        @block.sync
        def _(sp):
            sp.dma_start(hist[:, :, :, :], K.A.state_ffn_t).then_inc(hist_in, 16)
            stream_weights(sp, K, (full, used), K.A.w_up_t, KF, [KD, KD])
            sp.wait_ge(kept, 2 * KF)
            sp.dma_start(K.A.ffn_state_t, last[:, :, :, :]).then_inc(stored, 16)
            sp.wait_ge(stored, 16)

        @block.tensor
        def _(pe):
            with pe.Fori(0, KF) as i:
                for s in range(2):
                    pe.wait_ge(g_copied if s == 0 else multiplied, i * 3 if s == 0 else i)
                    pe.wait_ge(full[s], i * 16 + 16)
                    accumulate(nc, K, region(K.ps, s), s, KD, lambda k, at, n: K.h[:, k, at:at + n],
                               True, True).then_inc(used[s], 1)

        @block.scalar
        def _(act):
            act.wait_ge(hist_in, 16)
            with act.Fori(0, KF) as i:
                act.wait_ge(used[0], i + 1)
                act.wait_ge(tap_done, i * 6)
                act.wait_ge(kept, i * 2)
                nc.scalar.activation(g_prompt[:, FPAD:], gate[:, 0:SEQ], ACT.Identity).then_inc(g_copied, 1)
                nc.scalar.activation(g_sample[:, :, FPAD:], gate[:, SEQ:T].rearrange("p (b s) -> p b s", b=DEC_B),
                                     ACT.Identity).then_inc(g_copied, 1)
                nc.scalar.activation(g_sample[:, :, 0:FPAD], hist[:, bass.ds(i, 1), :, :].rearrange(
                    "p a b w -> p (a b) w"), ACT.Identity).then_inc(g_copied, 1)
                act.wait_ge(tap_done, i * 6 + 6)
                nc.scalar.activation(conv[:, :], conv[:, :], ACT.Silu).then_inc(acted, 1)

        @block.gpsimd
        def _(pool):
            with pool.Fori(0, KF) as i:
                pool.wait_ge(g_copied, i * 3 + 3)
                nc.gpsimd.tensor_copy(last[:, bass.ds(i, 1), 0, :].rearrange("p a w -> p (a w)"),
                                      g_prompt[:, SEQ:]).then_inc(kept, 1)
                nc.gpsimd.tensor_copy(last[:, bass.ds(i, 1), 1:, :].rearrange("p a b w -> p (a b) w"),
                                      g_sample[:, :, DEC_S:]).then_inc(kept, 1)

        @block.vector
        def _(dve):
            nc.vector.memset(g_prompt[:, 0:FPAD], 0.0).then_inc(padded, 1)
            dve.wait_ge(padded, 1)
            with dve.Fori(0, KF) as i:
                dve.wait_ge(g_copied, i * 3 + 3)
                for w in range(FFN_W):
                    scale = K.vecs[:, bass.ds(VEC_AT["w_fdw"] + i * FFN_W + w, 1)]
                    in_p, in_s = g_prompt[:, w:w + SEQ], g_sample[:, :, w:w + DEC_S]
                    if w == 0:
                        dve.wait_ge(multiplied, i)
                        bias = K.vecs[:, bass.ds(VEC_AT["b_fdw"] + i, 1)]
                        nc.vector.tensor_scalar(conv[:, 0:SEQ], in_p, scale, bias, ALU.mult, ALU.add
                                                ).then_inc(tap_done, 1)
                        nc.vector.tensor_scalar(conv_s, in_s, scale, bias, ALU.mult, ALU.add).then_inc(tap_done, 1)
                        continue
                    dve.wait_ge(tap_done, i * 6 + 2 * w - 1)
                    nc.vector.scalar_tensor_tensor(conv[:, 0:SEQ], in_p, scale, conv[:, 0:SEQ], ALU.mult, ALU.add
                                                   ).then_inc(tap_done, 1)
                    dve.wait_ge(tap_done, i * 6 + 2 * w)
                    nc.vector.scalar_tensor_tensor(conv_s, in_s, scale, conv_s, ALU.mult, ALU.add
                                                   ).then_inc(tap_done, 1)
                dve.wait_ge(acted, i + 1)
                dve.wait_ge(used[1], i + 1)
                nc.vector.tensor_tensor(hid[:, bass.ds(i, 1), :], value, conv[:, :], ALU.mult
                                        ).then_inc(multiplied, 1)


def build(nc, A):
    K = Names()
    K.A = A
    with ExitStack() as top:
        def sb(stack, name, shape):
            return stack.enter_context(nc.sbuf_tensor(name, shape, F32))

        K.ps = top.enter_context(nc.psum_tensor("ps", [P, 8, 512], F32))
        K.s_load = top.enter_context(nc.semaphore("s_load"))
        K.x = sb(top, "x", [P, KD, T])
        K.h = sb(top, "h", [P, KD, T])
        K.ring = sb(top, "ring", [P, 2, KD, P])
        K.vecs = sb(top, "vecs", [P, N_VEC])
        K.ident, K.ones, K.causal = (sb(top, n, [P, P]) for n in ("ident", "ones", "causal"))
        K.new_mask = sb(top, "new_mask", [HEADS * DEC_S, DEC_S])
        K.eps = sb(top, "eps", [P, 1])
        K.mix = K.h
        with ExitStack() as mixer:
            K.qlat = sb(mixer, "qlat", [P, KC * DEC_B, HEADS * DEC_S])[:, :, :].rearrange(
                "p (l b) (h s) -> p l b h s", l=KC, h=HEADS)
            K.qpe = sb(mixer, "qpe", [P, DEC_B, HEADS * DEC_S])[:, :, :].rearrange(
                "p b (h s) -> p b h s", h=HEADS)
            K.olat = sb(mixer, "olat", [P, KC, HEADS, SAMPLE])
            K.wuv = sb(mixer, "wuv", [P, KC, HEADS * VH])
            K.kh = sb(mixer, "kh", [P, T])
            K.c = sb(mixer, "c", [P, KC, T])
            with ExitStack() as prompt:
                K.lat = sb(prompt, "lat", [P, KQ + KC + 1, T])
                K.rope = sb(prompt, "rope", [P, T])
                load_stage(nc, K, A)
                norm_stage(nc, K, "pre_mix", K.x, KD, T, "g_pre_mix", K.h, D_MODEL)
                linear_stage(nc, K, "latents", A.w_in_t, K.h, K.lat, KQ + KC + 1)
                with ExitStack() as conv:
                    K.u_prompt = sb(conv, "u_prompt", [P, KU, CPAD + SEQ])
                    K.u_sample = sb(conv, "u_sample", [P, KU, DEC_B, CPAD + DEC_S])
                    glu_stage(nc, K)
                    rope_k_stage(nc, K)
                    conv_stage(nc, K)
                norm_stage(nc, K, "conv_norm", K.mix[:, KU:, :], KU, T, "g_cln", K.mix[:, KU:, :], D_CONV,
                           center=True, bias="b_cln", func=ACT.Silu)
                norm_stage(nc, K, "q_norm", K.lat[:, 0:KQ, :], KQ, T, "g_q_a", K.lat[:, 0:KQ, :], Q_LORA)

                def store_latents(sp, stored):
                    sp.dma_start(A.kv_latent_t, K.c[:, :, :]).then_inc(stored, 16)
                    return 1

                norm_stage(nc, K, "kv_norm", K.lat[:, KQ:KQ + KC, :], KC, T, "g_kv_a", K.c, KV_LORA, store=store_latents)
                K.v = sb(prompt, "v", [P, QT, HEADS * VH])
                K.attn = sb(prompt, "attn", [P, QT, HEADS * VH])
                value_stage(nc, K)
                prompt_attention_stage(nc, K)
                turn_attention_stage(nc, K)
            paged_attention_stage(nc, K)
            sample_value_stage(nc, K)
        with ExitStack() as cross:
            m = sb(cross, "m", [P, KD, T])
            linear_stage(nc, K, "out", A.w_out_t, K.mix, m, KD)
            norm_stage(nc, K, "post_mix", m, KD, T, "g_post_mix", K.x, D_MODEL, add_to=K.x)
            norm_stage(nc, K, "pre_x", K.x, KD, T, "g_pre_x", K.h, D_MODEL)
            mem = sb(cross, "mem", [P, KD, N_MEM])
            mem_k = sb(cross, "mem_k", [P, KD, N_MEM])
            mem_v = sb(cross, "mem_v", [P, 2, D_MODEL])
            xq_sample = sb(cross, "xq_sample", [P, KD, SAMPLE])
            mem_in = cross.enter_context(nc.semaphore("mem_in"))
            with nc.Block() as block:
                @block.sync
                def _(sp):
                    sp.dma_start(mem[:, :, :], A.mem_t).then_inc(mem_in, 16)
                    sp.wait_ge(mem_in, 16)
            norm_stage(nc, K, "mem_norm", mem, KD, N_MEM, "g_mem", mem, D_MODEL)
            memory_stage(nc, K, mem, mem_k, mem_v)
            prompt_cross_stage(nc, K, mem_k, mem_v, m, xq_sample)
            sample_cross_stage(nc, K, m, xq_sample)
            linear_stage(nc, K, "xo", A.w_xo_t, m, K.h, KD)
        norm_stage(nc, K, "post_x", K.h, KD, T, "g_post_x", K.x, D_MODEL, add_to=K.x)
        norm_stage(nc, K, "pre_ffn", K.x, KD, T, "g_pre_ffn", K.h, D_MODEL)
        with ExitStack() as ffn:
            hid = sb(ffn, "hid", [P, KF, T])
            ffn_up_stage(nc, K, hid)
            linear_stage(nc, K, "down", A.w_down_t, hid, K.h, KD, units=DOWN_KT)

        def store_y(sp, stored):
            sp.dma_start(A.y_t, K.x[:, :, :]).then_inc(stored, 16)
            return 1

        norm_stage(nc, K, "post_ffn", K.h, KD, T, "g_post_ffn", K.x, D_MODEL, add_to=K.x, store=store_y)


OUTS = {
    "y_t": [P, KD, T], "kv_latent_t": [P, KC, T], "k_rope_t": [ROPE, T],
    "conv_prompt_t": [KU, P, CPAD], "conv_sample_t": [KU, P, DEC_B, CPAD],
    "ffn_state_t": [P, KF, 1 + DEC_B, FPAD], "mem_k_t": [P, KD, N_MEM], "mem_v_t": [P, 2, D_MODEL],
}


def kernel(**inputs):
    import numpy as np
    import concourse.bacc as bacc
    from concourse.bass_utils import run_bass_kernel_spmd

    a = {k: np.asarray(v) for k, v in inputs.items()}
    w = {k: v[0] for k, v in a.items() if k[0:2] in ("w_", "g_", "b_")}

    def by_feature(rows):
        return rows.reshape(rows.shape[0], -1, P).transpose(2, 1, 0)

    def tiles(m):
        k, f = m.shape
        return m.reshape(k // P, P, f // P, P).transpose(2, 1, 0, 3).reshape(f // P, P, k)

    def columns(v):
        return v.reshape(-1, P, int(v.size // v.shape[0])).transpose(1, 0, 2).reshape(P, -1)

    d = {}
    d["x_t"] = by_feature(np.concatenate([a["x_prompt"][0], a["x_sample"].reshape(SAMPLE, D_MODEL)]))
    d["mem_t"] = by_feature(a["mem_prompt"][0])
    per_feature = dict(w, w_dw=w["w_dw"].T, w_fdw=w["w_fdw"].T)
    d["vecs"] = np.concatenate([columns(per_feature[n]) for n, _ in VEC_SIZES], axis=1)

    pos = np.concatenate([np.arange(SEQ), PAST + np.tile(np.arange(DEC_S), DEC_B)]).astype(np.float32)
    half = ROPE // 2
    inv = (np.float32(10000.0) ** (-np.arange(half, dtype=np.float32) / np.float32(half))).astype(np.float32)
    ang = (pos[None, :] * inv[:, None]).astype(np.float32)
    cos, sin = np.cos(ang), np.sin(ang)
    d["rope"] = np.concatenate([cos, cos, -sin, sin]).astype(np.float32)
    d["ident"] = np.eye(P, dtype=np.float32)
    d["causal"] = np.triu(np.full((P, P), -1e30, np.float32), 1)
    d["new_mask"] = np.tile(np.triu(np.full((DEC_S, DEC_S), -1e30, np.float32), 1), (HEADS, 1))

    def swapped(cols):
        return np.concatenate([cols[..., half:], cols[..., :half]], axis=-1)

    cuts = np.cumsum([Q_LORA, KV_LORA, ROPE, D_CONV])
    wq, wc, wpe, wa, wb = np.split(w["w_in"], cuts, axis=1)
    glu = np.concatenate([x for k in range(KU) for x in (wb[:, k * P:(k + 1) * P], wa[:, k * P:(k + 1) * P])], axis=1)
    d["w_in_t"] = tiles(np.concatenate([wq, wc, wpe, wpe, wpe, swapped(wpe), glu], axis=1))
    heads = w["w_q_b"].reshape(KQ, P, HEADS, NOPE + ROPE)
    heads = np.concatenate([heads, swapped(heads[..., NOPE:])], axis=-1).transpose(2, 1, 0, 3).reshape(HEADS, P, -1)
    uk = w["w_uk"].reshape(KC, P, HEADS, NOPE).transpose(2, 1, 0, 3).reshape(HEADS, P, -1)
    uk_t = w["w_uk"].transpose(1, 2, 0)
    d["w_head_t"] = np.concatenate([heads, uk, np.concatenate([uk_t, uk_t], axis=1)], axis=2)
    d["w_uv_t"] = w["w_uv"].reshape(KC, P, HEADS * VH).transpose(1, 0, 2)
    for name in ("w_out", "w_xq", "w_xk", "w_xv", "w_xo"):
        d[name + "_t"] = tiles(w[name])
    value, gate = np.split(w["w_up"], 2, axis=1)
    d["w_up_t"] = tiles(np.concatenate([gate.reshape(D_MODEL, KF, 1, P), value.reshape(D_MODEL, KF, 1, P)], axis=2)
                        .reshape(D_MODEL, 2 * D_FF))
    down, at, parts = tiles(w["w_down"]), 0, []
    for kt in DOWN_KT:
        part = down[:, :, at * P:(at + kt) * P]
        parts.append(np.concatenate([part, part[:, :, 0:(KD - kt) * P]], axis=2))
        at += kt
    d["w_down_t"] = np.stack(parts, axis=1).reshape(KD * len(DOWN_KT), P, KD * P)

    lat = a["cache_kv_latent"][0]
    d["lat"] = lat
    d["lat_t"] = lat.transpose(0, 2, 1).reshape(-1, KC, P, PAGE)
    d["pe_t"] = a["cache_k_rope"][0].transpose(0, 2, 1)
    d["page_table"] = a["page_table"].reshape(1, -1)
    d["cache_k_t"] = a["cache_mem_k"][0].reshape(DEC_B, N_MEM, KD, P).transpose(0, 3, 2, 1)
    d["cache_v_t"] = a["cache_mem_v"][0].reshape(DEC_B, 2, P, D_MODEL).transpose(0, 2, 1, 3)
    d["state_conv_t"] = a["state_conv"][0].reshape(DEC_B, CPAD, KU, P).transpose(2, 3, 0, 1)
    d["state_ffn_t"] = a["state_ffn_conv"][0].reshape(DEC_B, FPAD, KF, P).transpose(3, 2, 0, 1)

    nc = bacc.Bacc("TRN2", target_bir_lowering=False, num_devices=1)
    A, arrays = Names(), {}
    for name, arr in d.items():
        arr = np.ascontiguousarray(arr)
        arrays[f"in_{name}"] = arr
        A.__dict__[name] = nc.dram_tensor(f"in_{name}", arr.shape, mybir.dt.from_np(arr.dtype),
                                          kind="ExternalInput").ap()
    for name, shape in OUTS.items():
        A.__dict__[name] = nc.dram_tensor(f"out_{name}", shape, F32, kind="ExternalOutput").ap()
    build(nc, A)
    got = run_bass_kernel_spmd(nc, [arrays], core_ids=[0]).results[0]
    r = {name: np.asarray(got[f"out_{name}"]) for name in OUTS}

    def rows(t):
        return t.transpose(2, 1, 0).reshape(t.shape[2], -1)

    y, c, pe = rows(r["y_t"]), rows(r["kv_latent_t"]), r["k_rope_t"].T
    ffn = r["ffn_state_t"].transpose(2, 3, 1, 0).reshape(1 + DEC_B, FPAD, D_FF)
    return (
        y[None, :SEQ], y[SEQ:].reshape(DEC_B, DEC_S, D_MODEL),
        c[None, None, :SEQ], pe[None, None, :SEQ],
        r["conv_prompt_t"].transpose(2, 0, 1).reshape(1, 1, CPAD, D_CONV), ffn[None, 0:1],
        rows(r["mem_k_t"]).reshape(1, 1, N_MEM, XH, XD),
        r["mem_v_t"].transpose(1, 0, 2).reshape(1, 1, N_MEM, XH, XD),
        c[SEQ:].reshape(1, DEC_B, DEC_S, KV_LORA), pe[SEQ:].reshape(1, DEC_B, DEC_S, ROPE),
        r["conv_sample_t"].transpose(2, 3, 0, 1).reshape(1, DEC_B, CPAD, D_CONV), ffn[None, 1:],
    )
```

```python
from contextlib import ExitStack

import concourse.bass as bass
from concourse import mybir

P = 128
F32 = mybir.dt.float32
F32R = mybir.dt.float32r
I32 = mybir.dt.int32
ALU = mybir.AluOpType
ACT = mybir.ActivationFunctionType
AX_X = mybir.AxisListType.X

D_MODEL, SEQ, DEC_B, DEC_S = 1024, 1024, 8, 8
PAST, PAGE = 2048, 128
HEADS, NOPE, ROPE, VH = 8, 64, 32, 64
Q_LORA, KV_LORA, D_CONV, CONV_W = 384, 256, 512, 31
XH, XD, N_MEM = 4, 256, 256
D_FF, FFN_W = 2816, 3
EPS = 1e-6
SAMPLE = DEC_B * DEC_S
T = SEQ + SAMPLE
KD = D_MODEL // P
KQ, KC, KU, KF = Q_LORA // P, KV_LORA // P, D_CONV // P, D_FF // P
PAGES = PAST // PAGE
PARTS = P // PAGES
PER_ROW = PAGE // PARTS
QT = SEQ // P
SCALE = float(NOPE + ROPE) ** -0.5
X_SCALE = float(XD) ** -0.5
CHUNKS = [(0, 512), (512, 512), (1024, SAMPLE)]
THIRD = 384
THIRDS = [(0, THIRD), (THIRD, THIRD), (2 * THIRD, T - 2 * THIRD)]
CPAD, FPAD = CONV_W - 1, FFN_W - 1
DOWN_F = 4

VEC_SIZES = [("g_pre_mix", KD), ("g_post_mix", KD), ("g_pre_x", KD), ("g_post_x", KD),
             ("g_pre_ffn", KD), ("g_post_ffn", KD), ("g_mem", KD), ("g_q_a", KQ), ("g_kv_a", KC),
             ("b_dw", 2 * KU), ("g_cln", KU), ("b_cln", KU), ("b_fdw", KF),
             ("w_dw", 2 * KU * CONV_W), ("w_fdw", KF * FFN_W)]
VEC_AT, _n = {}, 0
for _name, _size in VEC_SIZES:
    VEC_AT[_name] = _n
    _n += _size
N_VEC = _n


def region(ps, s):
    return ps[:, 3 * s:3 * s + 3, :].rearrange("p a b -> p (a b)")[:, 0:T]


def thirds(ps, s):
    return lambda at, n: ps[:, 3 * s + at // THIRD, 0:n]


def pieces(ps, s):
    return [(ps[:, 3 * s:3 * s + 2, 0:THIRD], 0, 2 * THIRD, 2),
            (ps[:, 3 * s + 2:3 * s + 3, 0:T - 2 * THIRD], 2 * THIRD, T - 2 * THIRD, 1)]


def piece(ap, at, n, a):
    return ap[:, at:at + n].rearrange("p (a c) -> p a c", a=a)


def vec(K, name, j):
    a = VEC_AT[name] + j
    return K.vecs[:, a:a + 1]


class Names:
    pass


def semaphores(nc, ctx, stage):
    made = []
    ctx.callback(lambda: [nc.gpsimd.sem_clear(s) for s in made])

    def sem(what):
        made.append(ctx.enter_context(nc.semaphore(f"{stage}_{what}")))
        return made[-1]

    return sem


def load_stage(nc, K, A):
    with nc.Block() as block:
        @block.sync
        def _(sp):
            sp.dma_start(K.x[:, :, :], A.x_t).then_inc(K.s_load, 16)
            sp.dma_start(K.vecs[:, :], A.vecs).then_inc(K.s_load, 16)
            sp.dma_start(K.ident[:, :], A.ident).then_inc(K.s_load, 16)
            sp.dma_start(K.rope[64:128, :], A.rope).then_inc(K.s_load, 16)
            sp.dma_start(K.causal[:, :], A.causal).then_inc(K.s_load, 16)
            sp.dma_start(K.pages[:, :], A.pages).then_inc(K.s_load, 16)
            sp.dma_start(K.part[:, :], A.part).then_inc(K.s_load, 16)
            sp.wait_ge(K.s_load, 112)

        @block.vector
        def _(dve):
            nc.vector.memset(K.ones[:, :], 1.0)
            nc.vector.memset(K.eps[:, :], EPS)
            dve.wait_ge(K.s_load, 112)
            nc.vector.scalar_tensor_tensor(K.page_rows[:, :], K.pages[:, :], float(PARTS), K.part[:, :], ALU.mult,
                                           ALU.add)


def norm_stage(nc, K, name, src, n_k, width, gain, dst, dim, add_to=None, center=False, bias=None, func=None,
               store=None, split=None, prefetch=False):
    chunks = CHUNKS if width == T else [(0, width)]
    with ExitStack() as ctx:
        sq = ctx.enter_context(nc.sbuf_tensor(f"{name}_sq", [P, 2, width], F32))
        acc = ctx.enter_context(nc.sbuf_tensor(f"{name}_acc", [P, width], F32))
        rstd = ctx.enter_context(nc.sbuf_tensor(f"{name}_rstd", [P, width], F32))
        if split is not None:
            whole = ctx.enter_context(nc.sbuf_tensor(f"{name}_whole", [P, 2, width], F32))

        sem = semaphores(nc, ctx, name)

        summed, mean_ready, centered = sem("summed"), sem("mean_ready"), sem("centered")
        squared, sq_added, total_ready, rooted = sem("squared"), sem("sq_added"), sem("total_ready"), sem("rooted")
        rstd_ready, scaled, done, stored = sem("rstd_ready"), sem("scaled"), sem("done"), sem("stored")
        hi_ready = sem("hi_ready")
        block = ctx.enter_context(nc.Block())
        total = region(K.ps, 0)[:, 0:width]
        mean_total = region(K.ps, 1)[:, 0:width]

        @block.scalar
        def _(act):
            if center:
                act.wait_ge(centered, n_k)
            for k in range(n_k):
                if k >= 2:
                    act.wait_ge(sq_added, k - 1)
                nc.scalar.activation(sq[:, k % 2, :], src[:, k, :], ACT.Square).then_inc(squared, 1)
            act.wait_ge(total_ready, 1)
            nc.scalar.activation(rstd[:, :], total, ACT.Sqrt, bias=K.eps[:, :], scale=1.0 / dim).then_inc(rooted, 1)
            if split is not None:
                for k in range(n_k):
                    act.wait_ge(scaled, k + 1)
                    nc.scalar.activation(split[0][:, k, :], whole[:, k % 2, :], ACT.Identity).then_inc(hi_ready, 1)
            if func is not None:
                for k in range(n_k):
                    act.wait_ge(scaled, k + 1)
                    nc.scalar.activation(dst[:, k, :], dst[:, k, :], func, bias=vec(K, bias, k)).then_inc(done, 1)

        @block.tensor
        def _(pe):
            if center:
                pe.wait_ge(summed, n_k)
                for at, n in chunks:
                    mm = nc.tensor.matmul(mean_total[:, at:at + n], K.ones[:, :], acc[:, at:at + n],
                                          start=True, stop=True)
                mm.then_inc(mean_ready, 1)
            pe.wait_ge(sq_added, n_k)
            for at, n in chunks:
                mm = nc.tensor.matmul(total[:, at:at + n], K.ones[:, :], acc[:, at:at + n], start=True, stop=True)
            mm.then_inc(total_ready, 1)

        @block.vector
        def _(dve):
            if center:
                nc.vector.tensor_copy(acc[:, :], src[:, 0, :]).then_inc(summed, 1)
                for k in range(1, n_k):
                    dve.wait_ge(summed, k)
                    nc.vector.tensor_tensor(acc[:, :], acc[:, :], src[:, k, :], ALU.add).then_inc(summed, 1)
                dve.wait_ge(mean_ready, 1)
                for k in range(n_k):
                    nc.vector.scalar_tensor_tensor(src[:, k, :], mean_total, -1.0 / dim, src[:, k, :],
                                                   ALU.mult, ALU.add).then_inc(centered, 1)
            dve.wait_ge(squared, 1)
            nc.vector.tensor_copy(acc[:, :], sq[:, 0, :]).then_inc(sq_added, 1)
            for k in range(1, n_k):
                dve.wait_ge(squared, k + 1)
                dve.wait_ge(sq_added, k)
                nc.vector.tensor_tensor(acc[:, :], acc[:, :], sq[:, k % 2, :], ALU.add).then_inc(sq_added, 1)
            dve.wait_ge(rooted, 1)
            nc.vector.reciprocal(rstd[:, :], rstd[:, :]).then_inc(rstd_ready, 1)
            dve.wait_ge(rstd_ready, 1)

            def low_half(k):
                dve.wait_ge(hi_ready, k + 1)
                nc.vector.tensor_tensor(split[1][:, k, :], whole[:, k % 2, :], split[0][:, k, :].bitcast(F32),
                                        ALU.subtract).then_inc(done, 1)

            for k in range(n_k):
                if split is not None:
                    if k >= 2:
                        dve.wait_ge(done, k - 1)
                    nc.vector.scalar_tensor_tensor(whole[:, k % 2, :], src[:, k, :], vec(K, gain, k), rstd[:, :],
                                                   ALU.mult, ALU.mult).then_inc(scaled, 1)
                    if k >= 1:
                        low_half(k - 1)
                    if k == n_k - 1:
                        low_half(k)
                elif add_to is None:
                    nc.vector.scalar_tensor_tensor(dst[:, k, :], src[:, k, :], vec(K, gain, k), rstd[:, :],
                                                   ALU.mult, ALU.mult).then_inc(done if func is None else scaled, 1)
                else:
                    nc.vector.scalar_tensor_tensor(src[:, k, :], src[:, k, :], vec(K, gain, k), rstd[:, :],
                                                   ALU.mult, ALU.mult).then_inc(scaled, 1)
                    dve.wait_ge(scaled, k + 1)
                    nc.vector.tensor_tensor(dst[:, k, :], add_to[:, k, :], src[:, k, :], ALU.add).then_inc(done, 1)

        @block.sync
        def _(sp):
            if prefetch:
                load_units(sp, K, 1)
            if store is not None:
                sp.wait_ge(done, n_k)
                sp.wait_ge(stored, 16 * store(sp, stored))

        if prefetch:
            @block.gpsimd
            def _(pool):
                split_units(nc, pool, K, 1)

    if prefetch:
        K.fed += 1


def load_units(sp, K, n):
    with sp.Fori(K.fed, K.fed + n) as j:
        for s in range(2):
            sp.wait_ge(K.split_done[s], j)
            sp.sem_inc(K.may_fetch, 1)
            sp.dma_start(K.raw[:, s, :], K.A.units[bass.ds(2 * j + s, 1)].rearrange("a p c -> p (a c)")
                         ).then_inc(K.unit_in[s], 16)


def split_units(nc, pool, K, n):
    with pool.Fori(K.fed, K.fed + n) as j:
        for s in range(2):
            pool.wait_ge(K.unit_in[s], 16 * j + 16)
            pool.wait_ge(K.unit_used[s], j)
            pool.sem_inc(K.may_split, 1)
            nc.gpsimd.tensor_copy(K.w_hi[:, s, :], K.raw[:, s, :]).then_inc(K.hi_done[s], 1)
            pool.wait_ge(K.hi_done[s], j + 1)
            nc.gpsimd.tensor_tensor(K.w_lo[:, s, :], K.raw[:, s, :], K.w_hi[:, s, :].bitcast(F32), ALU.subtract
                                    ).then_inc(K.split_done[s], 1)


def feed(nc, K, block, pairs, last):
    n = pairs - 1 if last else pairs

    @block.sync
    def _(sp):
        load_units(sp, K, n)

    @block.gpsimd
    def _(pool):
        split_units(nc, pool, K, n)

    return n


def accumulate(nc, K, out, slot, hi, lo, first=True, last=True, tiles=range(KD), chunks=THIRDS):
    for k, tile in enumerate(tiles):
        w_hi, w_lo = (w[:, slot, tile * P:(tile + 1) * P] for w in (K.w_hi, K.w_lo))
        for p, (w, x) in enumerate(((w_hi, hi), (w_hi, lo), (w_lo, hi))):
            for at, n in chunks:
                mm = nc.tensor.matmul(out(at, n), w, x(k, at, n), start=first and k == 0 and p == 0,
                                      stop=last and k == len(tiles) - 1 and p == 2)
    return mm


def linear_stage(nc, K, name, dst, n_f, halves, src=None, last=True):
    n = n_f // 2
    hi, lo = halves
    with ExitStack() as ctx:
        sem = semaphores(nc, ctx, name)
        copied = [sem(f"copied{s}") for s in range(2)]
        hi_made, lo_made = sem("hi_made"), sem("lo_made")
        block = ctx.enter_context(nc.Block())
        fed = feed(nc, K, block, n, last)
        used, base = K.unit_used, K.pair

        def x_hi(k, at, n):
            return hi[:, k, at:at + n]

        def x_lo(k, at, n):
            return lo[:, k, at:at + n]

        @block.tensor
        def _(pe):
            def unit(i, s, first_k=0):
                pe.wait_ge(copied[s], i)
                pe.wait_ge(K.split_done[s], i + (base + 1))
                accumulate(nc, K, thirds(K.ps, s), s, x_hi, x_lo).then_inc(used[s], 1)

            if src is not None:
                pe.wait_ge(K.split_done[0], base + 1)
                for k in range(KD):
                    pe.wait_ge(lo_made, k + 1)
                    mm = accumulate(nc, K, thirds(K.ps, 0), 0, lambda _, at, n: x_hi(k, at, n),
                                    lambda _, at, n: x_lo(k, at, n), first=k == 0, last=k == KD - 1, tiles=[k])
                mm.then_inc(used[0], 1)
                unit(0, 1)
                with pe.Fori(1, n) as i:
                    unit(i, 0)
                    unit(i, 1)
            else:
                with pe.Fori(0, n) as i:
                    unit(i, 0)
                    unit(i, 1)

        @block.scalar
        def _(act):
            if src is not None:
                for k in range(KD):
                    nc.scalar.activation(hi[:, k, :], src[:, k, :], ACT.Identity).then_inc(hi_made, 1)
            with act.Fori(0, n) as i:
                act.wait_ge(used[0], i + (base + 1))
                for acc, at, n_at, a in pieces(K.ps, 0):
                    ins = nc.scalar.activation(dst[:, bass.ds(2 * i, 1), at:at + n_at].rearrange(
                        "p b (a c) -> p (b a) c", a=a), acc, ACT.Identity)
                ins.then_inc(copied[0], 1)

        @block.vector
        def _(dve):
            if src is not None:
                for k in range(KD):
                    dve.wait_ge(hi_made, k + 1)
                    nc.vector.tensor_tensor(lo[:, k, :], src[:, k, :], hi[:, k, :].bitcast(F32), ALU.subtract
                                            ).then_inc(lo_made, 1)
            with dve.Fori(0, n) as i:
                dve.wait_ge(used[1], i + (base + 1))
                for acc, at, n_at, a in pieces(K.ps, 1):
                    ins = nc.vector.tensor_copy(dst[:, bass.ds(2 * i + 1, 1), at:at + n_at].rearrange(
                        "p b (a c) -> p (b a) c", a=a), acc)
                ins.then_inc(copied[1], 1)
    K.pair += n
    K.fed += fed


def glu_stage(nc, K, halves):
    hi, lo = halves
    with ExitStack() as ctx:
        sem = semaphores(nc, ctx, "glu")
        gate = ctx.enter_context(nc.sbuf_tensor("glu_gate", [P, T], F32))
        gated, multiplied, hist, padded = (sem(w) for w in ("gated", "multiplied", "hist", "padded"))
        block = ctx.enter_context(nc.Block())
        base = K.pair
        n = KU - 1

        @block.sync
        def _(sp):
            for k in range(KU):
                sp.dma_start(K.u_sample[:, k * DEC_B:(k + 1) * DEC_B, 0:CPAD], K.A.state_conv_t[k]).then_inc(hist, 16)
            load_units(sp, K, n)
            sp.wait_ge(hist, 16 * KU)

        @block.gpsimd
        def _(pool):
            split_units(nc, pool, K, n)

        @block.tensor
        def _(pe):
            with pe.Fori(0, KU) as i:
                for s in range(2):
                    pe.wait_ge(gated if s == 0 else multiplied, i)
                    pe.wait_ge(K.split_done[s], i + (base + 1))
                    accumulate(nc, K, thirds(K.ps, s), s, lambda k, at, n: hi[:, k, at:at + n],
                               lambda k, at, n: lo[:, k, at:at + n]).then_inc(K.unit_used[s], 1)

        @block.scalar
        def _(act):
            with act.Fori(0, KU) as i:
                act.wait_ge(K.unit_used[0], i + (base + 1))
                act.wait_ge(multiplied, i)
                for acc, at, n_at, a in pieces(K.ps, 0):
                    ins = nc.scalar.activation(piece(gate, at, n_at, a), acc, ACT.Sigmoid)
                ins.then_inc(gated, 1)

        @block.vector
        def _(dve):
            nc.vector.memset(K.u_prompt[:, :, 0:CPAD], 0.0).then_inc(padded, 1)
            dve.wait_ge(padded, 1)
            with dve.Fori(0, KU) as i:
                dve.wait_ge(K.unit_used[1], i + (base + 1))
                dve.wait_ge(gated, i + 1)
                for block_at, to, at, n_at in ((0, 0, 0, THIRD), (0, THIRD, THIRD, 512 - THIRD),
                                               (1, -CPAD, 512 - CPAD, CPAD), (1, 0, 512, 2 * THIRD - 512),
                                               (1, 2 * THIRD - 512, 2 * THIRD, SEQ - 2 * THIRD)):
                    a = K.ps[:, 3 + at // THIRD, at % THIRD:at % THIRD + n_at]
                    nc.vector.tensor_tensor(K.u_prompt[:, bass.ds(2 * i + block_at, 1), CPAD + to:CPAD + to + n_at],
                                            a, gate[:, at:at + n_at], ALU.mult)
                nc.vector.tensor_tensor(K.u_sample[:, bass.ds(i * DEC_B, DEC_B), CPAD:],
                                        K.ps[:, 5, SEQ % THIRD:T % THIRD].rearrange("p (b s) -> p b s", b=DEC_B),
                                        gate[:, SEQ:T].rearrange("p (b s) -> p b s", b=DEC_B),
                                        ALU.mult).then_inc(multiplied, 1)
    K.pair += KU
    K.fed += n


def rope_k_stage(nc, K):
    with ExitStack() as ctx:
        sem = semaphores(nc, ctx, "rope")
        part = ctx.enter_context(nc.sbuf_tensor("rope_part", [P, 2, T], F32))
        products, rotated = (sem(w) for w in ("products", "rotated"))
        stored = sem("stored")
        block = ctx.enter_context(nc.Block())

        @block.vector
        def _(dve):
            nc.vector.tensor_tensor(part[64:96, 0, :], K.lat[64:96, 5, :], K.rope[64:96, :], ALU.mult
                                    ).then_inc(products, 1)
            nc.vector.tensor_tensor(part[64:96, 1, :], K.lat[96:128, 5, :], K.rope[96:128, :], ALU.mult
                                    ).then_inc(products, 1)
            dve.wait_ge(products, 2)
            nc.vector.tensor_tensor(K.kh[64:96, :], part[64:96, 0, :], part[64:96, 1, :], ALU.add
                                    ).then_inc(rotated, 1)

        @block.sync
        def _(sp):
            sp.wait_ge(rotated, 1)
            sp.dma_start(K.A.k_rope_t, K.kh[64:96, :]).then_inc(stored, 16)
            for k in range(KU):
                sp.dma_start(K.A.conv_prompt_t[k], K.u_prompt[:, 2 * k + 1, 512:]).then_inc(stored, 16)
                sp.dma_start(K.A.conv_sample_t[k], K.u_sample[:, k * DEC_B:(k + 1) * DEC_B, DEC_S:]).then_inc(stored, 16)
            sp.wait_ge(stored, 16 + 32 * KU)


def gather_conv_stage(nc, K):
    with ExitStack() as ctx:
        block = ctx.enter_context(nc.Block())

        @block.scalar
        def _(act):
            for k in range(KU):
                nc.scalar.activation(K.mix[:, KU + k, 0:SEQ].rearrange("p (a t) -> p a t", a=2),
                                     K.cv_prompt[:, 2 * k:2 * k + 2, :], ACT.Identity)

        @block.vector
        def _(dve):
            for k in range(KU):
                nc.vector.tensor_copy(K.mix[:, KU + k, SEQ:T].rearrange("p (b s) -> p b s", b=DEC_B),
                                      K.cv_sample[:, k * DEC_B:(k + 1) * DEC_B, :])


def value_stage(nc, K):
    with ExitStack() as ctx:
        sem = semaphores(nc, ctx, "value")
        wuv_full, summed, copied = (sem(w)
                                    for w in ("wuv_full", "summed", "copied"))
        block = ctx.enter_context(nc.Block())

        @block.sync
        def _(sp):
            sp.dma_start(K.wuv[:, :, :], K.A.w_uv_t).then_inc(wuv_full, 16)

        @block.tensor
        def _(pe):
            pe.wait_ge(wuv_full, 16)
            for t in range(QT):
                if t >= 4:
                    pe.wait_ge(copied, t - 3)
                for l in range(KC):
                    mm = nc.tensor.matmul(K.ps[:, t % 4, :], K.c[:, l, t * P:(t + 1) * P], K.wuv[:, l, :],
                                          start=l == 0, stop=l == KC - 1)
                mm.then_inc(summed, 1)

        @block.scalar
        def _(act):
            for t in range(QT):
                act.wait_ge(summed, t + 1)
                nc.scalar.activation(K.v[:, t, :], K.ps[:, t % 4, :], ACT.Identity).then_inc(copied, 1)


def prompt_attention_stage(nc, K):
    with ExitStack() as ctx:
        def sb(what, shape):
            return ctx.enter_context(nc.sbuf_tensor(f"mla_{what}", shape, F32))

        sem = semaphores(nc, ctx, "mla")

        wh = sb("wh", [P, KQ * P + KC * NOPE + KV_LORA])
        wq = wh[:, 0:KQ * P].rearrange("p (k f) -> p k f", k=KQ)
        wuk = wh[:, KQ * P:KQ * P + KC * NOPE].rearrange("p (k f) -> p k f", k=KC)
        wuk_t = wh[0:NOPE, KQ * P + KC * NOPE:]
        qh = sb("qh", [P, T])
        part = sb("part", [P, 2, T])
        tap_done = sem("tap_done")
        prob = sb("prob", [P, 2, SEQ])
        prob_t = sb("prob_t", [P, 2, SEQ])
        top = sb("top", [P, QT])
        neg_top = sb("neg_top", [P, QT])
        den = sb("den", [P, QT])
        inv = sb("inv", [P, QT])
        w_full, proj_done, nope_ready, rope_parts, q_ready, ql_done, ql_copied = (
            sem(x) for x in ("w_full", "proj_done", "nope_ready", "rope_parts", "q_ready", "ql_done", "ql_copied"))
        scored, masked, top_found, top_ready, exped, turned, turned_copied, summed, inv_ready, normed = (
            sem(x) for x in ("scored", "masked", "top_found", "top_ready", "exped", "turned", "turned_copied",
                             "summed", "inv_ready", "normed"))
        block = ctx.enter_context(nc.Block())
        q_acc = region(K.ps, 0)
        k_acc = K.ps[0:NOPE, 4:6, :].rearrange("p a b -> p (a b)")
        turn = K.ps[:, 4:6, :].rearrange("p a b -> p (a b)")
        ql_acc = K.ps[:, 6, 0:KC * SAMPLE].rearrange("p (l t) -> p l t", l=KC)

        def score(i):
            return K.ps[:, 2 * (i % 2):2 * (i % 2) + 2, :].rearrange("p a b -> p (a b)")[:, 0:(i + 1) * P]

        @block.sync
        def _(sp):
            with sp.Fori(0, HEADS) as h:
                sp.wait_ge(ql_done, h)
                sp.dma_start(wh[:, :], K.A.w_head_t[bass.ds(h, 1)].rearrange("a p c -> p (a c)")
                             ).then_inc(w_full, 16)

        @block.tensor
        def _(pe):
            with pe.Fori(0, HEADS) as h:
                def scores(i):
                    if i >= 2:
                        pe.wait_ge(exped, h * QT + i - 1)
                    for at in range(0, (i + 1) * P, 512):
                        n = min(512, (i + 1) * P - at)
                        mm = nc.tensor.matmul(score(i)[:, at:at + n], qh[0:96, i * P:(i + 1) * P],
                                              K.kh[0:96, at:at + n], start=True, stop=True)
                    mm.then_inc(scored, 1)

                pe.wait_ge(w_full, h * 16 + 16)
                pe.wait_ge(exped, h * QT)
                pe.wait_ge(turned_copied, h * QT)
                for k in range(KQ):
                    for at, n in CHUNKS:
                        nc.tensor.matmul(q_acc[:, at:at + n], wq[:, k, :], K.qn[:, k, at:at + n],
                                         start=k == 0, stop=k == KQ - 1)
                for l in range(KC):
                    for at, n in CHUNKS[:2]:
                        mm = nc.tensor.matmul(k_acc[:, at:at + n], wuk[:, l, :], K.c[:, l, at:at + n],
                                              start=l == 0, stop=l == KC - 1)
                mm.then_inc(proj_done, 1)
                pe.wait_ge(nope_ready, h * 2 + 2)
                pe.wait_ge(q_ready, h + 1)
                pe.wait_ge(normed, h * QT)
                for l in range(KC):
                    mm = nc.tensor.matmul(ql_acc[:, l, :], wuk_t[:, l * P:(l + 1) * P], qh[0:NOPE, SEQ:T],
                                          start=True, stop=True)
                mm.then_inc(ql_done, 1)
                scores(0)
                scores(1)
                pe.wait_ge(ql_copied, h + 1)
                for i in range(QT):
                    pe.wait_ge(exped, h * QT + i + 1)
                    if i >= 1:
                        pe.wait_ge(turned_copied, h * QT + i)
                    for j in range(i + 1):
                        mm = nc.tensor.transpose(turn[:, j * P:(j + 1) * P], prob[:, i % 2, j * P:(j + 1) * P],
                                                 K.ident[:, :])
                    mm.then_inc(turned, 1)
                    if i + 2 < QT:
                        scores(i + 2)
                    pe.wait_ge(turned_copied, h * QT + i + 1)
                    if i >= 2:
                        pe.wait_ge(normed, h * QT + i - 1)
                    for j in range(i + 1):
                        mm = nc.tensor.matmul(K.ps[:, 6 + i % 2, 0:VH], prob_t[:, i % 2, j * P:(j + 1) * P],
                                              K.v[:, j, bass.ds(h * VH, VH)], start=j == 0, stop=j == i)
                    mm.then_inc(summed, 1)

        @block.scalar
        def _(act):
            with act.Fori(0, HEADS) as h:
                def exp(i):
                    act.wait_ge(top_ready, h * QT + i + 1)
                    nc.scalar.activation(prob[:, i % 2, 0:(i + 1) * P], score(i), ACT.Exp, bias=neg_top[:, i:i + 1],
                                         scale=SCALE, accum_out=den[:, i:i + 1]).then_inc(exped, 1)

                act.wait_ge(proj_done, h + 1)
                nc.scalar.activation(qh[0:NOPE, :], q_acc[0:NOPE, :], ACT.Identity).then_inc(nope_ready, 1)
                nc.scalar.activation(K.kh[0:NOPE, 0:SEQ], k_acc, ACT.Identity).then_inc(nope_ready, 1)
                exp(0)
                exp(1)
                for i in range(QT):
                    act.wait_ge(turned, h * QT + i + 1)
                    if i >= 2:
                        act.wait_ge(summed, h * QT + i - 1)
                    nc.scalar.activation(prob_t[:, i % 2, 0:(i + 1) * P], turn[:, 0:(i + 1) * P], ACT.Identity
                                         ).then_inc(turned_copied, 1)
                    if i + 2 < QT:
                        exp(i + 2)

        @block.vector
        def _(dve):
            with dve.Fori(0, HEADS) as h:
                def find_top(i):
                    n = h * QT + i + 1
                    diag = score(i)[:, i * P:(i + 1) * P]
                    dve.wait_ge(scored, n)
                    nc.vector.tensor_tensor(diag, diag, K.causal[:, :], ALU.add).then_inc(masked, 1)
                    dve.wait_ge(masked, n)
                    nc.vector.tensor_reduce(top[:, i:i + 1], score(i), AX_X, ALU.max).then_inc(top_found, 1)
                    dve.wait_ge(top_found, n)
                    nc.vector.tensor_scalar(neg_top[:, i:i + 1], top[:, i:i + 1], -SCALE, None, ALU.mult
                                            ).then_inc(top_ready, 1)

                def conv_taps(first, last):
                    base = h * (2 * CONV_W)
                    out_p, out_s = K.cv_prompt[:, bass.ds(h, 1), :], K.cv_sample[:, bass.ds(h * 4, 4), :]
                    for w in range(first, last):
                        in_p = K.u_prompt[:, bass.ds(h, 1), w:w + 512]
                        in_s = K.u_sample[:, bass.ds(h * 4, 4), w:w + DEC_S]
                        scale = K.vecs[:, bass.ds(h * CONV_W + (VEC_AT["w_dw"] + w), 1)]
                        if w == 0:
                            bias = K.vecs[:, bass.ds(h + VEC_AT["b_dw"], 1)]
                            nc.vector.tensor_scalar(out_p, in_p, scale, bias, ALU.mult, ALU.add
                                                    ).then_inc(tap_done, 1)
                            nc.vector.tensor_scalar(out_s, in_s, scale, bias, ALU.mult, ALU.add
                                                    ).then_inc(tap_done, 1)
                            continue
                        dve.wait_ge(tap_done, base + 2 * w - 1)
                        nc.vector.scalar_tensor_tensor(out_p, in_p, scale, out_p, ALU.mult, ALU.add
                                                       ).then_inc(tap_done, 1)
                        dve.wait_ge(tap_done, base + 2 * w)
                        nc.vector.scalar_tensor_tensor(out_s, in_s, scale, out_s, ALU.mult, ALU.add
                                                       ).then_inc(tap_done, 1)

                conv_taps(0, 7)
                dve.wait_ge(proj_done, h + 1)
                nc.vector.tensor_tensor(part[64:96, 0, :], q_acc[64:96, :], K.rope[64:96, :], ALU.mult
                                        ).then_inc(rope_parts, 1)
                nc.vector.tensor_tensor(part[64:96, 1, :], q_acc[96:128, :], K.rope[96:128, :], ALU.mult
                                        ).then_inc(rope_parts, 1)
                dve.wait_ge(rope_parts, h * 2 + 2)
                nc.vector.tensor_tensor(qh[64:96, :], part[64:96, 0, :], part[64:96, 1, :], ALU.add
                                        ).then_inc(q_ready, 1)
                dve.wait_ge(q_ready, h + 1)
                nc.vector.tensor_copy(K.qpe[64:96, :, bass.ds(h, 1), :].rearrange("p b a s -> p b (a s)"),
                                      qh[64:96, SEQ:T].rearrange("p (b s) -> p b s", b=DEC_B))
                dve.wait_ge(ql_done, h + 1)
                for l in range(KC):
                    ins = nc.vector.tensor_copy(
                        K.qlat[:, l, :, bass.ds(h, 1), :].rearrange("p b a s -> p b (a s)"),
                        ql_acc[:, l, :].rearrange("p (b s) -> p b s", b=DEC_B))
                ins.then_inc(ql_copied, 1)
                find_top(0)
                find_top(1)
                for i in range(QT):
                    if i + 2 < QT:
                        find_top(i + 2)
                    conv_taps(7 + 3 * i, 10 + 3 * i)
                    dve.wait_ge(exped, h * QT + i + 1)
                    nc.vector.reciprocal(inv[:, i:i + 1], den[:, i:i + 1]).then_inc(inv_ready, 1)
                    dve.wait_ge(inv_ready, h * QT + i + 1)
                    dve.wait_ge(summed, h * QT + i + 1)
                    nc.vector.tensor_scalar(K.attn[:, i, bass.ds(h * VH, VH)], K.ps[:, 6 + i % 2, 0:VH],
                                            inv[:, i:i + 1], None, ALU.mult).then_inc(normed, 1)


def turn_attention_stage(nc, K):
    with ExitStack() as ctx:
        sem = semaphores(nc, ctx, "turn")
        turned, copied = (sem(w) for w in ("turned", "copied"))
        block = ctx.enter_context(nc.Block())

        @block.tensor
        def _(pe):
            for t in range(QT):
                if t >= 4:
                    pe.wait_ge(copied, t - 3)
                for f in range(4):
                    mm = nc.tensor.transpose(K.ps[:, t % 4, f * P:(f + 1) * P], K.attn[:, t, f * P:(f + 1) * P],
                                             K.ident[:, :])
                mm.then_inc(turned, 1)

        @block.vector
        def _(dve):
            for t in range(QT):
                dve.wait_ge(turned, t + 1)
                nc.vector.tensor_copy(K.mix[:, 0:4, t * P:(t + 1) * P],
                                      K.ps[:, t % 4, :].rearrange("p (f q) -> p f q", f=4)).then_inc(copied, 1)


def paged_attention_stage(nc, K):
    with ExitStack() as ctx:
        def sb(what, shape, dt=F32):
            return ctx.enter_context(nc.sbuf_tensor(f"paged_{what}", shape, dt))

        sem = semaphores(nc, ctx, "paged")

        R = HEADS * DEC_S
        BANK = 512 // P
        GROUPS = PER_ROW * KC // BANK
        ROPE_AT = PER_ROW * KV_LORA
        ACT_GROUPS, DVE_GROUPS = [0, 1, 2, GROUPS - 1, GROUPS], list(range(3, GROUPS - 1))
        past = [sb(f"past{s}", [P, PER_ROW * (KV_LORA + ROPE)]) for s in range(2)]
        all_q_rope = sb("all_q_rope", [P, DEC_B, BANK * R])
        q_rope = sb("q_rope", [P, BANK * R])
        q_lat = sb("q_lat", [P, KC, R])
        rope_t = sb("rope_t", [P, BANK * P])
        lat_t = sb("lat_t", [P, KC, PAST])
        new_rope_t = sb("new_rope_t", [P, SAMPLE])
        new_rows = sb("new_rows", [SAMPLE, KV_LORA])
        mask = sb("mask", [R, DEC_B * SAMPLE])
        prob = sb("prob", [R, PAST + SAMPLE])
        prob_t = sb("prob_t", [P, PER_ROW * R])
        prob_new = sb("prob_new", [SAMPLE, R])
        o = sb("o", [R, KV_LORA])
        tops, sums = sb("tops", [R, 3]), sb("sums", [R, 4])
        gathered = [sem(f"gathered{s}") for s in range(2)]
        prepared, rows_turned, rows_copied, mask_in = (
            sem(x) for x in ("prepared", "rows_turned", "rows_copied", "mask_in"))
        turned, act_copied, dve_copied, staged, scored = (
            sem(x) for x in ("turned", "act_copied", "dve_copied", "staged", "scored"))
        new_masked, tops_found, top_ready, exped, summed, inv_ready = (
            sem(x) for x in ("new_masked", "tops_found", "top_ready", "exped", "summed", "inv_ready"))
        probs_turned, act_probs, dve_probs, attended, normed, o_turned, o_copied, may_go = (
            sem(x) for x in ("probs_turned", "act_probs", "dve_probs", "attended", "normed", "o_turned", "o_copied",
                             "may_go"))
        block = ctx.enter_context(nc.Block())
        scores = K.ps[0:R, 0:BANK, :].rearrange("p a b -> p (a b)")
        prob_banks = [K.ps[:, 6, :], K.ps[:, 5, :]]
        last = K.ps[:, 7, :]
        o_acc, s_new = last[0:R, 0:KV_LORA], last[0:R, 256:256 + SAMPLE]
        new_turn, o_turn = K.ps[0:SAMPLE, 0, 0:R], K.ps[:, 6, 0:KC * R]
        half = PER_ROW // 2 * R

        def bank(q):
            return K.ps[:, 4 + q % 2, :]

        def token(position):
            own, j = divmod(position, BANK)
            return j * BANK + own

        def sequences(step):
            def loop(engine):
                with engine.Fori(0, DEC_B // 2 - 1) as i:
                    for s in range(2):
                        step(2 * i + s, s, True)
                for s in range(2):
                    step(DEC_B - 2 + s, s, s == 0)
            return loop

        @block.gpsimd
        def _(pool):
            for b in range(DEC_B):
                if b >= 2:
                    pool.wait_ge(attended, b - 1)
                pool.indirect_dma_start(
                    out=past[b % 2][:, :], out_offset=None, in_=K.A.cache,
                    in_offset=bass.IndirectOffsetOnAxis(ap=K.page_rows[:, b:b + 1], axis=0)
                ).then_inc(gathered[b % 2], 16)

        @block.sync
        def _(sp):
            sp.dma_start(mask[:, :], K.A.new_mask).then_inc(mask_in, 16)

        @block.tensor
        def _(pe):
            def copied(b, q):
                if q in ACT_GROUPS:
                    pe.wait_ge(act_copied, b * len(ACT_GROUPS) + (ACT_GROUPS.index(q) + 1))
                else:
                    pe.wait_ge(dve_copied, b * len(DVE_GROUPS) + (DVE_GROUPS.index(q) + 1))

            def turn(b, s):
                for q in range(GROUPS + 1):
                    if q == 0:
                        pe.wait_ge(act_copied, b * len(ACT_GROUPS))
                        tiles = [ROPE_AT + j * P for j in range(BANK)]
                    else:
                        if q >= 2:
                            copied(b, q - 2)
                        tiles = [(token(t) * KC + l) * P for l in range(KC) for t in (2 * q - 2, 2 * q - 1)]
                    for j, at in enumerate(tiles):
                        mm = nc.tensor.transpose(bank(q)[:, j * P:(j + 1) * P], past[s][:, at:at + P], K.ident[:, :])
                    mm.then_inc(turned, 1)

            def score(b, between=None):
                copied(b, GROUPS)
                copied(b, GROUPS - 2)
                pe.wait_ge(staged, 2 * b + 2)
                for c in range(BANK):
                    at = slice(c * 512, (c + 1) * 512)
                    nc.tensor.matmul(scores[:, at], q_rope[:, c * R:(c + 1) * R], rope_t[:, :], start=True, stop=False)
                    for l in range(KC):
                        nc.tensor.matmul(scores[:, at], q_lat[:, l, :], lat_t[:, l, at], start=False, stop=l == KC - 1)
                    if c == 1 and between is not None:
                        between()
                nc.tensor.matmul(s_new, q_rope[:, 2 * R:3 * R], new_rope_t[:, :], start=True, stop=False)
                for l in range(KC):
                    mm = nc.tensor.matmul(s_new, q_lat[:, l, :], K.c[:, l, SEQ:T], start=False, stop=l == KC - 1)
                mm.then_inc(scored, 1)

            def attend(b, s, more):
                pe.wait_ge(exped, 2 * b + 2)
                if more:
                    copied(b + 1, GROUPS - 1)
                pe.wait_ge(o_copied, KC * b)
                pe.sem_inc(may_go, 1)
                for h in range(2):
                    for j in range(PER_ROW // 2):
                        t = h * (PER_ROW // 2) + j
                        mm = nc.tensor.transpose(prob_banks[h][:, j * R:(j + 1) * R], prob[:, t * P:(t + 1) * P],
                                                 K.ident[0:R, 0:R])
                    if h == 0:
                        mm.then_inc(probs_turned, 1)
                nc.tensor.transpose(new_turn, prob[:, PAST:], K.ident[0:R, 0:R]).then_inc(probs_turned, 1)
                pe.wait_ge(act_probs, b + 1)
                for t in range(PER_ROW):
                    if t == PER_ROW // 2:
                        pe.wait_ge(dve_probs, b + 1)
                    at = token(t) * KV_LORA
                    nc.tensor.matmul(o_acc, prob_t[:, t * R:(t + 1) * R], past[s][:, at:at + KV_LORA], start=t == 0,
                                     stop=False)
                nc.tensor.matmul(o_acc, prob_new[:, :], new_rows[:, :], start=False, stop=True).then_inc(attended, 1)

            def turn_out(b):
                pe.wait_ge(normed, b + 1)
                pe.sem_inc(may_go, 1)
                for l in range(KC):
                    mm = nc.tensor.transpose(o_turn[:, l * R:(l + 1) * R], o[:, l * P:(l + 1) * P],
                                             K.ident[0:R, 0:R])
                mm.then_inc(o_turned, 1)

            pe.wait_ge(prepared, 5)
            for l in range(KC):
                mm = nc.tensor.transpose(last[0:SAMPLE, l * P:(l + 1) * P], K.c[:, l, SEQ:T], K.ident[:, :])
            mm.then_inc(rows_turned, 1)
            pe.wait_ge(gathered[0], 16)
            turn(0, 0)
            pe.wait_ge(rows_copied, 1)
            score(0)

            def step(b, s, more):
                if more:
                    pe.wait_ge(gathered[1 - s], 8 * (b + s) + 16)
                    pe.wait_ge(dve_probs, b)
                    turn(b + 1, 1 - s)
                attend(b, s, more)
                if more:
                    score(b + 1, lambda: turn_out(b))
                else:
                    turn_out(b)

            sequences(step)(pe)

        @block.scalar
        def _(act):
            def copies(b, groups):
                for q in groups:
                    act.wait_ge(turned, b * (GROUPS + 1) + (q + 1))
                    if q == 0:
                        nc.scalar.activation(rope_t[:, :], bank(q), ACT.Identity).then_inc(act_copied, 1)
                    else:
                        nc.scalar.activation(lat_t[:, :, (2 * q - 2) * P:2 * q * P],
                                             bank(q).rearrange("p (l c) -> p l c", l=KC), ACT.Identity
                                             ).then_inc(act_copied, 1)

            def stage(b):
                act.wait_ge(scored, b)
                nc.scalar.activation(q_lat[:, :, :], K.qlat[:, :, bass.ds(b, 1), :, :].rearrange(
                    "p l a h s -> p l (a h s)"), ACT.Identity).then_inc(staged, 1)
                nc.scalar.activation(q_rope[:, :], all_q_rope[:, bass.ds(b, 1), :].rearrange("p a r -> p (a r)"),
                                     ACT.Identity).then_inc(staged, 1)

            act.wait_ge(prepared, 5)
            stage(0)
            copies(0, ACT_GROUPS)

            def step(b, s, more):
                if more:
                    stage(b + 1)
                    copies(b + 1, ACT_GROUPS[0:3])
                act.wait_ge(top_ready, b + 1)
                act.wait_ge(probs_turned, 2 * b)
                nc.scalar.activation(prob[:, 0:PAST], scores, ACT.Exp, bias=tops[:, 2:3], scale=SCALE,
                                     accum_out=sums[:, 0:1]).then_inc(exped, 1)
                nc.scalar.activation(prob[:, PAST:], s_new, ACT.Exp, bias=tops[:, 2:3], scale=SCALE,
                                     accum_out=sums[:, 1:2]).then_inc(exped, 1)
                if more:
                    copies(b + 1, ACT_GROUPS[3:])
                act.wait_ge(probs_turned, 2 * b + 1)
                act.wait_ge(attended, b)
                nc.scalar.activation(prob_t[:, 0:half], prob_banks[0], ACT.Identity).then_inc(act_probs, 1)

            sequences(step)(act)

        @block.vector
        def _(dve):
            def copies(b):
                dve.wait_ge(scored, b)
                for q in DVE_GROUPS:
                    dve.wait_ge(turned, b * (GROUPS + 1) + (q + 1))
                    nc.vector.tensor_copy(lat_t[:, :, (2 * q - 2) * P:2 * q * P],
                                          bank(q).rearrange("p (l c) -> p l c", l=KC)).then_inc(dve_copied, 1)

            nc.vector.memset(all_q_rope[:, :, :], 0.0).then_inc(prepared, 1)
            nc.vector.memset(new_rope_t[:, :], 0.0).then_inc(prepared, 1)
            dve.wait_ge(prepared, 2)
            for own in range(BANK):
                ins = nc.vector.tensor_copy(all_q_rope[own * ROPE:(own + 1) * ROPE, :, own * R:(own + 1) * R],
                                            K.qpe[64:96, :, :, :].rearrange("p b h s -> p b (h s)"))
            ins.then_inc(prepared, 2)
            nc.vector.tensor_copy(new_rope_t[64:96, :], K.kh[64:96, SEQ:T]).then_inc(prepared, 1)
            dve.wait_ge(rows_turned, 1)
            nc.vector.tensor_copy(new_rows[:, :], last[0:SAMPLE, 0:KV_LORA]).then_inc(rows_copied, 1)
            copies(0)
            dve.wait_ge(mask_in, 16)

            def step(b, s, more):
                dve.wait_ge(scored, b + 1)
                nc.vector.tensor_tensor(s_new, s_new, mask[:, bass.ds(b * SAMPLE, SAMPLE)], ALU.add
                                        ).then_inc(new_masked, 1)
                nc.vector.tensor_reduce(tops[:, 0:1], scores, AX_X, ALU.max).then_inc(tops_found, 1)
                dve.wait_ge(new_masked, b + 1)
                nc.vector.tensor_reduce(tops[:, 1:2], s_new, AX_X, ALU.max).then_inc(tops_found, 1)
                dve.wait_ge(tops_found, 2 * b + 2)
                nc.vector.tensor_scalar(tops[:, 2:3], tops[:, 0:1], tops[:, 1:2], -SCALE, ALU.max, ALU.mult
                                        ).then_inc(top_ready, 1)
                if more:
                    copies(b + 1)
                dve.wait_ge(exped, 2 * b + 2)
                nc.vector.tensor_tensor(sums[:, 2:3], sums[:, 0:1], sums[:, 1:2], ALU.add).then_inc(summed, 1)
                dve.wait_ge(summed, b + 1)
                nc.vector.reciprocal(sums[:, 3:4], sums[:, 2:3]).then_inc(inv_ready, 1)
                dve.wait_ge(probs_turned, 2 * b + 2)
                dve.wait_ge(attended, b)
                nc.vector.tensor_copy(prob_new[:, :], new_turn)
                nc.vector.tensor_copy(prob_t[:, half:], prob_banks[1]).then_inc(dve_probs, 1)
                dve.wait_ge(inv_ready, b + 1)
                dve.wait_ge(attended, b + 1)
                nc.vector.tensor_scalar(o[:, :], o_acc, sums[:, 3:4], None, ALU.mult).then_inc(normed, 1)
                dve.wait_ge(o_turned, b + 1)
                for l in range(KC):
                    nc.vector.tensor_copy(K.olat[:, l, :, bass.ds(b * DEC_S, DEC_S)],
                                          o_turn[:, l * R:(l + 1) * R].rearrange("p (h s) -> p h s", h=HEADS)
                                          ).then_inc(o_copied, 1)

            sequences(step)(dve)


def sample_value_stage(nc, K):
    with ExitStack() as ctx:
        sem = semaphores(nc, ctx, "sv")
        summed, copied = (sem(w) for w in ("summed", "copied"))
        block = ctx.enter_context(nc.Block())

        @block.tensor
        def _(pe):
            for j in range(HEADS // 2):
                for par in range(2):
                    for l in range(KC):
                        mm = nc.tensor.matmul(K.ps[:, j, par * SAMPLE:(par + 1) * SAMPLE],
                                              K.wuv[:, l, j * P:(j + 1) * P], K.olat[:, l, 2 * j + par, :],
                                              start=l == 0, stop=l == KC - 1)
                mm.then_inc(summed, 1)

        @block.vector
        def _(dve):
            for j in range(HEADS // 2):
                dve.wait_ge(summed, j + 1)
                for par in range(2):
                    rows = slice(par * VH, (par + 1) * VH)
                    nc.vector.tensor_copy(K.mix[rows, j, SEQ:T], K.ps[rows, j, par * SAMPLE:(par + 1) * SAMPLE])


def memory_stage(nc, K, halves, mem_k, mem_v):
    with ExitStack() as ctx:
        sem = semaphores(nc, ctx, "mem")
        hi, lo = halves
        base, used = K.pair, K.unit_used
        copied = [sem(f"copied{s}") for s in range(2)]
        stored = sem("stored")
        block = ctx.enter_context(nc.Block())

        @block.sync
        def _(sp):
            load_units(sp, K, KD - 1)
            sp.wait_ge(copied[0], KD)
            sp.dma_start(K.A.mem_k_t, mem_k[:, :, :]).then_inc(stored, 16)
            sp.wait_ge(copied[1], KD)
            sp.dma_start(K.A.mem_v_t, mem_v[:, :, :]).then_inc(stored, 16)
            sp.wait_ge(stored, 32)

        @block.tensor
        def _(pe):
            with pe.Fori(0, KD) as f:
                pe.wait_ge(K.split_done[0], f + (base + 1))
                pe.wait_ge(copied[0], f)
                accumulate(nc, K, lambda at, n: K.ps[:, 0, at:at + n], 0, lambda k, at, n: hi[:, k, :], lambda k, at, n: lo[:, k, :],
                           chunks=[(0, N_MEM)]).then_inc(used[0], 1)
                pe.wait_ge(K.split_done[1], f + (base + 1))
                pe.wait_ge(copied[1], f)
                for n in range(N_MEM // P):
                    for k in range(KD):
                        w_hi, w_lo = (w[:, 1, k * P:(k + 1) * P] for w in (K.w_hi, K.w_lo))
                        x_hi, x_lo = (x[:, k, n * P:(n + 1) * P] for x in halves)
                        for p, (x, w) in enumerate(((x_hi, w_hi), (x_hi, w_lo), (x_lo, w_hi))):
                            mm = nc.tensor.matmul(K.ps[:, 1 + n, 0:P], x, w, start=k == 0 and p == 0,
                                                  stop=k == KD - 1 and p == 2)
                mm.then_inc(used[1], 1)

        @block.scalar
        def _(act):
            def high_half(j, s):
                act.wait_ge(K.unit_in[s], 16 * j + 16)
                act.wait_ge(used[s], j)
                nc.scalar.activation(K.w_hi[:, s, :], K.raw[:, s, :], ACT.Identity).then_inc(K.hi_done[s], 1)

            def copy(f):
                act.wait_ge(used[0], f + (base + 1))
                nc.scalar.activation(mem_k[:, bass.ds(f, 1), :], K.ps[:, 0, 0:N_MEM], ACT.Identity
                                     ).then_inc(copied[0], 1)

            with act.Fori(0, KD - 1) as f:
                high_half(f + (base + 1), 0)
                copy(f)
                high_half(f + (base + 1), 1)
            copy(KD - 1)

        @block.vector
        def _(dve):
            def low_half(j, s):
                dve.wait_ge(K.hi_done[s], j + 1)
                nc.vector.tensor_tensor(K.w_lo[:, s, :], K.raw[:, s, :], K.w_hi[:, s, :].bitcast(F32), ALU.subtract
                                        ).then_inc(K.split_done[s], 1)

            def copy(f):
                dve.wait_ge(used[1], f + (base + 1))
                nc.vector.tensor_copy(mem_v[:, :, bass.ds(f * P, P)], K.ps[:, 1:3, 0:P]).then_inc(copied[1], 1)

            with dve.Fori(0, KD - 1) as f:
                low_half(f + (base + 1), 0)
                copy(f)
                low_half(f + (base + 1), 1)
            copy(KD - 1)
    K.pair += KD
    K.fed += KD - 1


def prompt_cross_stage(nc, K, halves, mem_k, mem_v, xo, xq_sample):
    with ExitStack() as ctx:
        def sb(what, shape):
            return ctx.enter_context(nc.sbuf_tensor(f"xp_{what}", shape, F32))

        sem = semaphores(nc, ctx, "xp")

        GROUPS = QT // 2
        q, q_next = sb("q", [P, 2, T]), sb("q_next", [P, T])
        vh = sb("vh", [P, 2, XD])
        prob = sb("prob", [P, 2, N_MEM])
        prob_t = sb("prob_t", [P, 2, 2, 2 * P])
        top, neg_top, den, inv = (sb(x, [P, QT]) for x in ("top", "neg_top", "den", "inv"))
        hi, lo = halves
        base, used = K.pair, K.unit_used
        q_kept, q_set, vh_set, scored, top_found, top_ready, exped, inv_ready, normed, turned, turned_copied = (
            sem(x) for x in ("q_kept", "q_set", "vh_set", "scored", "top_found", "top_ready", "exped", "inv_ready",
                             "normed", "turned", "turned_copied"))
        q_odd_set, sample_kept, summed, out = (sem(x) for x in ("q_odd_set", "sample_kept", "summed", "out"))
        block = ctx.enter_context(nc.Block())
        turn = K.ps[:, 5, :].rearrange("p (n c) -> p n c", n=2)
        fed = feed(nc, K, block, XH, True)

        def score(i):
            return K.ps[:, 3 + i % 2, 0:N_MEM]

        def heads(body):
            def loop(engine):
                with engine.Fori(0, XH - 1) as h:
                    body(h, True)
                body(XH - 1, False)
            return loop

        @block.tensor
        def _(pe):
            def project(h, s, first, last):
                if first == 0:
                    pe.wait_ge(q_odd_set if s == 0 else q_kept, h + s)
                    pe.wait_ge(K.split_done[s], h + (base + 1))
                mm = accumulate(nc, K, thirds(K.ps, 0), s, lambda _, at, n: hi_of(first, _, at, n),
                                lambda _, at, n: lo_of(first, _, at, n), first=first == 0, last=last == KD,
                                tiles=list(range(first, last)))
                if last == KD:
                    mm.then_inc(used[s], 1)

            def hi_of(first, k, at, n):
                return hi[:, first + k, at:at + n]

            def lo_of(first, k, at, n):
                return lo[:, first + k, at:at + n]

            def scores(h, i):
                pe.wait_ge(exped, h * QT + max(i - 1, 0))
                for k in range(2):
                    mm = nc.tensor.matmul(score(i), q[:, k, i * P:(i + 1) * P],
                                          mem_k[:, bass.ds(2 * h + k, 1), :].rearrange("p a n -> p (a n)"),
                                          start=k == 0, stop=k == 1)
                mm.then_inc(scored, 1)

            for s in range(2):
                project(0, s, 0, KD)

            def body(h, more):
                pe.wait_ge(q_set, h + 1)
                pe.wait_ge(q_odd_set, h + 1)
                scores(h, 0)
                scores(h, 1)
                for i in range(QT):
                    g = i // 2
                    pe.wait_ge(normed, h * QT + i + 1)
                    pe.wait_ge(turned_copied, h * GROUPS + g)
                    for n in range(2):
                        mm = nc.tensor.transpose(turn[:, n, (i % 2) * P:(i % 2 + 1) * P],
                                                 prob[:, i % 2, n * P:(n + 1) * P], K.ident[:, :])
                    mm.then_inc(turned, 1)
                    if i + 2 < QT:
                        scores(h, i + 2)
                    if more:
                        s, k = divmod(2 * i, KD)
                        project(h + 1, s, k, k + 2)
                    if i % 2 == 1:
                        pe.wait_ge(turned_copied, h * GROUPS + g + 1)
                        pe.wait_ge(vh_set, h + 1)
                        pe.wait_ge(out, h * GROUPS + g)
                        for f in range(2):
                            for n in range(2):
                                mm = nc.tensor.matmul(K.ps[:, 6 + f, 0:2 * P], vh[:, n, f * P:(f + 1) * P],
                                                      prob_t[:, g % 2, n, :], start=n == 0, stop=n == 1)
                        mm.then_inc(summed, 1)

            heads(body)(pe)

        @block.scalar
        def _(act):
            def keep_q(h):
                act.wait_ge(used[0], h + (base + 1))
                act.wait_ge(q_set, h)
                for acc, at, n, a in pieces(K.ps, 0):
                    ins = nc.scalar.activation(piece(q_next, at, n, a), acc, ACT.Identity)
                ins.then_inc(q_kept, 1)

            def set_q(h):
                act.wait_ge(q_kept, h + 1)
                act.wait_ge(scored, h * QT)
                act.wait_ge(sample_kept, h)
                nc.scalar.activation(q[:, 0, :], q_next[:, :], ACT.Identity).then_inc(q_set, 1)
                act.wait_ge(summed, h * GROUPS)
                nc.scalar.activation(vh[:, :, :], mem_v[:, :, bass.ds(h * XD, XD)], ACT.Identity
                                     ).then_inc(vh_set, 1)

            def exp(h, i):
                act.wait_ge(top_ready, h * QT + i + 1)
                act.wait_ge(turned, h * QT + max(i - 1, 0))
                nc.scalar.activation(prob[:, i % 2, :], score(i), ACT.Exp, bias=neg_top[:, i:i + 1],
                                     scale=X_SCALE, accum_out=den[:, i:i + 1]).then_inc(exped, 1)

            def copy_turned(h, g):
                act.wait_ge(turned, h * QT + 2 * g + 2)
                act.wait_ge(summed, h * GROUPS + max(g - 1, 0))
                nc.scalar.activation(prob_t[:, g % 2, :, :], turn, ACT.Identity).then_inc(turned_copied, 1)

            keep_q(0)
            set_q(0)

            def body(h, more):
                for i in range(2):
                    exp(h, i)
                for g in range(GROUPS - 1):
                    exp(h, 2 * g + 2)
                    copy_turned(h, g)
                    exp(h, 2 * g + 3)
                    if g == 1 and more:
                        keep_q(h + 1)
                copy_turned(h, GROUPS - 1)
                if more:
                    set_q(h + 1)

            heads(body)(act)

        @block.vector
        def _(dve):
            def set_q_odd(h):
                dve.wait_ge(used[1], h + (base + 1))
                dve.wait_ge(scored, h * QT)
                dve.wait_ge(sample_kept, h)
                for acc, at, n, a in pieces(K.ps, 0):
                    ins = nc.vector.tensor_copy(piece(q[:, 1, :], at, n, a), acc)
                ins.then_inc(q_odd_set, 1)

            def find_top(h, i):
                n = h * QT + i + 1
                dve.wait_ge(scored, n)
                nc.vector.tensor_reduce(top[:, i:i + 1], score(i), AX_X, ALU.max).then_inc(top_found, 1)
                dve.wait_ge(top_found, n)
                nc.vector.tensor_scalar(neg_top[:, i:i + 1], top[:, i:i + 1], -X_SCALE, None, ALU.mult
                                        ).then_inc(top_ready, 1)

            def copy_out(h, g):
                dve.wait_ge(summed, h * GROUPS + g + 1)
                nc.vector.tensor_copy(xo[:, bass.ds(2 * h, 2), g * 2 * P:(g + 1) * 2 * P], K.ps[:, 6:8, 0:2 * P]
                                      ).then_inc(out, 1)

            set_q_odd(0)

            def body(h, more):
                find_top(h, 0)
                find_top(h, 1)
                dve.wait_ge(q_odd_set, h + 1)
                dve.wait_ge(q_set, h + 1)
                nc.vector.tensor_copy(xq_sample[:, bass.ds(2 * h, 2), :], q[:, :, SEQ:T]).then_inc(sample_kept, 1)
                for i in range(QT):
                    dve.wait_ge(exped, h * QT + i + 1)
                    nc.vector.reciprocal(inv[:, i:i + 1], den[:, i:i + 1]).then_inc(inv_ready, 1)
                    dve.wait_ge(inv_ready, h * QT + i + 1)
                    nc.vector.tensor_scalar(prob[:, i % 2, :], prob[:, i % 2, :], inv[:, i:i + 1], None, ALU.mult
                                            ).then_inc(normed, 1)
                    if i % 2 == 0 and i > 0:
                        copy_out(h, i // 2 - 1)
                    if i + 2 < QT:
                        find_top(h, i + 2)
                if more:
                    set_q_odd(h + 1)
                copy_out(h, GROUPS - 1)

            heads(body)(dve)
    K.pair += XH
    K.fed += fed


def sample_cross_stage(nc, K, xo, xq_sample):
    with ExitStack() as ctx:
        def sb(what, shape):
            return ctx.enter_context(nc.sbuf_tensor(f"xs_{what}", shape, F32))

        sem = semaphores(nc, ctx, "xs")

        R = XH * DEC_S
        may_turn = sem("may_turn")
        keys = sb("keys", [P, 2, KD, N_MEM])
        vals = sb("vals", [P, 2, 2, D_MODEL])
        qd = sb("qd", [P, 2, KD, R])
        prob = sb("prob", [R, 2, N_MEM])
        prob_t = sb("prob_t", [P, 2, 2, R])
        stats = sb("stats", [R, 2, 4])
        loaded = [sem(f"loaded{s}") for s in range(2)]
        cleared, staged, scored, top_found, top_ready, exped, inv_ready, normed, turned, turned_copied, summed, out = (
            sem(x) for x in ("cleared", "staged", "scored", "top_found", "top_ready", "exped", "inv_ready", "normed",
                             "turned", "turned_copied", "summed", "out"))
        block = ctx.enter_context(nc.Block())

        @block.gpsimd
        def _(pool):
            split_units(nc, pool, K, 1)

        @block.sync
        def _(sp):
            load_units(sp, K, 1)
            with sp.Fori(0, DEC_B // 2) as i:
                for s in range(2):
                    sp.wait_ge(summed, 2 * i)
                    sp.dma_start(keys[:, s, :, :], K.A.cache_k_t[bass.ds(2 * i + s, 1)].rearrange(
                        "a p k n -> p (a k) n")).then_inc(loaded[s], 16)
                    sp.dma_start(vals[:, s, :, :], K.A.cache_v_t[bass.ds(2 * i + s, 1)].rearrange(
                        "a p k n -> p (a k) n")).then_inc(loaded[s], 16)

        @block.tensor
        def _(pe):
            with pe.Fori(0, DEC_B // 2) as i:
                for s in range(2):
                    b = 2 * i + s
                    pe.wait_ge(loaded[s], i * 32 + 32)
                    pe.wait_ge(staged, b * 4 + 4)
                    pe.wait_ge(exped, b)
                    for k in range(KD):
                        mm = nc.tensor.matmul(K.ps[0:R, 4 * s, 0:N_MEM], qd[:, s, k, :], keys[:, s, k, :],
                                              start=k == 0, stop=k == KD - 1)
                    mm.then_inc(scored, 1)
                    pe.wait_ge(normed, b + 1)
                    pe.sem_inc(may_turn, 1)
                    for n in range(2):
                        mm = nc.tensor.transpose(K.ps[:, 4 * s + 1, n * R:(n + 1) * R],
                                                 prob[:, s, n * P:(n + 1) * P], K.ident[0:R, 0:R])
                    mm.then_inc(turned, 1)
                    pe.wait_ge(turned_copied, b + 1)
                    for f in range(KD):
                        for n in range(2):
                            mm = nc.tensor.matmul(K.ps[:, 4 * s + 2, f * DEC_S:(f + 1) * DEC_S],
                                                  vals[:, s, n, f * P:(f + 1) * P],
                                                  prob_t[:, s, n, (f // 2) * DEC_S:(f // 2 + 1) * DEC_S],
                                                  start=n == 0, stop=n == 1)
                    mm.then_inc(summed, 1)

        @block.scalar
        def _(act):
            act.wait_ge(cleared, 1)
            with act.Fori(0, DEC_B // 2) as i:
                for s in range(2):
                    b = 2 * i + s
                    act.wait_ge(scored, 2 * i)
                    for h in range(XH):
                        nc.scalar.activation(qd[:, s, 2 * h:2 * h + 2, h * DEC_S:(h + 1) * DEC_S],
                                             xq_sample[:, 2 * h:2 * h + 2, bass.ds(b * DEC_S, DEC_S)], ACT.Identity
                                             ).then_inc(staged, 1)
                    act.wait_ge(top_ready, b + 1)
                    act.wait_ge(turned, 2 * i)
                    nc.scalar.activation(prob[:, s, :], K.ps[0:R, 4 * s, 0:N_MEM], ACT.Exp, bias=stats[:, s, 1:2],
                                         scale=X_SCALE, accum_out=stats[:, s, 2:3]).then_inc(exped, 1)

        @block.vector
        def _(dve):
            nc.vector.memset(qd[:, :, :, :], 0.0).then_inc(cleared, 1)
            with dve.Fori(0, DEC_B // 2) as i:
                for s in range(2):
                    b = 2 * i + s
                    dve.wait_ge(scored, b + 1)
                    nc.vector.tensor_reduce(stats[:, s, 0:1], K.ps[0:R, 4 * s, 0:N_MEM], AX_X, ALU.max
                                            ).then_inc(top_found, 1)
                    dve.wait_ge(top_found, b + 1)
                    nc.vector.tensor_scalar(stats[:, s, 1:2], stats[:, s, 0:1], -X_SCALE, None, ALU.mult
                                            ).then_inc(top_ready, 1)
                    dve.wait_ge(exped, b + 1)
                    nc.vector.reciprocal(stats[:, s, 3:4], stats[:, s, 2:3]).then_inc(inv_ready, 1)
                    dve.wait_ge(inv_ready, b + 1)
                    nc.vector.tensor_scalar(prob[:, s, :], prob[:, s, :], stats[:, s, 3:4], None, ALU.mult
                                            ).then_inc(normed, 1)
                    dve.wait_ge(turned, b + 1)
                    nc.vector.tensor_copy(prob_t[:, s, :, :].rearrange("p n r -> p (n r)"),
                                          K.ps[:, 4 * s + 1, 0:2 * R]).then_inc(turned_copied, 1)
                    dve.wait_ge(summed, b + 1)
                    nc.vector.tensor_copy(xo[:, :, bass.ds(SEQ + b * DEC_S, DEC_S)],
                                          K.ps[:, 4 * s + 2, 0:KD * DEC_S].rearrange("p (f s) -> p f s", f=KD)
                                          ).then_inc(out, 1)
    K.fed += 1


def ffn_stage(nc, K, halves, y):
    hi, lo = halves
    STEPS = KF // 2
    with ExitStack() as ctx:
        def sb(what, shape, dt=F32):
            return ctx.enter_context(nc.sbuf_tensor(f"ffn_{what}", shape, dt))

        sem = semaphores(nc, ctx, "ffn")
        g_prompt = sb("g_prompt", [P, FPAD + SEQ])
        g_sample = sb("g_sample", [P, DEC_B, FPAD + DEC_S])
        hist = sb("hist", [P, KF, DEC_B, FPAD])
        last = sb("last", [P, KF, 1 + DEC_B, FPAD])
        conv = sb("conv", [P, T])
        hid = sb("hid", [P, T])
        hid_hi, hid_lo = sb("hid_hi", [P, 2, T], F32R), sb("hid_lo", [P, 2, T], F32R)
        hist_in, padded, g_copied, tap_done, kept, acted, multiplied, stored = (
            sem(x) for x in ("hist_in", "padded", "g_copied", "tap_done", "kept", "acted", "multiplied", "stored"))
        hid_hi_made, hid_made, down_done, added = (sem(x) for x in ("hid_hi_made", "hid_made", "down_done", "added"))
        block = ctx.enter_context(nc.Block())
        conv_s = conv[:, SEQ:T].rearrange("p (b s) -> p b s", b=DEC_B)
        base, n_pairs = K.pair, 3 * STEPS
        used = K.unit_used

        def pair(i, which):
            if isinstance(i, int) and i == 0:
                return base + (0 if which == 0 else 1)
            return i * 3 + (base - 1 + which)

        @block.sync
        def _(sp):
            sp.dma_start(hist[:, :, :, :], K.A.state_ffn_t).then_inc(hist_in, 16)
            load_units(sp, K, n_pairs - 1)
            sp.wait_ge(kept, 2 * KF)
            sp.dma_start(K.A.ffn_state_t, last[:, :, :, :]).then_inc(stored, 16)
            sp.wait_ge(stored, 16)

        @block.tensor
        def _(pe):
            def up(f, j, outs):
                for s in range(2):
                    pe.wait_ge(g_copied if s == 0 else multiplied, f * 4 if s == 0 else f)
                    pe.wait_ge(added, outs)
                    pe.wait_ge(K.split_done[s], j + 1)
                    accumulate(nc, K, thirds(K.ps, s), s, lambda k, at, n: hi[:, k, at:at + n],
                               lambda k, at, n: lo[:, k, at:at + n]).then_inc(used[s], 1)

            def down(f, j, outs):
                pe.wait_ge(hid_made, f)
                for t in range(KD):
                    if t < 2:
                        pe.wait_ge(g_copied if t == 0 else multiplied, f * 4 + 4 if t == 0 else f + 1)
                    else:
                        pe.wait_ge(added, outs + t - 1)
                    if t % DOWN_F == 0:
                        pe.wait_ge(K.split_done[t // DOWN_F], j + 1)
                    mm = accumulate(nc, K, thirds(K.ps, t % 2), t // DOWN_F, lambda k, at, n: hid_hi[:, k, at:at + n],
                                    lambda k, at, n: hid_lo[:, k, at:at + n],
                                    tiles=[2 * (t % DOWN_F), 2 * (t % DOWN_F) + 1])
                    mm.then_inc(down_done, 1)
                    if t % DOWN_F == DOWN_F - 1:
                        nc.tensor.drain().then_inc(used[t // DOWN_F], 1)

            up(0, pair(0, 0), 0)
            up(1, pair(0, 2), 0)
            with pe.Fori(1, STEPS) as i:
                up(2 * i, pair(i, 0), i * KD - KD)
                down(2 * i, pair(i, 1), i * KD - KD)
                up(2 * i + 1, pair(i, 2), i * KD)
            pe.wait_ge(hid_made, KF)
            for t in range(KD):
                if t < 2:
                    pe.wait_ge(g_copied if t == 0 else multiplied, 4 * KF if t == 0 else KF)
                else:
                    pe.wait_ge(added, (STEPS - 1) * KD + t - 1)
                if t % DOWN_F == 0:
                    pe.wait_ge(K.split_done[t // DOWN_F], base + n_pairs)
                accumulate(nc, K, thirds(K.ps, t % 2), t // DOWN_F, lambda k, at, n: hid_hi[:, k, at:at + n],
                           lambda k, at, n: hid_lo[:, k, at:at + n],
                           tiles=[2 * (t % DOWN_F), 2 * (t % DOWN_F) + 1]).then_inc(down_done, 1)
            pe.wait_ge(down_done, STEPS * KD)
            for s in range(2):
                pe.sem_inc(used[s], 1)

        @block.scalar
        def _(act):
            def up(f, j):
                act.wait_ge(used[0], j + 1)
                act.wait_ge(tap_done, f * 6)
                act.wait_ge(kept, f * 2)
                nc.scalar.activation(piece(g_prompt, FPAD, 2 * THIRD, 2), K.ps[:, 0:2, 0:THIRD], ACT.Identity
                                     ).then_inc(g_copied, 1)
                nc.scalar.activation(g_prompt[:, FPAD + 2 * THIRD:], K.ps[:, 2, 0:SEQ % THIRD], ACT.Identity
                                     ).then_inc(g_copied, 1)
                nc.scalar.activation(g_sample[:, :, FPAD:], K.ps[:, 2, SEQ % THIRD:T % THIRD].rearrange("p (b s) -> p b s", b=DEC_B),
                                     ACT.Identity).then_inc(g_copied, 1)
                nc.scalar.activation(g_sample[:, :, 0:FPAD], hist[:, bass.ds(f, 1), :, :].rearrange(
                    "p a b w -> p (a b) w"), ACT.Identity).then_inc(g_copied, 1)
                act.wait_ge(tap_done, f * 6 + 6)
                nc.scalar.activation(conv[:, :], conv[:, :], ACT.Silu).then_inc(acted, 1)

            def high_half(f, slot, downs):
                act.wait_ge(multiplied, f + 1)
                act.wait_ge(down_done, downs)
                nc.scalar.activation(hid_hi[:, slot, :], hid[:, :], ACT.Identity).then_inc(hid_hi_made, 1)

            act.wait_ge(hist_in, 16)
            up(0, pair(0, 0))
            high_half(0, 0, 0)
            up(1, pair(0, 2))
            high_half(1, 1, 0)
            with act.Fori(1, STEPS) as i:
                up(2 * i, pair(i, 0))
                high_half(2 * i, 0, i * KD)
                up(2 * i + 1, pair(i, 2))
                high_half(2 * i + 1, 1, i * KD)

        @block.gpsimd
        def _(pool):
            split_units(nc, pool, K, n_pairs - 1)

        @block.vector
        def _(dve):
            def up(f, j):
                dve.wait_ge(g_copied, f * 4 + 4)
                nc.vector.tensor_copy(last[:, bass.ds(f, 1), 0, :].rearrange("p a w -> p (a w)"),
                                      g_prompt[:, SEQ:]).then_inc(kept, 1)
                nc.vector.tensor_copy(last[:, bass.ds(f, 1), 1:, :].rearrange("p a b w -> p (a b) w"),
                                      g_sample[:, :, DEC_S:]).then_inc(kept, 1)
                for w in range(FFN_W):
                    scale = K.vecs[:, bass.ds(f * FFN_W + (VEC_AT["w_fdw"] + w), 1)]
                    in_p, in_s = g_prompt[:, w:w + SEQ], g_sample[:, :, w:w + DEC_S]
                    if w == 0:
                        dve.wait_ge(multiplied, f)
                        bias = K.vecs[:, bass.ds(f + VEC_AT["b_fdw"], 1)]
                        nc.vector.tensor_scalar(conv[:, 0:SEQ], in_p, scale, bias, ALU.mult, ALU.add
                                                ).then_inc(tap_done, 1)
                        nc.vector.tensor_scalar(conv_s, in_s, scale, bias, ALU.mult, ALU.add).then_inc(tap_done, 1)
                        continue
                    dve.wait_ge(tap_done, f * 6 + (2 * w - 1))
                    nc.vector.scalar_tensor_tensor(conv[:, 0:SEQ], in_p, scale, conv[:, 0:SEQ], ALU.mult, ALU.add
                                                   ).then_inc(tap_done, 1)
                    dve.wait_ge(tap_done, f * 6 + 2 * w)
                    nc.vector.scalar_tensor_tensor(conv_s, in_s, scale, conv_s, ALU.mult, ALU.add
                                                   ).then_inc(tap_done, 1)
                dve.wait_ge(acted, f + 1)
                dve.wait_ge(used[1], j + 1)
                dve.wait_ge(hid_made, f)
                for acc, at, n, a in pieces(K.ps, 1):
                    ins = nc.vector.tensor_tensor(piece(hid, at, n, a), acc, piece(conv, at, n, a), ALU.mult)
                ins.then_inc(multiplied, 1)

            def low_half(f, slot):
                dve.wait_ge(hid_hi_made, f + 1)
                nc.vector.tensor_tensor(hid_lo[:, slot, :], hid[:, :], hid_hi[:, slot, :].bitcast(F32), ALU.subtract
                                        ).then_inc(hid_made, 1)

            def add_down(outs):
                for t in range(KD):
                    dve.wait_ge(down_done, outs + t + 1)
                    for acc, at, n, a in pieces(K.ps, t % 2):
                        y_at = piece(y[:, t, :], at, n, a)
                        ins = nc.vector.tensor_tensor(y_at, acc, y_at, ALU.add)
                    ins.then_inc(added, 1)

            nc.vector.memset(g_prompt[:, 0:FPAD], 0.0).then_inc(padded, 1)
            nc.vector.memset(y[:, :, :], 0.0).then_inc(padded, 1)
            dve.wait_ge(padded, 2)
            up(0, pair(0, 0))
            low_half(0, 0)
            up(1, pair(0, 2))
            low_half(1, 1)
            with dve.Fori(1, STEPS) as i:
                dve.wait_ge(added, i * KD - KD)
                up(2 * i, pair(i, 0))
                add_down(i * KD - KD)
                low_half(2 * i, 0)
                up(2 * i + 1, pair(i, 2))
                low_half(2 * i + 1, 1)
            dve.wait_ge(added, (STEPS - 1) * KD)
            add_down((STEPS - 1) * KD)
    K.pair += n_pairs
    K.fed += n_pairs - 1


def build(nc, A):
    K = Names()
    K.A = A
    with ExitStack() as top:
        def sb(stack, name, shape, dt=F32, side="left"):
            return stack.enter_context(nc.sbuf_tensor(name, shape, dt, side=side))

        K.ps = top.enter_context(nc.psum_tensor("ps", [P, 8, 512], F32))
        K.s_load = top.enter_context(nc.semaphore("s_load"))
        K.unit_in, K.hi_done, K.split_done, K.unit_used = (
            [top.enter_context(nc.semaphore(f"{x}{s}")) for s in range(2)]
            for x in ("unit_in", "hi_done", "split_done", "unit_used"))
        K.may_split, K.may_fetch = (top.enter_context(nc.semaphore(x)) for x in ("may_split", "may_fetch"))
        K.pair = K.fed = 0
        K.x = sb(top, "x", [P, KD, T])
        K.raw = sb(top, "raw", [P, 2, KD * P])
        K.w_hi, K.w_lo = (sb(top, n, [P, 2, KD * P], F32R) for n in ("w_hi", "w_lo"))
        K.vecs = sb(top, "vecs", [P, N_VEC])
        K.ident, K.ones, K.causal = (sb(top, n, [P, P]) for n in ("ident", "ones", "causal"))
        K.pages, K.part, K.page_rows = (sb(top, n, [P, DEC_B], I32) for n in ("pages", "part", "page_rows"))
        K.eps = sb(top, "eps", [P, 1])

        def halves_of_x(stack, name):
            return [sb(stack, f"{name}_{h}", [P, KD, T], F32R, "right") for h in ("hi", "lo")]

        with ExitStack() as mixed:
            with ExitStack() as mixer:
                K.qlat = sb(mixer, "qlat", [P, KC * DEC_B, HEADS * DEC_S], F32, "right")[:, :, :].rearrange(
                    "p (l b) (h s) -> p l b h s", l=KC, h=HEADS)
                K.qpe = sb(mixer, "qpe", [P, DEC_B, HEADS * DEC_S], F32, "right")[:, :, :].rearrange(
                    "p b (h s) -> p b h s", h=HEADS)
                K.wuv = sb(mixer, "wuv", [P, KC, HEADS * VH], F32, "right")
                K.kh = sb(mixer, "kh", [P, T], F32, "right")
                K.c = sb(mixer, "c", [P, KC, T], F32, "right")
                with ExitStack() as prompt:
                    with ExitStack() as conv:
                        with ExitStack() as latents:
                            K.lat = sb(latents, "lat", [P, KQ + KC + 1, T], F32, "right")
                            K.rope = sb(conv, "rope", [P, T])
                            load_stage(nc, K, A)
                            with ExitStack() as proj:
                                h = halves_of_x(proj, "h")
                                norm_stage(nc, K, "pre_mix", K.x, KD, T, "g_pre_mix", None, D_MODEL, split=h,
                                           prefetch=True)
                                linear_stage(nc, K, "latents", K.lat, KQ + KC + 1, h, last=False)
                                K.u_prompt = sb(conv, "u_prompt", [P, 2 * KU, CPAD + 512])
                                K.u_sample = sb(conv, "u_sample", [P, KU * DEC_B, CPAD + DEC_S])
                                glu_stage(nc, K, h)
                            rope_k_stage(nc, K)
                            K.qn = sb(conv, "qn", [P, KQ, T])
                            norm_stage(nc, K, "q_norm", K.lat[:, 0:KQ, :], KQ, T, "g_q_a", K.qn, Q_LORA)

                            def store_latents(sp, stored):
                                sp.dma_start(A.kv_latent_t, K.c[:, :, :]).then_inc(stored, 16)
                                return 1

                            norm_stage(nc, K, "kv_norm", K.lat[:, KQ:KQ + KC, :], KC, T, "g_kv_a", K.c, KV_LORA,
                                       store=store_latents)
                        K.cv_prompt = sb(prompt, "cv_prompt", [P, 2 * KU, 512], F32, "right")
                        K.cv_sample = sb(prompt, "cv_sample", [P, KU * DEC_B, DEC_S], F32, "right")
                        K.attn = sb(prompt, "attn", [P, QT, HEADS * VH], F32, "right")
                        K.v = sb(conv, "v", [P, QT, HEADS * VH])
                        value_stage(nc, K)
                        prompt_attention_stage(nc, K)
                    K.mix = sb(mixed, "mix", [P, KD, T])
                    turn_attention_stage(nc, K)
                    gather_conv_stage(nc, K)
                    norm_stage(nc, K, "conv_norm", K.mix[:, KU:, :], KU, T, "g_cln", K.mix[:, KU:, :], D_CONV,
                               center=True, bias="b_cln", func=ACT.Silu, prefetch=True)
                K.olat = sb(mixer, "olat", [P, KC, HEADS, SAMPLE], F32, "right")
                paged_attention_stage(nc, K)
                sample_value_stage(nc, K)
            m = sb(mixed, "m", [P, KD, T])
            with ExitStack() as proj:
                linear_stage(nc, K, "out", m, KD, halves_of_x(proj, "mix"), src=K.mix)
            norm_stage(nc, K, "post_mix", m, KD, T, "g_post_mix", K.x, D_MODEL, add_to=K.x, prefetch=True)
        with ExitStack() as cross:
            with ExitStack() as keys:
                mem_k = sb(keys, "mem_k", [P, KD, N_MEM], F32, "right")
                mem_v = sb(keys, "mem_v", [P, 2, D_MODEL], F32, "right")
                xq_sample = sb(keys, "xq_sample", [P, KD, SAMPLE], F32, "right")
                with ExitStack() as memory:
                    mem = sb(memory, "mem", [P, KD, N_MEM])
                    mem_halves = [sb(memory, f"mem_{x}", [P, KD, N_MEM], F32R) for x in ("hi", "lo")]
                    mem_in = memory.enter_context(nc.semaphore("mem_in"))
                    with nc.Block() as block:
                        @block.sync
                        def _(sp):
                            sp.dma_start(mem[:, :, :], A.mem_t).then_inc(mem_in, 16)
                            sp.wait_ge(mem_in, 16)
                    norm_stage(nc, K, "mem_norm", mem, KD, N_MEM, "g_mem", None, D_MODEL, split=mem_halves)
                    memory_stage(nc, K, mem_halves, mem_k, mem_v)
                with ExitStack() as proj:
                    h = halves_of_x(proj, "hx")
                    norm_stage(nc, K, "pre_x", K.x, KD, T, "g_pre_x", None, D_MODEL, split=h, prefetch=True)
                    xo = sb(cross, "xo", [P, KD, T])
                    prompt_cross_stage(nc, K, h, mem_k, mem_v, xo, xq_sample)
                sample_cross_stage(nc, K, xo, xq_sample)
            xz = sb(cross, "xz", [P, KD, T])
            with ExitStack() as proj:
                linear_stage(nc, K, "xo", xz, KD, halves_of_x(proj, "xo"), src=xo)
            norm_stage(nc, K, "post_x", xz, KD, T, "g_post_x", K.x, D_MODEL, add_to=K.x)
        with ExitStack() as ffn:
            h = halves_of_x(ffn, "hf")
            norm_stage(nc, K, "pre_ffn", K.x, KD, T, "g_pre_ffn", None, D_MODEL, split=h, prefetch=True)
            y = sb(ffn, "y", [P, KD, T])
            ffn_stage(nc, K, h, y)

            def store_y(sp, stored):
                sp.dma_start(A.y_t, K.x[:, :, :]).then_inc(stored, 16)
                return 1

            norm_stage(nc, K, "post_ffn", y, KD, T, "g_post_ffn", K.x, D_MODEL, add_to=K.x, store=store_y)


OUTS = {
    "y_t": [P, KD, T], "kv_latent_t": [P, KC, T], "k_rope_t": [ROPE, T],
    "conv_prompt_t": [KU, P, CPAD], "conv_sample_t": [KU, P, DEC_B, CPAD],
    "ffn_state_t": [P, KF, 1 + DEC_B, FPAD], "mem_k_t": [P, KD, N_MEM], "mem_v_t": [P, 2, D_MODEL],
}


def kernel(**inputs):
    import numpy as np
    import concourse.bacc as bacc
    from concourse.bass_utils import run_bass_kernel_spmd

    a = {k: np.asarray(v) for k, v in inputs.items()}
    w = {k: v[0] for k, v in a.items() if k[0:2] in ("w_", "g_", "b_")}

    def by_feature(rows):
        return rows.reshape(rows.shape[0], -1, P).transpose(2, 1, 0)

    def tiles(m):
        k, f = m.shape
        return m.reshape(k // P, P, f // P, P).transpose(2, 1, 0, 3).reshape(f // P, P, k)

    def columns(v):
        return v.reshape(-1, P, int(v.size // v.shape[0])).transpose(1, 0, 2).reshape(P, -1)

    d = {}
    d["x_t"] = by_feature(np.concatenate([a["x_prompt"][0], a["x_sample"].reshape(SAMPLE, D_MODEL)]))
    d["mem_t"] = by_feature(a["mem_prompt"][0])
    twice = np.repeat(np.arange(KU), 2)
    per_feature = dict(w, w_fdw=w["w_fdw"].T,
                       w_dw=w["w_dw"].T.reshape(KU, P, CONV_W)[twice].reshape(-1, CONV_W),
                       b_dw=w["b_dw"].reshape(KU, P)[twice].reshape(-1))
    d["vecs"] = np.concatenate([columns(per_feature[n]) for n, _ in VEC_SIZES], axis=1)

    pos = np.concatenate([np.arange(SEQ), PAST + np.tile(np.arange(DEC_S), DEC_B)]).astype(np.float32)
    half = ROPE // 2
    inv = (np.float32(10000.0) ** (-np.arange(half, dtype=np.float32) / np.float32(half))).astype(np.float32)
    ang = (pos[None, :] * inv[:, None]).astype(np.float32)
    cos, sin = np.cos(ang), np.sin(ang)
    d["rope"] = np.concatenate([cos, cos, -sin, sin]).astype(np.float32)
    d["ident"] = np.eye(P, dtype=np.float32)
    d["causal"] = np.triu(np.full((P, P), -1e30, np.float32), 1)
    same = np.eye(DEC_B, dtype=bool)[None, :, :, None] & np.tril(np.ones((DEC_S, DEC_S), bool))[:, None, None, :]
    mask = np.where(same, 0.0, -1e30).astype(np.float32)
    d["new_mask"] = np.tile(mask.reshape(DEC_S, -1), (HEADS, 1))
    d["part"] = np.tile((np.arange(P, dtype=np.int32) % PARTS)[:, None], (1, DEC_B))

    def swapped(cols):
        return np.concatenate([cols[..., half:], cols[..., :half]], axis=-1)

    cuts = np.cumsum([Q_LORA, KV_LORA, ROPE, D_CONV])
    wq, wc, wpe, wa, wb = np.split(w["w_in"], cuts, axis=1)
    glu = np.concatenate([x for k in range(KU) for x in (wb[:, k * P:(k + 1) * P], wa[:, k * P:(k + 1) * P])], axis=1)
    units = [tiles(np.concatenate([wq, wc, wpe, wpe, wpe, swapped(wpe), glu], axis=1)), tiles(w["w_out"]),
             np.stack([tiles(w["w_xk"]), tiles(w["w_xv"])], axis=1).reshape(2 * KD, P, D_MODEL),
             tiles(w["w_xq"]), tiles(w["w_xo"])]
    heads = w["w_q_b"].reshape(KQ, P, HEADS, NOPE + ROPE)
    heads = np.concatenate([heads, swapped(heads[..., NOPE:])], axis=-1).transpose(2, 1, 0, 3).reshape(HEADS, P, -1)
    uk = w["w_uk"].reshape(KC, P, HEADS, NOPE).transpose(2, 1, 0, 3).reshape(HEADS, P, -1)
    uk_t = w["w_uk"].transpose(1, 2, 0)
    d["w_head_t"] = np.concatenate([heads, uk, np.concatenate([uk_t, uk_t], axis=1)], axis=2)
    d["w_uv_t"] = w["w_uv"].reshape(KC, P, HEADS * VH).transpose(1, 0, 2)
    value, gate = np.split(w["w_up"], 2, axis=1)
    up = np.stack([tiles(gate), tiles(value)], axis=1)
    down = w["w_down"].reshape(KF // 2, 2, P, KD // DOWN_F, DOWN_F, P).transpose(0, 3, 2, 4, 1, 5)
    down = down.reshape(KF // 2, KD // DOWN_F, P, D_MODEL)
    units += [up[0], up[1]]
    for i in range(1, KF // 2):
        units += [up[2 * i], down[i - 1], up[2 * i + 1]]
    d["units"] = np.concatenate(units + [down[-1]])

    d["cache"] = np.concatenate([a["cache_kv_latent"][0].reshape(-1, PER_ROW * KV_LORA),
                                 a["cache_k_rope"][0].reshape(-1, PER_ROW * ROPE)], axis=1)
    d["pages"] = np.repeat(a["page_table"].T, PARTS, axis=0)
    d["cache_k_t"] = a["cache_mem_k"][0].reshape(DEC_B, N_MEM, KD, P).transpose(0, 3, 2, 1)
    d["cache_v_t"] = a["cache_mem_v"][0].reshape(DEC_B, 2, P, D_MODEL).transpose(0, 2, 1, 3)
    d["state_conv_t"] = a["state_conv"][0].reshape(DEC_B, CPAD, KU, P).transpose(2, 3, 0, 1)
    d["state_ffn_t"] = a["state_ffn_conv"][0].reshape(DEC_B, FPAD, KF, P).transpose(3, 2, 0, 1)

    nc = bacc.Bacc("TRN2", target_bir_lowering=False, num_devices=1)
    A, arrays = Names(), {}
    for name, arr in d.items():
        arr = np.ascontiguousarray(arr)
        arrays[f"in_{name}"] = arr
        A.__dict__[name] = nc.dram_tensor(f"in_{name}", arr.shape, mybir.dt.from_np(arr.dtype),
                                          kind="ExternalInput").ap()
    for name, shape in OUTS.items():
        A.__dict__[name] = nc.dram_tensor(f"out_{name}", shape, F32, kind="ExternalOutput").ap()
    build(nc, A)
    got = run_bass_kernel_spmd(nc, [arrays], core_ids=[0]).results[0]
    r = {name: np.asarray(got[f"out_{name}"]) for name in OUTS}

    def rows(t):
        return t.transpose(2, 1, 0).reshape(t.shape[2], -1)

    y, c, pe = rows(r["y_t"]), rows(r["kv_latent_t"]), r["k_rope_t"].T
    ffn = r["ffn_state_t"].transpose(2, 3, 1, 0).reshape(1 + DEC_B, FPAD, D_FF)
    return (
        y[None, :SEQ], y[SEQ:].reshape(DEC_B, DEC_S, D_MODEL),
        c[None, None, :SEQ], pe[None, None, :SEQ],
        r["conv_prompt_t"].transpose(2, 0, 1).reshape(1, 1, CPAD, D_CONV), ffn[None, 0:1],
        rows(r["mem_k_t"]).reshape(1, 1, N_MEM, XH, XD),
        r["mem_v_t"].transpose(1, 0, 2).reshape(1, 1, N_MEM, XH, XD),
        c[SEQ:].reshape(1, DEC_B, DEC_S, KV_LORA), pe[SEQ:].reshape(1, DEC_B, DEC_S, ROPE),
        r["conv_sample_t"].transpose(2, 3, 0, 1).reshape(1, DEC_B, CPAD, D_CONV), ffn[None, 1:],
    )
```

```python
from contextlib import ExitStack

import concourse.bass as bass
from concourse import mybir

P = 128
F32 = mybir.dt.float32
F32R = mybir.dt.float32r
I32 = mybir.dt.int32
ALU = mybir.AluOpType
ACT = mybir.ActivationFunctionType
AX_X = mybir.AxisListType.X

D_MODEL, SEQ, DEC_B, DEC_S = 1024, 1024, 8, 8
PAST, PAGE = 2048, 128
HEADS, NOPE, ROPE, VH = 8, 64, 32, 64
Q_LORA, KV_LORA, D_CONV, CONV_W = 384, 256, 512, 31
XH, XD, N_MEM = 4, 256, 256
D_FF, FFN_W = 2816, 3
EPS = 1e-6
SAMPLE = DEC_B * DEC_S
T = SEQ + SAMPLE
KD = D_MODEL // P
KQ, KC, KU, KF = Q_LORA // P, KV_LORA // P, D_CONV // P, D_FF // P
PAGES = PAST // PAGE
PARTS = P // PAGES
PER_ROW = PAGE // PARTS
QT = SEQ // P
SCALE = float(NOPE + ROPE) ** -0.5
X_SCALE = float(XD) ** -0.5
CHUNKS = [(0, 512), (512, 512), (1024, SAMPLE)]
THIRD = 384
THIRDS = [(0, THIRD), (THIRD, THIRD), (2 * THIRD, T - 2 * THIRD)]
CPAD, FPAD = CONV_W - 1, FFN_W - 1
DOWN_F = 4

VEC_SIZES = [("g_pre_mix", KD), ("g_post_mix", KD), ("g_pre_x", KD), ("g_post_x", KD),
             ("g_pre_ffn", KD), ("g_post_ffn", KD), ("g_mem", KD), ("g_q_a", KQ), ("g_kv_a", KC),
             ("b_dw", 2 * KU), ("g_cln", KU), ("b_cln", KU), ("b_fdw", KF),
             ("w_dw", 2 * KU * CONV_W), ("w_fdw", KF * FFN_W)]
VEC_AT, _n = {}, 0
for _name, _size in VEC_SIZES:
    VEC_AT[_name] = _n
    _n += _size
N_VEC = _n


def region(ps, s):
    return ps[:, 3 * s:3 * s + 3, :].rearrange("p a b -> p (a b)")[:, 0:T]


def thirds(ps, s):
    return lambda at, n: ps[:, 3 * s + at // THIRD, 0:n]


def pieces(ps, s):
    return [(ps[:, 3 * s:3 * s + 2, 0:THIRD], 0, 2 * THIRD, 2),
            (ps[:, 3 * s + 2:3 * s + 3, 0:T - 2 * THIRD], 2 * THIRD, T - 2 * THIRD, 1)]


def piece(ap, at, n, a):
    return ap[:, at:at + n].rearrange("p (a c) -> p a c", a=a)


def vec(K, name, j):
    a = VEC_AT[name] + j
    return K.vecs[:, a:a + 1]


class Names:
    pass


def semaphores(nc, ctx, stage):
    made = []
    ctx.callback(lambda: [nc.gpsimd.sem_clear(s) for s in made])

    def sem(what):
        made.append(ctx.enter_context(nc.semaphore(f"{stage}_{what}")))
        return made[-1]

    return sem


def load_stage(nc, K, A):
    with nc.Block() as block:
        @block.sync
        def _(sp):
            sp.dma_start(K.x[:, :, :], A.x_t).then_inc(K.s_load, 16)
            sp.dma_start(K.vecs[:, :], A.vecs).then_inc(K.s_load, 16)
            sp.dma_start(K.ident[:, :], A.ident).then_inc(K.s_load, 16)
            sp.dma_start(K.rope[64:128, :], A.rope).then_inc(K.s_load, 16)
            sp.dma_start(K.causal[:, :], A.causal).then_inc(K.s_load, 16)
            sp.dma_start(K.pages[:, :], A.pages).then_inc(K.s_load, 16)
            sp.dma_start(K.part[:, :], A.part).then_inc(K.s_load, 16)
            sp.wait_ge(K.s_load, 112)

        @block.vector
        def _(dve):
            nc.vector.memset(K.ones[:, :], 1.0)
            nc.vector.memset(K.eps[:, :], EPS)
            dve.wait_ge(K.s_load, 112)
            nc.vector.scalar_tensor_tensor(K.page_rows[:, :], K.pages[:, :], float(PARTS), K.part[:, :], ALU.mult,
                                           ALU.add)


def norm_stage(nc, K, name, src, n_k, width, gain, dst, dim, add_to=None, center=False, bias=None, func=None,
               store=None, split=None, prefetch=False):
    chunks = CHUNKS if width == T else [(0, width)]
    with ExitStack() as ctx:
        sq = ctx.enter_context(nc.sbuf_tensor(f"{name}_sq", [P, 2, width], F32))
        acc = ctx.enter_context(nc.sbuf_tensor(f"{name}_acc", [P, width], F32))
        rstd = ctx.enter_context(nc.sbuf_tensor(f"{name}_rstd", [P, width], F32))
        if split is not None:
            whole = ctx.enter_context(nc.sbuf_tensor(f"{name}_whole", [P, 2, width], F32))

        sem = semaphores(nc, ctx, name)

        summed, mean_ready, centered = sem("summed"), sem("mean_ready"), sem("centered")
        squared, sq_added, total_ready, rooted = sem("squared"), sem("sq_added"), sem("total_ready"), sem("rooted")
        rstd_ready, scaled, done, stored = sem("rstd_ready"), sem("scaled"), sem("done"), sem("stored")
        hi_ready = sem("hi_ready")
        block = ctx.enter_context(nc.Block())
        total = region(K.ps, 0)[:, 0:width]
        mean_total = region(K.ps, 1)[:, 0:width]

        @block.scalar
        def _(act):
            if center:
                act.wait_ge(centered, n_k)
            for k in range(n_k):
                if k >= 2:
                    act.wait_ge(sq_added, k - 1)
                nc.scalar.activation(sq[:, k % 2, :], src[:, k, :], ACT.Square).then_inc(squared, 1)
            act.wait_ge(total_ready, 1)
            nc.scalar.activation(rstd[:, :], total, ACT.Sqrt, bias=K.eps[:, :], scale=1.0 / dim).then_inc(rooted, 1)
            if split is not None:
                for k in range(n_k):
                    act.wait_ge(scaled, k + 1)
                    nc.scalar.activation(split[0][:, k, :], whole[:, k % 2, :], ACT.Identity).then_inc(hi_ready, 1)
            if func is not None:
                for k in range(n_k):
                    act.wait_ge(scaled, k + 1)
                    nc.scalar.activation(dst[:, k, :], dst[:, k, :], func, bias=vec(K, bias, k)).then_inc(done, 1)

        @block.tensor
        def _(pe):
            if center:
                pe.wait_ge(summed, n_k)
                for at, n in chunks:
                    mm = nc.tensor.matmul(mean_total[:, at:at + n], K.ones[:, :], acc[:, at:at + n],
                                          start=True, stop=True)
                mm.then_inc(mean_ready, 1)
            pe.wait_ge(sq_added, n_k)
            for at, n in chunks:
                mm = nc.tensor.matmul(total[:, at:at + n], K.ones[:, :], acc[:, at:at + n], start=True, stop=True)
            mm.then_inc(total_ready, 1)

        @block.vector
        def _(dve):
            if center:
                nc.vector.tensor_copy(acc[:, :], src[:, 0, :]).then_inc(summed, 1)
                for k in range(1, n_k):
                    dve.wait_ge(summed, k)
                    nc.vector.tensor_tensor(acc[:, :], acc[:, :], src[:, k, :], ALU.add).then_inc(summed, 1)
                dve.wait_ge(mean_ready, 1)
                for k in range(n_k):
                    nc.vector.scalar_tensor_tensor(src[:, k, :], mean_total, -1.0 / dim, src[:, k, :],
                                                   ALU.mult, ALU.add).then_inc(centered, 1)
            dve.wait_ge(squared, 1)
            nc.vector.tensor_copy(acc[:, :], sq[:, 0, :]).then_inc(sq_added, 1)
            for k in range(1, n_k):
                dve.wait_ge(squared, k + 1)
                dve.wait_ge(sq_added, k)
                nc.vector.tensor_tensor(acc[:, :], acc[:, :], sq[:, k % 2, :], ALU.add).then_inc(sq_added, 1)
            dve.wait_ge(rooted, 1)
            nc.vector.reciprocal(rstd[:, :], rstd[:, :]).then_inc(rstd_ready, 1)
            dve.wait_ge(rstd_ready, 1)

            def low_half(k):
                dve.wait_ge(hi_ready, k + 1)
                nc.vector.tensor_tensor(split[1][:, k, :], whole[:, k % 2, :], split[0][:, k, :].bitcast(F32),
                                        ALU.subtract).then_inc(done, 1)

            for k in range(n_k):
                if split is not None:
                    if k >= 2:
                        dve.wait_ge(done, k - 1)
                    nc.vector.scalar_tensor_tensor(whole[:, k % 2, :], src[:, k, :], vec(K, gain, k), rstd[:, :],
                                                   ALU.mult, ALU.mult).then_inc(scaled, 1)
                    if k >= 1:
                        low_half(k - 1)
                    if k == n_k - 1:
                        low_half(k)
                elif add_to is None:
                    nc.vector.scalar_tensor_tensor(dst[:, k, :], src[:, k, :], vec(K, gain, k), rstd[:, :],
                                                   ALU.mult, ALU.mult).then_inc(done if func is None else scaled, 1)
                else:
                    nc.vector.scalar_tensor_tensor(src[:, k, :], src[:, k, :], vec(K, gain, k), rstd[:, :],
                                                   ALU.mult, ALU.mult).then_inc(scaled, 1)
                    dve.wait_ge(scaled, k + 1)
                    nc.vector.tensor_tensor(dst[:, k, :], add_to[:, k, :], src[:, k, :], ALU.add).then_inc(done, 1)

        @block.sync
        def _(sp):
            if prefetch:
                load_units(sp, K, 1)
            if store is not None:
                sp.wait_ge(done, n_k)
                sp.wait_ge(stored, 16 * store(sp, stored))

        if prefetch:
            @block.gpsimd
            def _(pool):
                split_units(nc, pool, K, 1)

    if prefetch:
        K.fed += 1


def load_units(sp, K, n):
    with sp.Fori(K.fed, K.fed + n) as j:
        for s in range(2):
            sp.wait_ge(K.split_done[s], j)
            sp.sem_inc(K.may_fetch, 1)
            sp.dma_start(K.raw[:, s, :], K.A.units[bass.ds(2 * j + s, 1)].rearrange("a p c -> p (a c)")
                         ).then_inc(K.unit_in[s], 16)


def split_units(nc, pool, K, n):
    with pool.Fori(K.fed, K.fed + n) as j:
        for s in range(2):
            pool.wait_ge(K.unit_in[s], 16 * j + 16)
            pool.wait_ge(K.unit_used[s], j)
            pool.sem_inc(K.may_split, 1)
            nc.gpsimd.tensor_copy(K.w_hi[:, s, :], K.raw[:, s, :]).then_inc(K.hi_done[s], 1)
            pool.wait_ge(K.hi_done[s], j + 1)
            nc.gpsimd.tensor_tensor(K.w_lo[:, s, :], K.raw[:, s, :], K.w_hi[:, s, :].bitcast(F32), ALU.subtract
                                    ).then_inc(K.split_done[s], 1)


def feed(nc, K, block, pairs, last):
    n = pairs - 1 if last else pairs

    @block.sync
    def _(sp):
        load_units(sp, K, n)

    @block.gpsimd
    def _(pool):
        split_units(nc, pool, K, n)

    return n


def accumulate(nc, K, out, slot, hi, lo, first=True, last=True, tiles=range(KD), chunks=THIRDS):
    for k, tile in enumerate(tiles):
        w_hi, w_lo = (w[:, slot, tile * P:(tile + 1) * P] for w in (K.w_hi, K.w_lo))
        for p, (w, x) in enumerate(((w_hi, hi), (w_hi, lo), (w_lo, hi))):
            for at, n in chunks:
                mm = nc.tensor.matmul(out(at, n), w, x(k, at, n), start=first and k == 0 and p == 0,
                                      stop=last and k == len(tiles) - 1 and p == 2)
    return mm


def linear_stage(nc, K, name, dst, n_f, halves, src=None, last=True):
    n = n_f // 2
    hi, lo = halves
    with ExitStack() as ctx:
        sem = semaphores(nc, ctx, name)
        copied = [sem(f"copied{s}") for s in range(2)]
        hi_made, lo_made = sem("hi_made"), sem("lo_made")
        block = ctx.enter_context(nc.Block())
        fed = feed(nc, K, block, n, last)
        used, base = K.unit_used, K.pair

        def x_hi(k, at, n):
            return hi[:, k, at:at + n]

        def x_lo(k, at, n):
            return lo[:, k, at:at + n]

        @block.tensor
        def _(pe):
            def unit(i, s):
                pe.wait_ge(copied[s], i)
                pe.wait_ge(K.split_done[s], i + (base + 1))
                accumulate(nc, K, thirds(K.ps, s), s, x_hi, x_lo).then_inc(used[s], 1)

            if src is not None:
                pe.wait_ge(K.split_done[0], base + 1)
                for k in range(KD):
                    pe.wait_ge(lo_made, k + 1)
                    mm = accumulate(nc, K, thirds(K.ps, 0), 0, lambda _, at, n: x_hi(k, at, n),
                                    lambda _, at, n: x_lo(k, at, n), first=k == 0, last=k == KD - 1, tiles=[k])
                mm.then_inc(used[0], 1)
                unit(0, 1)
                with pe.Fori(1, n) as i:
                    unit(i, 0)
                    unit(i, 1)
            else:
                with pe.Fori(0, n) as i:
                    unit(i, 0)
                    unit(i, 1)

        @block.scalar
        def _(act):
            if src is not None:
                for k in range(KD):
                    nc.scalar.activation(hi[:, k, :], src[:, k, :], ACT.Identity).then_inc(hi_made, 1)
            with act.Fori(0, n) as i:
                act.wait_ge(used[0], i + (base + 1))
                for acc, at, n_at, a in pieces(K.ps, 0):
                    ins = nc.scalar.activation(dst[:, bass.ds(2 * i, 1), at:at + n_at].rearrange(
                        "p b (a c) -> p (b a) c", a=a), acc, ACT.Identity)
                ins.then_inc(copied[0], 1)

        @block.vector
        def _(dve):
            if src is not None:
                for k in range(KD):
                    dve.wait_ge(hi_made, k + 1)
                    nc.vector.tensor_tensor(lo[:, k, :], src[:, k, :], hi[:, k, :].bitcast(F32), ALU.subtract
                                            ).then_inc(lo_made, 1)
            with dve.Fori(0, n) as i:
                dve.wait_ge(used[1], i + (base + 1))
                for acc, at, n_at, a in pieces(K.ps, 1):
                    ins = nc.vector.tensor_copy(dst[:, bass.ds(2 * i + 1, 1), at:at + n_at].rearrange(
                        "p b (a c) -> p (b a) c", a=a), acc)
                ins.then_inc(copied[1], 1)
    K.pair += n
    K.fed += fed


def glu_stage(nc, K, halves):
    hi, lo = halves
    with ExitStack() as ctx:
        sem = semaphores(nc, ctx, "glu")
        gate = ctx.enter_context(nc.sbuf_tensor("glu_gate", [P, T], F32))
        gated, multiplied, hist, padded = (sem(w) for w in ("gated", "multiplied", "hist", "padded"))
        block = ctx.enter_context(nc.Block())
        base = K.pair
        n = KU - 1

        @block.sync
        def _(sp):
            for k in range(KU):
                sp.dma_start(K.u_sample[:, k * DEC_B:(k + 1) * DEC_B, 0:CPAD], K.A.state_conv_t[k]).then_inc(hist, 16)
            load_units(sp, K, n)
            sp.wait_ge(hist, 16 * KU)

        @block.gpsimd
        def _(pool):
            split_units(nc, pool, K, n)

        @block.tensor
        def _(pe):
            with pe.Fori(0, KU) as i:
                for s in range(2):
                    pe.wait_ge(gated if s == 0 else multiplied, i)
                    pe.wait_ge(K.split_done[s], i + (base + 1))
                    accumulate(nc, K, thirds(K.ps, s), s, lambda k, at, n: hi[:, k, at:at + n],
                               lambda k, at, n: lo[:, k, at:at + n]).then_inc(K.unit_used[s], 1)

        @block.scalar
        def _(act):
            with act.Fori(0, KU) as i:
                act.wait_ge(K.unit_used[0], i + (base + 1))
                act.wait_ge(multiplied, i)
                for acc, at, n_at, a in pieces(K.ps, 0):
                    ins = nc.scalar.activation(piece(gate, at, n_at, a), acc, ACT.Sigmoid)
                ins.then_inc(gated, 1)

        @block.vector
        def _(dve):
            nc.vector.memset(K.u_prompt[:, :, 0:CPAD], 0.0).then_inc(padded, 1)
            dve.wait_ge(padded, 1)
            with dve.Fori(0, KU) as i:
                dve.wait_ge(K.unit_used[1], i + (base + 1))
                dve.wait_ge(gated, i + 1)
                for block_at, to, at, n_at in ((0, 0, 0, THIRD), (0, THIRD, THIRD, 512 - THIRD),
                                               (1, -CPAD, 512 - CPAD, CPAD), (1, 0, 512, 2 * THIRD - 512),
                                               (1, 2 * THIRD - 512, 2 * THIRD, SEQ - 2 * THIRD)):
                    a = K.ps[:, 3 + at // THIRD, at % THIRD:at % THIRD + n_at]
                    nc.vector.tensor_tensor(K.u_prompt[:, bass.ds(2 * i + block_at, 1), CPAD + to:CPAD + to + n_at],
                                            a, gate[:, at:at + n_at], ALU.mult)
                nc.vector.tensor_tensor(K.u_sample[:, bass.ds(i * DEC_B, DEC_B), CPAD:],
                                        K.ps[:, 5, SEQ % THIRD:T % THIRD].rearrange("p (b s) -> p b s", b=DEC_B),
                                        gate[:, SEQ:T].rearrange("p (b s) -> p b s", b=DEC_B),
                                        ALU.mult).then_inc(multiplied, 1)
    K.pair += KU
    K.fed += n


def rope_k_stage(nc, K):
    with ExitStack() as ctx:
        sem = semaphores(nc, ctx, "rope")
        part = ctx.enter_context(nc.sbuf_tensor("rope_part", [P, 2, T], F32))
        products, rotated = (sem(w) for w in ("products", "rotated"))
        stored = sem("stored")
        block = ctx.enter_context(nc.Block())

        @block.vector
        def _(dve):
            nc.vector.tensor_tensor(part[64:96, 0, :], K.lat[64:96, 5, :], K.rope[64:96, :], ALU.mult
                                    ).then_inc(products, 1)
            nc.vector.tensor_tensor(part[64:96, 1, :], K.lat[96:128, 5, :], K.rope[96:128, :], ALU.mult
                                    ).then_inc(products, 1)
            dve.wait_ge(products, 2)
            nc.vector.tensor_tensor(K.kh[64:96, :], part[64:96, 0, :], part[64:96, 1, :], ALU.add
                                    ).then_inc(rotated, 1)

        @block.sync
        def _(sp):
            sp.wait_ge(rotated, 1)
            sp.dma_start(K.A.k_rope_t, K.kh[64:96, :]).then_inc(stored, 16)
            for k in range(KU):
                sp.dma_start(K.A.conv_prompt_t[k], K.u_prompt[:, 2 * k + 1, 512:]).then_inc(stored, 16)
                sp.dma_start(K.A.conv_sample_t[k], K.u_sample[:, k * DEC_B:(k + 1) * DEC_B, DEC_S:]
                             ).then_inc(stored, 16)
            sp.wait_ge(stored, 16 + 32 * KU)


def gather_mix_stage(nc, K):
    with ExitStack() as ctx:
        block = ctx.enter_context(nc.Block())

        attn = K.attn[:, :].rearrange("p (a t) -> p a t", a=HEADS // 2)

        @block.gpsimd
        def _(pool):
            nc.gpsimd.tensor_copy(K.mix[:, 0, 0:SEQ], attn[:, 0, :])

        @block.scalar
        def _(act):
            for k in range(KU):
                nc.scalar.activation(K.mix[:, KU + k, 0:SEQ].rearrange("p (a t) -> p a t", a=2),
                                     K.cv_prompt[:, 2 * k:2 * k + 2, :], ACT.Identity)

        @block.vector
        def _(dve):
            for k in range(1, HEADS // 2):
                nc.vector.tensor_copy(K.mix[:, k, 0:SEQ], attn[:, k, :])
            for k in range(KU):
                nc.vector.tensor_copy(K.mix[:, KU + k, SEQ:T].rearrange("p (b s) -> p b s", b=DEC_B),
                                      K.cv_sample[:, k * DEC_B:(k + 1) * DEC_B, :])


def value_stage(nc, K):
    with ExitStack() as ctx:
        sem = semaphores(nc, ctx, "value")
        wuv_full, summed, copied = (sem(w)
                                    for w in ("wuv_full", "summed", "copied"))
        block = ctx.enter_context(nc.Block())

        @block.sync
        def _(sp):
            sp.dma_start(K.wuv[:, :, :], K.A.w_uv_t).then_inc(wuv_full, 16)

        @block.tensor
        def _(pe):
            pe.wait_ge(wuv_full, 16)
            for t in range(QT):
                if t >= 4:
                    pe.wait_ge(copied, t - 3)
                for l in range(KC):
                    mm = nc.tensor.matmul(K.ps[:, t % 4, :], K.c[:, l, t * P:(t + 1) * P], K.wuv[:, l, :],
                                          start=l == 0, stop=l == KC - 1)
                mm.then_inc(summed, 1)

        @block.scalar
        def _(act):
            for t in range(QT):
                act.wait_ge(summed, t + 1)
                nc.scalar.activation(K.v[:, t, :], K.ps[:, t % 4, :], ACT.Identity).then_inc(copied, 1)


def prompt_attention_stage(nc, K):
    with ExitStack() as ctx:
        def sb(what, shape):
            return ctx.enter_context(nc.sbuf_tensor(f"mla_{what}", shape, F32))

        sem = semaphores(nc, ctx, "mla")

        GROUPS = QT // 2
        JOBS_OF = [("q", 0, 0), ("k", 0, 1), ("q", 1, 2), ("k", 1, 3), ("q", 2, 5), ("latents", 0, 7)]
        TAPS_AT = [CONV_W * i // QT for i in range(QT + 1)]
        JOBS, COPIES, Q_JOBS = len(JOBS_OF), len(JOBS_OF) - 1, 3
        job_of_tile = {tile: n for n, (_, _, tile) in enumerate(JOBS_OF)}

        def q_jobs_before(n):
            return sum(what == "q" for what, _, _ in JOBS_OF[:n])

        def first(h, i):
            return isinstance(h, int) and h == 0 and i < 2

        def following(h, s, i, more):
            if i + 2 < QT:
                return h, s, i + 2
            return (h + 1, 1 - s, i + 2 - QT) if more else None

        wh = sb("wh", [P, KQ * P + KC * NOPE + KV_LORA])
        wq = wh[:, 0:KQ * P].rearrange("p (k f) -> p k f", k=KQ)
        wuk = wh[:, KQ * P:KQ * P + KC * NOPE].rearrange("p (k f) -> p k f", k=KC)
        wuk_t = wh[0:NOPE, KQ * P + KC * NOPE:]
        qh = [sb(f"qh{s}", [P, T]) for s in range(2)]
        kh = [K.kh, sb("kh", [P, SEQ])]
        vh = [sb(f"vh{s}", [P, QT, VH]) for s in range(2)]
        part = sb("part", [P, 2, 512])
        prob = sb("prob", [P, 2, SEQ])
        prob_t = K.raw[:, :, :].rearrange("p s (j q) -> p (s j) q", q=2 * P)
        top, neg_top, den, inv = (sb(x, [P, QT]) for x in ("top", "neg_top", "den", "inv"))
        w_full, k_rope_set, job_done, copied, rope_read, q_ready, ql_copied, vh_set, tap_done = (
            sem(x) for x in ("w_full", "k_rope_set", "job_done", "copied", "rope_read", "q_ready", "ql_copied",
                             "vh_set", "tap_done"))
        scored, masked, top_found, top_ready, exped, inv_ready, normed, turned, turned_copied = (
            sem(x) for x in ("scored", "masked", "top_found", "top_ready", "exped", "inv_ready", "normed", "turned",
                             "turned_copied"))
        attended, out, tapped, sample_tapped = (sem(x) for x in ("attended", "out", "tapped", "sample_tapped"))
        block = ctx.enter_context(nc.Block())
        turn = K.ps[:, 4:6, :].rearrange("p a b -> p (a b)")
        o_acc = K.ps[0:VH, 6, 0:2 * P]
        job_acc = K.ps[:, 7, :]
        ql_acc = K.ps[:, 7, 0:KC * SAMPLE].rearrange("p (l t) -> p l t", l=KC)

        def score(i):
            return K.ps[:, 2 * (i % 2):2 * (i % 2) + 2, :].rearrange("p a b -> p (a b)")[:, 0:(i + 1) * P]

        def attn_at(h, s, g):
            return K.attn[s * VH:(s + 1) * VH, bass.ds(h * (SEQ // 2) + (g * 2 * P - s * (SEQ // 2)), 2 * P)]

        def heads(body):
            def loop(engine):
                with engine.Fori(0, HEADS // 2 - 1) as i:
                    for s in range(2):
                        body(2 * i + s, s, True)
                for s in range(2):
                    body(HEADS - 2 + s, s, s == 0)
            return loop

        def tap(h, w):
            return K.vecs[:, bass.ds(h * CONV_W + (VEC_AT["w_dw"] + w), 1)]

        def conv_bias(h):
            return K.vecs[:, bass.ds(h + VEC_AT["b_dw"], 1)]

        @block.sync
        def _(sp):
            with sp.Fori(0, HEADS) as h:
                sp.wait_ge(job_done, h * JOBS)
                sp.dma_start(wh[:, :], K.A.w_head_t[bass.ds(h, 1)].rearrange("a p c -> p (a c)")
                             ).then_inc(w_full, 16)

        @block.tensor
        def _(pe):
            def job(h, s, n):
                what, chunk, _ = JOBS_OF[n]
                at, w = CHUNKS[chunk]
                if n == 0:
                    pe.wait_ge(w_full, h * 16 + 16)
                    pe.wait_ge(ql_copied, h)
                else:
                    pe.wait_ge(copied, h * COPIES + n)
                    pe.wait_ge(rope_read, h * (2 * Q_JOBS) + 2 * q_jobs_before(n))
                if what == "q":
                    for k in range(KQ):
                        mm = nc.tensor.matmul(job_acc[:, 0:w], wq[:, k, :], K.qn[:, k, at:at + w], start=k == 0,
                                              stop=k == KQ - 1)
                elif what == "k":
                    for l in range(KC):
                        mm = nc.tensor.matmul(job_acc[0:NOPE, 0:w], wuk[:, l, :], K.c[:, l, at:at + w],
                                              start=l == 0, stop=l == KC - 1)
                else:
                    for l in range(KC):
                        mm = nc.tensor.matmul(ql_acc[:, l, :], wuk_t[:, l * P:(l + 1) * P], qh[s][0:NOPE, SEQ:T],
                                              start=True, stop=True)
                mm.then_inc(job_done, 1)

            def scores(h, s, i):
                if i % 4 == 0:
                    pe.wait_ge(copied, h * COPIES + (2 + i // 2))
                    pe.wait_ge(q_ready, h * Q_JOBS + (1 + i // 4))
                if not first(h, i):
                    pe.wait_ge(exped, h * QT + (i - 1))
                for at in range(0, (i + 1) * P, 512):
                    n = min(512, (i + 1) * P - at)
                    mm = nc.tensor.matmul(score(i)[:, at:at + n], qh[s][0:96, i * P:(i + 1) * P],
                                          kh[s][0:96, at:at + n], start=True, stop=True)
                mm.then_inc(scored, 1)

            for n in range(JOBS):
                job(0, 0, n)
            pe.wait_ge(k_rope_set, 1)
            scores(0, 0, 0)
            scores(0, 0, 1)

            def body(h, s, more):
                for i in range(QT):
                    g = i // 2
                    pe.wait_ge(normed, h * QT + i + 1)
                    pe.wait_ge(turned_copied, h * QT + i)
                    for j in range(i + 1):
                        mm = nc.tensor.transpose(turn[:, j * P:(j + 1) * P], prob[:, i % 2, j * P:(j + 1) * P],
                                                 K.ident[:, :])
                    mm.then_inc(turned, 1)
                    after = following(h, s, i, more)
                    if after is not None:
                        scores(*after)
                    if more and i in job_of_tile:
                        job(h + 1, 1 - s, job_of_tile[i])
                    if i % 2 == 1:
                        pe.wait_ge(turned_copied, h * QT + i + 1)
                        pe.wait_ge(vh_set, h + 1)
                        pe.wait_ge(out, h * GROUPS + g)
                        for j in range(i):
                            nc.tensor.matmul(o_acc, vh[s][:, j, :], prob_t[:, j, :], start=j == 0, stop=False)
                        nc.tensor.matmul(o_acc[:, P:], vh[s][:, i, :], prob_t[:, i, P:], start=False, stop=True
                                         ).then_inc(attended, 1)

            heads(body)(pe)

        @block.scalar
        def _(act):
            def copy_job(h, s, n):
                act.wait_ge(job_done, h * JOBS + (n + 1))
                what, chunk, _ = JOBS_OF[n]
                at, w = CHUNKS[chunk]
                to = qh[s] if what == "q" else kh[s]
                nc.scalar.activation(to[0:NOPE, at:at + w], job_acc[0:NOPE, 0:w], ACT.Identity).then_inc(copied, 1)

            def set_vh(h, s):
                nc.scalar.activation(vh[s][:, :, :], K.v[:, :, bass.ds(h * VH, VH)], ACT.Identity
                                     ).then_inc(vh_set, 1)

            def exp(h, s, i):
                act.wait_ge(top_ready, h * QT + i + 1)
                if not first(h, i):
                    act.wait_ge(turned, h * QT + (i - 1))
                nc.scalar.activation(prob[:, i % 2, 0:(i + 1) * P], score(i), ACT.Exp, bias=neg_top[:, i:i + 1],
                                     scale=SCALE, accum_out=den[:, i:i + 1]).then_inc(exped, 1)

            def norm(h, i):
                act.wait_ge(inv_ready, h * QT + i + 1)
                nc.scalar.activation(prob[:, i % 2, 0:(i + 1) * P], prob[:, i % 2, 0:(i + 1) * P], ACT.Identity,
                                     scale=inv[:, i:i + 1]).then_inc(normed, 1)

            for n in range(COPIES):
                copy_job(0, 0, n)
            set_vh(0, 0)
            exp(0, 0, 0)
            exp(0, 0, 1)
            norm(0, 0)

            def body(h, s, more):
                for i in range(QT):
                    if i + 1 < QT:
                        norm(h, i + 1)
                    elif more:
                        norm(h + 1, 0)
                    act.wait_ge(turned, h * QT + i + 1)
                    act.wait_ge(attended, h * GROUPS + i // 2)
                    nc.scalar.activation(prob_t[:, 0:i + 1, (i % 2) * P:(i % 2 + 1) * P],
                                         turn[:, 0:(i + 1) * P].rearrange("p (j q) -> p j q", q=P), ACT.Identity
                                         ).then_inc(turned_copied, 1)
                    if i % 2 == 0 and i > 0:
                        act.wait_ge(attended, h * GROUPS + i // 2)
                        nc.scalar.activation(attn_at(h, s, i // 2 - 1), o_acc, ACT.Identity).then_inc(out, 1)
                    after = following(h, s, i, more)
                    if after is not None:
                        exp(*after)
                    if more and job_of_tile.get(i, COPIES) < COPIES:
                        copy_job(h + 1, 1 - s, job_of_tile[i])
                    elif more and i == QT - 2:
                        set_vh(h + 1, 1 - s)

            heads(body)(act)

        @block.vector
        def _(dve):
            def rope_job(h, s, n, tile):
                at, w = CHUNKS[n]
                dve.wait_ge(job_done, h * JOBS + (JOBS_OF.index(("q", n, tile)) + 1))
                dve.wait_ge(q_ready, h * Q_JOBS + n)
                nc.vector.tensor_tensor(part[64:96, 0, 0:w], job_acc[64:96, 0:w], K.rope[64:96, at:at + w], ALU.mult
                                        ).then_inc(rope_read, 1)
                nc.vector.tensor_tensor(part[64:96, 1, 0:w], job_acc[96:128, 0:w], K.rope[96:128, at:at + w],
                                        ALU.mult).then_inc(rope_read, 1)
                dve.wait_ge(rope_read, h * (2 * Q_JOBS) + (2 * n + 2))
                nc.vector.tensor_tensor(qh[s][64:96, at:at + w], part[64:96, 0, 0:w], part[64:96, 1, 0:w], ALU.add
                                        ).then_inc(q_ready, 1)
                if at == SEQ:
                    dve.wait_ge(q_ready, h * Q_JOBS + (n + 1))
                    nc.vector.tensor_copy(K.qpe[64:96, :, bass.ds(h, 1), :].rearrange("p b a s -> p b (a s)"),
                                          qh[s][64:96, SEQ:T].rearrange("p (b s) -> p b s", b=DEC_B))

            def copy_ql(h):
                dve.wait_ge(job_done, h * JOBS + JOBS)
                for l in range(KC):
                    ins = nc.vector.tensor_copy(
                        K.qlat[:, l, :, bass.ds(h, 1), :].rearrange("p b a s -> p b (a s)"),
                        ql_acc[:, l, :].rearrange("p (b s) -> p b s", b=DEC_B))
                ins.then_inc(ql_copied, 1)

            def find_top(h, s, i):
                n = h * QT + i + 1
                diag = score(i)[:, i * P:(i + 1) * P]
                dve.wait_ge(scored, n)
                nc.vector.tensor_tensor(diag, diag, K.causal[:, :], ALU.add).then_inc(masked, 1)
                dve.wait_ge(masked, n)
                nc.vector.tensor_reduce(top[:, i:i + 1], score(i), AX_X, ALU.max).then_inc(top_found, 1)
                dve.wait_ge(top_found, n)
                nc.vector.tensor_scalar(neg_top[:, i:i + 1], top[:, i:i + 1], -SCALE, None, ALU.mult
                                        ).then_inc(top_ready, 1)

            def invert(h, i):
                dve.wait_ge(exped, h * QT + i + 1)
                nc.vector.reciprocal(inv[:, i:i + 1], den[:, i:i + 1]).then_inc(inv_ready, 1)

            def prompt_taps(h, first, last):
                acc = K.cv_prompt[:, bass.ds(h, 1), :]
                for w in range(first, last):
                    taken = K.u_prompt[:, bass.ds(h, 1), w:w + 512]
                    if w == 0:
                        nc.vector.tensor_scalar(acc, taken, tap(h, w), conv_bias(h), ALU.mult, ALU.add
                                                ).then_inc(tapped, 1)
                        continue
                    dve.wait_ge(tapped, h * CONV_W + w)
                    nc.vector.scalar_tensor_tensor(acc, taken, tap(h, w), acc, ALU.mult, ALU.add
                                                   ).then_inc(tapped, 1)

            def sample_taps(h, s, first, last):
                acc = K.cv_sample[:, bass.ds(h * 4 - s * 4, DEC_B), :]
                for w in range(first, min(last, CONV_W)):
                    taken = K.u_sample[:, bass.ds(h * 4 - s * 4, DEC_B), w:w + DEC_S]
                    if w == 0:
                        nc.vector.tensor_scalar(acc, taken, tap(h, w), conv_bias(h), ALU.mult, ALU.add
                                                ).then_inc(sample_tapped, 2)
                        continue
                    dve.wait_ge(sample_tapped, h * CONV_W + (2 * w - s * CONV_W))
                    nc.vector.scalar_tensor_tensor(acc, taken, tap(h, w), acc, ALU.mult, ALU.add
                                                   ).then_inc(sample_tapped, 2)

            nc.vector.tensor_copy(kh[1][64:96, :], K.kh[64:96, 0:SEQ]).then_inc(k_rope_set, 1)
            for what, n, tile in JOBS_OF:
                if what == "q":
                    rope_job(0, 0, n, tile)
            copy_ql(0)
            find_top(0, 0, 0)
            find_top(0, 0, 1)
            invert(0, 0)

            def body(h, s, more):
                for i in range(QT):
                    if i + 1 < QT:
                        invert(h, i + 1)
                    elif more:
                        invert(h + 1, 0)
                    quarters = [TAPS_AT[i] + (TAPS_AT[i + 1] - TAPS_AT[i]) * j // 4 for j in range(5)]
                    prompt_taps(h, quarters[0], quarters[1])
                    sample_taps(h, s, 16 * s + 2 * i, 16 * s + 2 * i + 1)
                    prompt_taps(h, quarters[1], quarters[2])
                    after = following(h, s, i, more)
                    if after is not None:
                        find_top(*after)
                    prompt_taps(h, quarters[2], quarters[3])
                    sample_taps(h, s, 16 * s + 2 * i + 1, 16 * s + 2 * i + 2)
                    prompt_taps(h, quarters[3], quarters[4])
                    if more and i in job_of_tile:
                        what, n, tile = JOBS_OF[job_of_tile[i]]
                        if what == "q":
                            rope_job(h + 1, 1 - s, n, tile)
                        elif what == "latents":
                            copy_ql(h + 1)
                dve.wait_ge(attended, h * GROUPS + GROUPS)
                nc.vector.tensor_copy(attn_at(h, s, GROUPS - 1), o_acc).then_inc(out, 1)

            heads(body)(dve)


def paged_attention_stage(nc, K):
    with ExitStack() as ctx:
        def sb(what, shape, dt=F32):
            return ctx.enter_context(nc.sbuf_tensor(f"paged_{what}", shape, dt))

        sem = semaphores(nc, ctx, "paged")

        R = HEADS * DEC_S
        BANK = 512 // P
        GROUPS = PER_ROW * KC // BANK
        ROPE_AT = PER_ROW * KV_LORA
        ACT_GROUPS, DVE_GROUPS = [0, 1, 2, GROUPS - 1, GROUPS], list(range(3, GROUPS - 1))
        past = [sb(f"past{s}", [P, PER_ROW * (KV_LORA + ROPE)]) for s in range(2)]
        all_q_rope = sb("all_q_rope", [P, DEC_B, BANK * R])
        q_rope = sb("q_rope", [P, BANK * R])
        q_lat = sb("q_lat", [P, KC, R])
        rope_t = sb("rope_t", [P, BANK * P])
        lat_t = sb("lat_t", [P, KC, PAST])
        new_rope_t = sb("new_rope_t", [P, SAMPLE])
        new_rows = sb("new_rows", [SAMPLE, KV_LORA])
        mask = sb("mask", [R, DEC_B * SAMPLE])
        prob = sb("prob", [R, PAST + SAMPLE])
        prob_t = sb("prob_t", [P, PER_ROW * R])
        prob_new = sb("prob_new", [SAMPLE, R])
        o = sb("o", [R, KV_LORA])
        tops, sums = sb("tops", [R, 3]), sb("sums", [R, 4])
        gathered = [sem(f"gathered{s}") for s in range(2)]
        prepared, rows_turned, rows_copied, mask_in = (
            sem(x) for x in ("prepared", "rows_turned", "rows_copied", "mask_in"))
        turned, act_copied, dve_copied, staged, scored = (
            sem(x) for x in ("turned", "act_copied", "dve_copied", "staged", "scored"))
        new_masked, tops_found, top_ready, exped, summed, inv_ready = (
            sem(x) for x in ("new_masked", "tops_found", "top_ready", "exped", "summed", "inv_ready"))
        probs_turned, act_probs, dve_probs, attended, normed, o_turned, o_copied, may_go = (
            sem(x) for x in ("probs_turned", "act_probs", "dve_probs", "attended", "normed", "o_turned", "o_copied",
                             "may_go"))
        block = ctx.enter_context(nc.Block())
        scores = K.ps[0:R, 0:BANK, :].rearrange("p a b -> p (a b)")
        prob_banks = [K.ps[:, 6, :], K.ps[:, 5, :]]
        last = K.ps[:, 7, :]
        o_acc, s_new = last[0:R, 0:KV_LORA], last[0:R, 256:256 + SAMPLE]
        new_turn, o_turn = K.ps[0:SAMPLE, 0, 0:R], K.ps[:, 6, 0:KC * R]
        half = PER_ROW // 2 * R

        def bank(q):
            return K.ps[:, 4 + q % 2, :]

        def token(position):
            own, j = divmod(position, BANK)
            return j * BANK + own

        def sequences(step):
            def loop(engine):
                with engine.Fori(0, DEC_B // 2 - 1) as i:
                    for s in range(2):
                        step(2 * i + s, s, True)
                for s in range(2):
                    step(DEC_B - 2 + s, s, s == 0)
            return loop

        @block.gpsimd
        def _(pool):
            for b in range(DEC_B):
                if b >= 2:
                    pool.wait_ge(attended, b - 1)
                pool.indirect_dma_start(
                    out=past[b % 2][:, :], out_offset=None, in_=K.A.cache,
                    in_offset=bass.IndirectOffsetOnAxis(ap=K.page_rows[:, b:b + 1], axis=0)
                ).then_inc(gathered[b % 2], 16)

        @block.sync
        def _(sp):
            sp.dma_start(mask[:, :], K.A.new_mask).then_inc(mask_in, 16)

        @block.tensor
        def _(pe):
            def copied(b, q):
                if q in ACT_GROUPS:
                    pe.wait_ge(act_copied, b * len(ACT_GROUPS) + (ACT_GROUPS.index(q) + 1))
                else:
                    pe.wait_ge(dve_copied, b * len(DVE_GROUPS) + (DVE_GROUPS.index(q) + 1))

            def turn(b, s):
                for q in range(GROUPS + 1):
                    if q == 0:
                        pe.wait_ge(act_copied, b * len(ACT_GROUPS))
                        tiles = [ROPE_AT + j * P for j in range(BANK)]
                    else:
                        if q >= 2:
                            copied(b, q - 2)
                        tiles = [(token(t) * KC + l) * P for l in range(KC) for t in (2 * q - 2, 2 * q - 1)]
                    for j, at in enumerate(tiles):
                        mm = nc.tensor.transpose(bank(q)[:, j * P:(j + 1) * P], past[s][:, at:at + P], K.ident[:, :])
                    mm.then_inc(turned, 1)

            def score(b, between=None):
                copied(b, GROUPS)
                copied(b, GROUPS - 2)
                pe.wait_ge(staged, 2 * b + 2)
                for c in range(BANK):
                    at = slice(c * 512, (c + 1) * 512)
                    nc.tensor.matmul(scores[:, at], q_rope[:, c * R:(c + 1) * R], rope_t[:, :], start=True, stop=False)
                    for l in range(KC):
                        nc.tensor.matmul(scores[:, at], q_lat[:, l, :], lat_t[:, l, at], start=False, stop=l == KC - 1)
                    if c == 1 and between is not None:
                        between()
                nc.tensor.matmul(s_new, q_rope[:, 2 * R:3 * R], new_rope_t[:, :], start=True, stop=False)
                for l in range(KC):
                    mm = nc.tensor.matmul(s_new, q_lat[:, l, :], K.c[:, l, SEQ:T], start=False, stop=l == KC - 1)
                mm.then_inc(scored, 1)

            def attend(b, s, more):
                pe.wait_ge(exped, 2 * b + 2)
                if more:
                    copied(b + 1, GROUPS - 1)
                pe.wait_ge(o_copied, KC * b)
                pe.sem_inc(may_go, 1)
                for h in range(2):
                    for j in range(PER_ROW // 2):
                        t = h * (PER_ROW // 2) + j
                        mm = nc.tensor.transpose(prob_banks[h][:, j * R:(j + 1) * R], prob[:, t * P:(t + 1) * P],
                                                 K.ident[0:R, 0:R])
                    if h == 0:
                        mm.then_inc(probs_turned, 1)
                nc.tensor.transpose(new_turn, prob[:, PAST:], K.ident[0:R, 0:R]).then_inc(probs_turned, 1)
                pe.wait_ge(act_probs, b + 1)
                for t in range(PER_ROW):
                    if t == PER_ROW // 2:
                        pe.wait_ge(dve_probs, b + 1)
                    at = token(t) * KV_LORA
                    nc.tensor.matmul(o_acc, prob_t[:, t * R:(t + 1) * R], past[s][:, at:at + KV_LORA], start=t == 0,
                                     stop=False)
                nc.tensor.matmul(o_acc, prob_new[:, :], new_rows[:, :], start=False, stop=True).then_inc(attended, 1)

            def turn_out(b):
                pe.wait_ge(normed, b + 1)
                pe.sem_inc(may_go, 1)
                for l in range(KC):
                    mm = nc.tensor.transpose(o_turn[:, l * R:(l + 1) * R], o[:, l * P:(l + 1) * P],
                                             K.ident[0:R, 0:R])
                mm.then_inc(o_turned, 1)

            pe.wait_ge(prepared, 5)
            for l in range(KC):
                mm = nc.tensor.transpose(last[0:SAMPLE, l * P:(l + 1) * P], K.c[:, l, SEQ:T], K.ident[:, :])
            mm.then_inc(rows_turned, 1)
            pe.wait_ge(gathered[0], 16)
            turn(0, 0)
            pe.wait_ge(rows_copied, 1)
            score(0)

            def step(b, s, more):
                if more:
                    pe.wait_ge(gathered[1 - s], 8 * (b + s) + 16)
                    pe.wait_ge(dve_probs, b)
                    turn(b + 1, 1 - s)
                attend(b, s, more)
                if more:
                    score(b + 1, lambda: turn_out(b))
                else:
                    turn_out(b)

            sequences(step)(pe)

        @block.scalar
        def _(act):
            def copies(b, groups):
                for q in groups:
                    act.wait_ge(turned, b * (GROUPS + 1) + (q + 1))
                    if q == 0:
                        nc.scalar.activation(rope_t[:, :], bank(q), ACT.Identity).then_inc(act_copied, 1)
                    else:
                        nc.scalar.activation(lat_t[:, :, (2 * q - 2) * P:2 * q * P],
                                             bank(q).rearrange("p (l c) -> p l c", l=KC), ACT.Identity
                                             ).then_inc(act_copied, 1)

            def stage(b):
                act.wait_ge(scored, b)
                nc.scalar.activation(q_lat[:, :, :], K.qlat[:, :, bass.ds(b, 1), :, :].rearrange(
                    "p l a h s -> p l (a h s)"), ACT.Identity).then_inc(staged, 1)
                nc.scalar.activation(q_rope[:, :], all_q_rope[:, bass.ds(b, 1), :].rearrange("p a r -> p (a r)"),
                                     ACT.Identity).then_inc(staged, 1)

            act.wait_ge(prepared, 5)
            stage(0)
            copies(0, ACT_GROUPS)

            def step(b, s, more):
                if more:
                    stage(b + 1)
                    copies(b + 1, ACT_GROUPS[0:3])
                act.wait_ge(top_ready, b + 1)
                act.wait_ge(probs_turned, 2 * b)
                nc.scalar.activation(prob[:, 0:PAST], scores, ACT.Exp, bias=tops[:, 2:3], scale=SCALE,
                                     accum_out=sums[:, 0:1]).then_inc(exped, 1)
                nc.scalar.activation(prob[:, PAST:], s_new, ACT.Exp, bias=tops[:, 2:3], scale=SCALE,
                                     accum_out=sums[:, 1:2]).then_inc(exped, 1)
                if more:
                    copies(b + 1, ACT_GROUPS[3:])
                act.wait_ge(probs_turned, 2 * b + 1)
                act.wait_ge(attended, b)
                nc.scalar.activation(prob_t[:, 0:half], prob_banks[0], ACT.Identity).then_inc(act_probs, 1)

            sequences(step)(act)

        @block.vector
        def _(dve):
            def copies(b):
                dve.wait_ge(scored, b)
                for q in DVE_GROUPS:
                    dve.wait_ge(turned, b * (GROUPS + 1) + (q + 1))
                    nc.vector.tensor_copy(lat_t[:, :, (2 * q - 2) * P:2 * q * P],
                                          bank(q).rearrange("p (l c) -> p l c", l=KC)).then_inc(dve_copied, 1)

            nc.vector.memset(all_q_rope[:, :, :], 0.0).then_inc(prepared, 1)
            nc.vector.memset(new_rope_t[:, :], 0.0).then_inc(prepared, 1)
            dve.wait_ge(prepared, 2)
            for own in range(BANK):
                ins = nc.vector.tensor_copy(all_q_rope[own * ROPE:(own + 1) * ROPE, :, own * R:(own + 1) * R],
                                            K.qpe[64:96, :, :, :].rearrange("p b h s -> p b (h s)"))
            ins.then_inc(prepared, 2)
            nc.vector.tensor_copy(new_rope_t[64:96, :], K.kh[64:96, SEQ:T]).then_inc(prepared, 1)
            dve.wait_ge(rows_turned, 1)
            nc.vector.tensor_copy(new_rows[:, :], last[0:SAMPLE, 0:KV_LORA]).then_inc(rows_copied, 1)
            copies(0)
            dve.wait_ge(mask_in, 16)

            def step(b, s, more):
                dve.wait_ge(scored, b + 1)
                nc.vector.tensor_tensor(s_new, s_new, mask[:, bass.ds(b * SAMPLE, SAMPLE)], ALU.add
                                        ).then_inc(new_masked, 1)
                nc.vector.tensor_reduce(tops[:, 0:1], scores, AX_X, ALU.max).then_inc(tops_found, 1)
                dve.wait_ge(new_masked, b + 1)
                nc.vector.tensor_reduce(tops[:, 1:2], s_new, AX_X, ALU.max).then_inc(tops_found, 1)
                dve.wait_ge(tops_found, 2 * b + 2)
                nc.vector.tensor_scalar(tops[:, 2:3], tops[:, 0:1], tops[:, 1:2], -SCALE, ALU.max, ALU.mult
                                        ).then_inc(top_ready, 1)
                if more:
                    copies(b + 1)
                dve.wait_ge(exped, 2 * b + 2)
                nc.vector.tensor_tensor(sums[:, 2:3], sums[:, 0:1], sums[:, 1:2], ALU.add).then_inc(summed, 1)
                dve.wait_ge(summed, b + 1)
                nc.vector.reciprocal(sums[:, 3:4], sums[:, 2:3]).then_inc(inv_ready, 1)
                dve.wait_ge(probs_turned, 2 * b + 2)
                dve.wait_ge(attended, b)
                nc.vector.tensor_copy(prob_new[:, :], new_turn)
                nc.vector.tensor_copy(prob_t[:, half:], prob_banks[1]).then_inc(dve_probs, 1)
                dve.wait_ge(inv_ready, b + 1)
                dve.wait_ge(attended, b + 1)
                nc.vector.tensor_scalar(o[:, :], o_acc, sums[:, 3:4], None, ALU.mult).then_inc(normed, 1)
                dve.wait_ge(o_turned, b + 1)
                for l in range(KC):
                    nc.vector.tensor_copy(K.olat[:, l, :, bass.ds(b * DEC_S, DEC_S)],
                                          o_turn[:, l * R:(l + 1) * R].rearrange("p (h s) -> p h s", h=HEADS)
                                          ).then_inc(o_copied, 1)

            sequences(step)(dve)


def sample_value_stage(nc, K):
    with ExitStack() as ctx:
        sem = semaphores(nc, ctx, "sv")
        summed, copied = (sem(w) for w in ("summed", "copied"))
        block = ctx.enter_context(nc.Block())

        @block.tensor
        def _(pe):
            for j in range(HEADS // 2):
                for par in range(2):
                    for l in range(KC):
                        mm = nc.tensor.matmul(K.ps[:, j, par * SAMPLE:(par + 1) * SAMPLE],
                                              K.wuv[:, l, j * P:(j + 1) * P], K.olat[:, l, 2 * j + par, :],
                                              start=l == 0, stop=l == KC - 1)
                mm.then_inc(summed, 1)

        @block.vector
        def _(dve):
            for j in range(HEADS // 2):
                dve.wait_ge(summed, j + 1)
                for par in range(2):
                    rows = slice(par * VH, (par + 1) * VH)
                    nc.vector.tensor_copy(K.mix[rows, j, SEQ:T], K.ps[rows, j, par * SAMPLE:(par + 1) * SAMPLE])


def memory_stage(nc, K, halves, mem_k, mem_v):
    with ExitStack() as ctx:
        sem = semaphores(nc, ctx, "mem")
        hi, lo = halves
        base, used = K.pair, K.unit_used
        copied = [sem(f"copied{s}") for s in range(2)]
        stored = sem("stored")
        block = ctx.enter_context(nc.Block())

        @block.sync
        def _(sp):
            load_units(sp, K, KD - 1)
            sp.wait_ge(copied[0], KD)
            sp.dma_start(K.A.mem_k_t, mem_k[:, :, :]).then_inc(stored, 16)
            sp.wait_ge(copied[1], KD)
            sp.dma_start(K.A.mem_v_t, mem_v[:, :, :]).then_inc(stored, 16)
            sp.wait_ge(stored, 32)

        @block.tensor
        def _(pe):
            with pe.Fori(0, KD) as f:
                pe.wait_ge(K.split_done[0], f + (base + 1))
                pe.wait_ge(copied[0], f)
                accumulate(nc, K, lambda at, n: K.ps[:, 0, at:at + n], 0, lambda k, at, n: hi[:, k, at:at + n],
                           lambda k, at, n: lo[:, k, at:at + n], chunks=[(0, N_MEM)]).then_inc(used[0], 1)
                pe.wait_ge(K.split_done[1], f + (base + 1))
                pe.wait_ge(copied[1], f)
                for n in range(N_MEM // P):
                    for k in range(KD):
                        w_hi, w_lo = (w[:, 1, k * P:(k + 1) * P] for w in (K.w_hi, K.w_lo))
                        x_hi, x_lo = (x[:, k, n * P:(n + 1) * P] for x in halves)
                        for p, (x, w) in enumerate(((x_hi, w_hi), (x_hi, w_lo), (x_lo, w_hi))):
                            mm = nc.tensor.matmul(K.ps[:, 1 + n, 0:P], x, w, start=k == 0 and p == 0,
                                                  stop=k == KD - 1 and p == 2)
                mm.then_inc(used[1], 1)

        @block.scalar
        def _(act):
            def high_half(j, s):
                act.wait_ge(K.unit_in[s], 16 * j + 16)
                act.wait_ge(used[s], j)
                nc.scalar.activation(K.w_hi[:, s, :], K.raw[:, s, :], ACT.Identity).then_inc(K.hi_done[s], 1)

            def copy(f):
                act.wait_ge(used[0], f + (base + 1))
                nc.scalar.activation(mem_k[:, bass.ds(f, 1), :], K.ps[:, 0, 0:N_MEM], ACT.Identity
                                     ).then_inc(copied[0], 1)

            with act.Fori(0, KD - 1) as f:
                high_half(f + (base + 1), 0)
                copy(f)
                high_half(f + (base + 1), 1)
            copy(KD - 1)

        @block.vector
        def _(dve):
            def low_half(j, s):
                dve.wait_ge(K.hi_done[s], j + 1)
                nc.vector.tensor_tensor(K.w_lo[:, s, :], K.raw[:, s, :], K.w_hi[:, s, :].bitcast(F32), ALU.subtract
                                        ).then_inc(K.split_done[s], 1)

            def copy(f):
                dve.wait_ge(used[1], f + (base + 1))
                nc.vector.tensor_copy(mem_v[:, :, bass.ds(f * P, P)], K.ps[:, 1:3, 0:P]).then_inc(copied[1], 1)

            with dve.Fori(0, KD - 1) as f:
                low_half(f + (base + 1), 0)
                copy(f)
                low_half(f + (base + 1), 1)
            copy(KD - 1)
    K.pair += KD
    K.fed += KD - 1


def prompt_cross_stage(nc, K, halves, mem_k, mem_v, xo, xq_sample):
    with ExitStack() as ctx:
        def sb(what, shape):
            return ctx.enter_context(nc.sbuf_tensor(f"xp_{what}", shape, F32))

        sem = semaphores(nc, ctx, "xp")

        GROUPS = QT // 2
        q, q_next = sb("q", [P, 2, T]), sb("q_next", [P, T])
        vh = sb("vh", [P, 2, XD])
        prob = sb("prob", [P, 2, N_MEM])
        prob_t = sb("prob_t", [P, 2, 2, 2 * P])
        top, neg_top, den, inv = (sb(x, [P, QT]) for x in ("top", "neg_top", "den", "inv"))
        hi, lo = halves
        base, used = K.pair, K.unit_used
        q_kept, q_set, vh_set, scored, top_found, top_ready, exped, inv_ready, normed, turned, turned_copied = (
            sem(x) for x in ("q_kept", "q_set", "vh_set", "scored", "top_found", "top_ready", "exped", "inv_ready",
                             "normed", "turned", "turned_copied"))
        q_odd_set, sample_kept, summed, out = (sem(x) for x in ("q_odd_set", "sample_kept", "summed", "out"))
        block = ctx.enter_context(nc.Block())
        turn = K.ps[:, 5, :].rearrange("p (n c) -> p n c", n=2)
        fed = feed(nc, K, block, XH, True)

        def score(i):
            return K.ps[:, 3 + i % 2, 0:N_MEM]

        def heads(body):
            def loop(engine):
                with engine.Fori(0, XH - 1) as h:
                    body(h, True)
                body(XH - 1, False)
            return loop

        @block.tensor
        def _(pe):
            def project(h, s, first, last):
                if first == 0:
                    pe.wait_ge(q_odd_set if s == 0 else q_kept, h + s)
                    pe.wait_ge(K.split_done[s], h + (base + 1))
                mm = accumulate(nc, K, thirds(K.ps, 0), s, lambda k, at, n: hi[:, first + k, at:at + n],
                                lambda k, at, n: lo[:, first + k, at:at + n], first=first == 0, last=last == KD,
                                tiles=list(range(first, last)))
                if last == KD:
                    mm.then_inc(used[s], 1)

            def scores(h, i):
                pe.wait_ge(exped, h * QT + max(i - 1, 0))
                for k in range(2):
                    mm = nc.tensor.matmul(score(i), q[:, k, i * P:(i + 1) * P],
                                          mem_k[:, bass.ds(2 * h + k, 1), :].rearrange("p a n -> p (a n)"),
                                          start=k == 0, stop=k == 1)
                mm.then_inc(scored, 1)

            for s in range(2):
                project(0, s, 0, KD)

            def body(h, more):
                pe.wait_ge(q_set, h + 1)
                pe.wait_ge(q_odd_set, h + 1)
                scores(h, 0)
                scores(h, 1)
                for i in range(QT):
                    g = i // 2
                    pe.wait_ge(normed, h * QT + i + 1)
                    pe.wait_ge(turned_copied, h * GROUPS + g)
                    for n in range(2):
                        mm = nc.tensor.transpose(turn[:, n, (i % 2) * P:(i % 2 + 1) * P],
                                                 prob[:, i % 2, n * P:(n + 1) * P], K.ident[:, :])
                    mm.then_inc(turned, 1)
                    if i + 2 < QT:
                        scores(h, i + 2)
                    if more:
                        s, k = divmod(2 * i, KD)
                        project(h + 1, s, k, k + 2)
                    if i % 2 == 1:
                        pe.wait_ge(turned_copied, h * GROUPS + g + 1)
                        pe.wait_ge(vh_set, h + 1)
                        pe.wait_ge(out, h * GROUPS + g)
                        for f in range(2):
                            for n in range(2):
                                mm = nc.tensor.matmul(K.ps[:, 6 + f, 0:2 * P], vh[:, n, f * P:(f + 1) * P],
                                                      prob_t[:, g % 2, n, :], start=n == 0, stop=n == 1)
                        mm.then_inc(summed, 1)

            heads(body)(pe)

        @block.scalar
        def _(act):
            def keep_q(h):
                act.wait_ge(used[0], h + (base + 1))
                act.wait_ge(q_set, h)
                for acc, at, n, a in pieces(K.ps, 0):
                    ins = nc.scalar.activation(piece(q_next, at, n, a), acc, ACT.Identity)
                ins.then_inc(q_kept, 1)

            def set_q(h):
                act.wait_ge(q_kept, h + 1)
                act.wait_ge(scored, h * QT)
                act.wait_ge(sample_kept, h)
                nc.scalar.activation(q[:, 0, :], q_next[:, :], ACT.Identity).then_inc(q_set, 1)
                act.wait_ge(summed, h * GROUPS)
                nc.scalar.activation(vh[:, :, :], mem_v[:, :, bass.ds(h * XD, XD)], ACT.Identity
                                     ).then_inc(vh_set, 1)

            def exp(h, i):
                act.wait_ge(top_ready, h * QT + i + 1)
                act.wait_ge(turned, h * QT + max(i - 1, 0))
                nc.scalar.activation(prob[:, i % 2, :], score(i), ACT.Exp, bias=neg_top[:, i:i + 1],
                                     scale=X_SCALE, accum_out=den[:, i:i + 1]).then_inc(exped, 1)

            def copy_turned(h, g):
                act.wait_ge(turned, h * QT + 2 * g + 2)
                act.wait_ge(summed, h * GROUPS + max(g - 1, 0))
                nc.scalar.activation(prob_t[:, g % 2, :, :], turn, ACT.Identity).then_inc(turned_copied, 1)

            keep_q(0)
            set_q(0)

            def body(h, more):
                for i in range(2):
                    exp(h, i)
                for g in range(GROUPS - 1):
                    exp(h, 2 * g + 2)
                    copy_turned(h, g)
                    exp(h, 2 * g + 3)
                    if g == 1 and more:
                        keep_q(h + 1)
                copy_turned(h, GROUPS - 1)
                if more:
                    set_q(h + 1)

            heads(body)(act)

        @block.vector
        def _(dve):
            def set_q_odd(h):
                dve.wait_ge(used[1], h + (base + 1))
                dve.wait_ge(scored, h * QT)
                dve.wait_ge(sample_kept, h)
                for acc, at, n, a in pieces(K.ps, 0):
                    ins = nc.vector.tensor_copy(piece(q[:, 1, :], at, n, a), acc)
                ins.then_inc(q_odd_set, 1)

            def find_top(h, i):
                n = h * QT + i + 1
                dve.wait_ge(scored, n)
                nc.vector.tensor_reduce(top[:, i:i + 1], score(i), AX_X, ALU.max).then_inc(top_found, 1)
                dve.wait_ge(top_found, n)
                nc.vector.tensor_scalar(neg_top[:, i:i + 1], top[:, i:i + 1], -X_SCALE, None, ALU.mult
                                        ).then_inc(top_ready, 1)

            def copy_out(h, g):
                dve.wait_ge(summed, h * GROUPS + g + 1)
                nc.vector.tensor_copy(xo[:, bass.ds(2 * h, 2), g * 2 * P:(g + 1) * 2 * P], K.ps[:, 6:8, 0:2 * P]
                                      ).then_inc(out, 1)

            set_q_odd(0)

            def body(h, more):
                find_top(h, 0)
                find_top(h, 1)
                dve.wait_ge(q_odd_set, h + 1)
                dve.wait_ge(q_set, h + 1)
                nc.vector.tensor_copy(xq_sample[:, bass.ds(2 * h, 2), :], q[:, :, SEQ:T]).then_inc(sample_kept, 1)
                for i in range(QT):
                    dve.wait_ge(exped, h * QT + i + 1)
                    nc.vector.reciprocal(inv[:, i:i + 1], den[:, i:i + 1]).then_inc(inv_ready, 1)
                    dve.wait_ge(inv_ready, h * QT + i + 1)
                    nc.vector.tensor_scalar(prob[:, i % 2, :], prob[:, i % 2, :], inv[:, i:i + 1], None, ALU.mult
                                            ).then_inc(normed, 1)
                    if i % 2 == 0 and i > 0:
                        copy_out(h, i // 2 - 1)
                    if i + 2 < QT:
                        find_top(h, i + 2)
                if more:
                    set_q_odd(h + 1)
                copy_out(h, GROUPS - 1)

            heads(body)(dve)
    K.pair += XH
    K.fed += fed


def sample_cross_stage(nc, K, xo, xq_sample):
    with ExitStack() as ctx:
        def sb(what, shape):
            return ctx.enter_context(nc.sbuf_tensor(f"xs_{what}", shape, F32))

        sem = semaphores(nc, ctx, "xs")

        R = XH * DEC_S
        may_turn, may_load = sem("may_turn"), sem("may_load")
        keys = sb("keys", [P, 2, KD, N_MEM])
        vals = sb("vals", [P, 2, 2, D_MODEL])
        qd = sb("qd", [P, 2, KD, R])
        prob = sb("prob", [R, 2, N_MEM])
        prob_t = sb("prob_t", [P, 2, 2, R])
        stats = sb("stats", [R, 2, 4])
        keys_in, vals_in = ([sem(f"{x}{s}") for s in range(2)] for x in ("keys_in", "vals_in"))
        cleared, staged, scored, top_found, top_ready, exped, inv_ready, normed, turned, turned_copied, summed, out = (
            sem(x) for x in ("cleared", "staged", "scored", "top_found", "top_ready", "exped", "inv_ready", "normed",
                             "turned", "turned_copied", "summed", "out"))
        block = ctx.enter_context(nc.Block())

        def sequences(step):
            def loop(engine):
                with engine.Fori(0, DEC_B // 2 - 1) as i:
                    for s in range(2):
                        step(2 * i + s, s, i, True)
                for s in range(2):
                    step(DEC_B - 2 + s, s, DEC_B // 2 - 1, s == 0)
            return loop

        @block.gpsimd
        def _(pool):
            split_units(nc, pool, K, 1)

        @block.sync
        def _(sp):
            load_units(sp, K, 1)
            def load_keys(b, s, scores):
                if scores is not None:
                    sp.wait_ge(scored, scores)
                    sp.sem_inc(may_load, 1)
                sp.dma_start(keys[:, s, :, :], K.A.cache_k_t[bass.ds(b, 1)].rearrange("a p k n -> p (a k) n")
                             ).then_inc(keys_in[s], 16)

            def load_vals(b, s, sums):
                if sums is not None:
                    sp.wait_ge(summed, sums)
                    sp.sem_inc(may_load, 1)
                sp.dma_start(vals[:, s, :, :], K.A.cache_v_t[bass.ds(b, 1)].rearrange("a p k n -> p (a k) n")
                             ).then_inc(vals_in[s], 16)

            def steady(i, more):
                load_keys(2 * i + 1, 1, 2 * i)
                load_vals(2 * i, 0, 2 * i - 1)
                if more:
                    load_keys(2 * i + 2, 0, 2 * i + 1)
                load_vals(2 * i + 1, 1, 2 * i)

            for s in range(2):
                load_keys(s, s, None)
                load_vals(s, s, None)
            load_keys(2, 0, 1)
            with sp.Fori(1, DEC_B // 2 - 1) as i:
                steady(i, True)
            steady(DEC_B // 2 - 1, False)

        @block.tensor
        def _(pe):
            def score(b, s, loads):
                pe.wait_ge(keys_in[s], loads * 16)
                pe.wait_ge(staged, b * XH + XH)
                pe.wait_ge(exped, b - 1 if not isinstance(b, int) or b else 0)
                for k in range(KD):
                    mm = nc.tensor.matmul(K.ps[0:R, 4 * s, 0:N_MEM], qd[:, s, k, :], keys[:, s, k, :],
                                          start=k == 0, stop=k == KD - 1)
                mm.then_inc(scored, 1)

            score(0, 0, 1)

            def step(b, s, i, more):
                if more:
                    score(b + 1, 1 - s, i + 1 + s)
                pe.wait_ge(normed, b + 1)
                pe.sem_inc(may_turn, 1)
                for n in range(2):
                    mm = nc.tensor.transpose(K.ps[:, 4 * s + 1, n * R:(n + 1) * R], prob[:, s, n * P:(n + 1) * P],
                                             K.ident[0:R, 0:R])
                mm.then_inc(turned, 1)
                pe.wait_ge(vals_in[s], i * 16 + 16)
                pe.wait_ge(turned_copied, b + 1)
                for f in range(KD):
                    for n in range(2):
                        mm = nc.tensor.matmul(K.ps[:, 4 * s + 2, f * DEC_S:(f + 1) * DEC_S],
                                              vals[:, s, n, f * P:(f + 1) * P],
                                              prob_t[:, s, n, (f // 2) * DEC_S:(f // 2 + 1) * DEC_S],
                                              start=n == 0, stop=n == 1)
                mm.then_inc(summed, 1)

            sequences(step)(pe)

        @block.scalar
        def _(act):
            act.wait_ge(cleared, 1)
            def stage(b, s):
                act.wait_ge(scored, b - 1 if not isinstance(b, int) or b else 0)
                for h in range(XH):
                    nc.scalar.activation(qd[:, s, 2 * h:2 * h + 2, h * DEC_S:(h + 1) * DEC_S],
                                         xq_sample[:, 2 * h:2 * h + 2, bass.ds(b * DEC_S, DEC_S)], ACT.Identity
                                         ).then_inc(staged, 1)

            stage(0, 0)

            def step(b, s, i, more):
                if more:
                    stage(b + 1, 1 - s)
                act.wait_ge(top_ready, b + 1)
                act.wait_ge(turned, b)
                nc.scalar.activation(prob[:, s, :], K.ps[0:R, 4 * s, 0:N_MEM], ACT.Exp, bias=stats[:, s, 1:2],
                                     scale=X_SCALE, accum_out=stats[:, s, 2:3]).then_inc(exped, 1)

            sequences(step)(act)

        @block.vector
        def _(dve):
            nc.vector.memset(qd[:, :, :, :], 0.0).then_inc(cleared, 1)
            with dve.Fori(0, DEC_B // 2) as i:
                for s in range(2):
                    b = 2 * i + s
                    dve.wait_ge(scored, b + 1)
                    nc.vector.tensor_reduce(stats[:, s, 0:1], K.ps[0:R, 4 * s, 0:N_MEM], AX_X, ALU.max
                                            ).then_inc(top_found, 1)
                    dve.wait_ge(top_found, b + 1)
                    nc.vector.tensor_scalar(stats[:, s, 1:2], stats[:, s, 0:1], -X_SCALE, None, ALU.mult
                                            ).then_inc(top_ready, 1)
                    dve.wait_ge(exped, b + 1)
                    nc.vector.reciprocal(stats[:, s, 3:4], stats[:, s, 2:3]).then_inc(inv_ready, 1)
                    dve.wait_ge(inv_ready, b + 1)
                    nc.vector.tensor_scalar(prob[:, s, :], prob[:, s, :], stats[:, s, 3:4], None, ALU.mult
                                            ).then_inc(normed, 1)
                    dve.wait_ge(turned, b + 1)
                    nc.vector.tensor_copy(prob_t[:, s, :, :].rearrange("p n r -> p (n r)"),
                                          K.ps[:, 4 * s + 1, 0:2 * R]).then_inc(turned_copied, 1)
                    dve.wait_ge(summed, b + 1)
                    nc.vector.tensor_copy(xo[:, :, bass.ds(SEQ + b * DEC_S, DEC_S)],
                                          K.ps[:, 4 * s + 2, 0:KD * DEC_S].rearrange("p (f s) -> p f s", f=KD)
                                          ).then_inc(out, 1)
    K.fed += 1


def ffn_stage(nc, K, halves, y):
    hi, lo = halves
    STEPS = KF // 2
    with ExitStack() as ctx:
        def sb(what, shape, dt=F32):
            return ctx.enter_context(nc.sbuf_tensor(f"ffn_{what}", shape, dt))

        sem = semaphores(nc, ctx, "ffn")
        g_prompt = sb("g_prompt", [P, FPAD + SEQ])
        g_sample = sb("g_sample", [P, DEC_B, FPAD + DEC_S])
        hist = sb("hist", [P, KF, DEC_B, FPAD])
        last = sb("last", [P, KF, 1 + DEC_B, FPAD])
        conv = sb("conv", [P, T])
        hid = sb("hid", [P, T])
        hid_hi, hid_lo = sb("hid_hi", [P, 2, T], F32R), sb("hid_lo", [P, 2, T], F32R)
        hist_in, padded, g_copied, tap_done, kept, acted, multiplied, stored = (
            sem(x) for x in ("hist_in", "padded", "g_copied", "tap_done", "kept", "acted", "multiplied", "stored"))
        hid_hi_made, hid_made, down_done, added = (sem(x) for x in ("hid_hi_made", "hid_made", "down_done", "added"))
        block = ctx.enter_context(nc.Block())
        conv_s = conv[:, SEQ:T].rearrange("p (b s) -> p b s", b=DEC_B)
        base, n_pairs = K.pair, 3 * STEPS
        used = K.unit_used

        def pair(i, which):
            if isinstance(i, int) and i == 0:
                return base + (0 if which == 0 else 1)
            return i * 3 + (base - 1 + which)

        @block.sync
        def _(sp):
            sp.dma_start(hist[:, :, :, :], K.A.state_ffn_t).then_inc(hist_in, 16)
            load_units(sp, K, n_pairs - 1)
            sp.wait_ge(kept, 2 * KF)
            sp.dma_start(K.A.ffn_state_t, last[:, :, :, :]).then_inc(stored, 16)
            sp.wait_ge(stored, 16)

        @block.tensor
        def _(pe):
            def up(f, j, outs):
                for s in range(2):
                    pe.wait_ge(g_copied if s == 0 else multiplied, f * 4 if s == 0 else f)
                    pe.wait_ge(added, outs)
                    pe.wait_ge(K.split_done[s], j + 1)
                    accumulate(nc, K, thirds(K.ps, s), s, lambda k, at, n: hi[:, k, at:at + n],
                               lambda k, at, n: lo[:, k, at:at + n]).then_inc(used[s], 1)

            def down(f, j, outs):
                pe.wait_ge(hid_made, f)
                for t in range(KD):
                    if t < 2:
                        pe.wait_ge(g_copied if t == 0 else multiplied, f * 4 + 4 if t == 0 else f + 1)
                    else:
                        pe.wait_ge(added, outs + t - 1)
                    if t % DOWN_F == 0:
                        pe.wait_ge(K.split_done[t // DOWN_F], j + 1)
                    mm = accumulate(nc, K, thirds(K.ps, t % 2), t // DOWN_F, lambda k, at, n: hid_hi[:, k, at:at + n],
                                    lambda k, at, n: hid_lo[:, k, at:at + n],
                                    tiles=[2 * (t % DOWN_F), 2 * (t % DOWN_F) + 1])
                    mm.then_inc(down_done, 1)
                    if t % DOWN_F == DOWN_F - 1:
                        nc.tensor.drain().then_inc(used[t // DOWN_F], 1)

            up(0, pair(0, 0), 0)
            up(1, pair(0, 2), 0)
            with pe.Fori(1, STEPS) as i:
                up(2 * i, pair(i, 0), i * KD - KD)
                down(2 * i, pair(i, 1), i * KD - KD)
                up(2 * i + 1, pair(i, 2), i * KD)
            pe.wait_ge(hid_made, KF)
            for t in range(KD):
                if t < 2:
                    pe.wait_ge(g_copied if t == 0 else multiplied, 4 * KF if t == 0 else KF)
                else:
                    pe.wait_ge(added, (STEPS - 1) * KD + t - 1)
                if t % DOWN_F == 0:
                    pe.wait_ge(K.split_done[t // DOWN_F], base + n_pairs)
                accumulate(nc, K, thirds(K.ps, t % 2), t // DOWN_F, lambda k, at, n: hid_hi[:, k, at:at + n],
                           lambda k, at, n: hid_lo[:, k, at:at + n],
                           tiles=[2 * (t % DOWN_F), 2 * (t % DOWN_F) + 1]).then_inc(down_done, 1)
            pe.wait_ge(down_done, STEPS * KD)
            for s in range(2):
                pe.sem_inc(used[s], 1)

        @block.scalar
        def _(act):
            def up(f, j):
                act.wait_ge(used[0], j + 1)
                act.wait_ge(tap_done, f * 6)
                act.wait_ge(kept, f * 2)
                nc.scalar.activation(piece(g_prompt, FPAD, 2 * THIRD, 2), K.ps[:, 0:2, 0:THIRD], ACT.Identity
                                     ).then_inc(g_copied, 1)
                nc.scalar.activation(g_prompt[:, FPAD + 2 * THIRD:], K.ps[:, 2, 0:SEQ % THIRD], ACT.Identity
                                     ).then_inc(g_copied, 1)
                nc.scalar.activation(g_sample[:, :, FPAD:], K.ps[:, 2, SEQ % THIRD:T % THIRD].rearrange(
                    "p (b s) -> p b s", b=DEC_B), ACT.Identity).then_inc(g_copied, 1)
                nc.scalar.activation(g_sample[:, :, 0:FPAD], hist[:, bass.ds(f, 1), :, :].rearrange(
                    "p a b w -> p (a b) w"), ACT.Identity).then_inc(g_copied, 1)
                act.wait_ge(tap_done, f * 6 + 6)
                nc.scalar.activation(conv[:, :], conv[:, :], ACT.Silu).then_inc(acted, 1)

            def high_half(f, slot, downs):
                act.wait_ge(multiplied, f + 1)
                act.wait_ge(down_done, downs)
                nc.scalar.activation(hid_hi[:, slot, :], hid[:, :], ACT.Identity).then_inc(hid_hi_made, 1)

            act.wait_ge(hist_in, 16)
            up(0, pair(0, 0))
            high_half(0, 0, 0)
            up(1, pair(0, 2))
            high_half(1, 1, 0)
            with act.Fori(1, STEPS) as i:
                up(2 * i, pair(i, 0))
                high_half(2 * i, 0, i * KD)
                up(2 * i + 1, pair(i, 2))
                high_half(2 * i + 1, 1, i * KD)

        @block.gpsimd
        def _(pool):
            split_units(nc, pool, K, n_pairs - 1)

        @block.vector
        def _(dve):
            def up(f, j):
                dve.wait_ge(g_copied, f * 4 + 4)
                nc.vector.tensor_copy(last[:, bass.ds(f, 1), 0, :].rearrange("p a w -> p (a w)"),
                                      g_prompt[:, SEQ:]).then_inc(kept, 1)
                nc.vector.tensor_copy(last[:, bass.ds(f, 1), 1:, :].rearrange("p a b w -> p (a b) w"),
                                      g_sample[:, :, DEC_S:]).then_inc(kept, 1)
                for w in range(FFN_W):
                    scale = K.vecs[:, bass.ds(f * FFN_W + (VEC_AT["w_fdw"] + w), 1)]
                    in_p, in_s = g_prompt[:, w:w + SEQ], g_sample[:, :, w:w + DEC_S]
                    if w == 0:
                        dve.wait_ge(multiplied, f)
                        bias = K.vecs[:, bass.ds(f + VEC_AT["b_fdw"], 1)]
                        nc.vector.tensor_scalar(conv[:, 0:SEQ], in_p, scale, bias, ALU.mult, ALU.add
                                                ).then_inc(tap_done, 1)
                        nc.vector.tensor_scalar(conv_s, in_s, scale, bias, ALU.mult, ALU.add).then_inc(tap_done, 1)
                        continue
                    dve.wait_ge(tap_done, f * 6 + (2 * w - 1))
                    nc.vector.scalar_tensor_tensor(conv[:, 0:SEQ], in_p, scale, conv[:, 0:SEQ], ALU.mult, ALU.add
                                                   ).then_inc(tap_done, 1)
                    dve.wait_ge(tap_done, f * 6 + 2 * w)
                    nc.vector.scalar_tensor_tensor(conv_s, in_s, scale, conv_s, ALU.mult, ALU.add
                                                   ).then_inc(tap_done, 1)
                dve.wait_ge(acted, f + 1)
                dve.wait_ge(used[1], j + 1)
                dve.wait_ge(hid_made, f)
                for acc, at, n, a in pieces(K.ps, 1):
                    ins = nc.vector.tensor_tensor(piece(hid, at, n, a), acc, piece(conv, at, n, a), ALU.mult)
                ins.then_inc(multiplied, 1)

            def low_half(f, slot):
                dve.wait_ge(hid_hi_made, f + 1)
                nc.vector.tensor_tensor(hid_lo[:, slot, :], hid[:, :], hid_hi[:, slot, :].bitcast(F32), ALU.subtract
                                        ).then_inc(hid_made, 1)

            def add_down(outs):
                for t in range(KD):
                    dve.wait_ge(down_done, outs + t + 1)
                    for acc, at, n, a in pieces(K.ps, t % 2):
                        y_at = piece(y[:, t, :], at, n, a)
                        ins = nc.vector.tensor_tensor(y_at, acc, y_at, ALU.add)
                    ins.then_inc(added, 1)

            nc.vector.memset(g_prompt[:, 0:FPAD], 0.0).then_inc(padded, 1)
            nc.vector.memset(y[:, :, :], 0.0).then_inc(padded, 1)
            dve.wait_ge(padded, 2)
            up(0, pair(0, 0))
            low_half(0, 0)
            up(1, pair(0, 2))
            low_half(1, 1)
            with dve.Fori(1, STEPS) as i:
                dve.wait_ge(added, i * KD - KD)
                up(2 * i, pair(i, 0))
                add_down(i * KD - KD)
                low_half(2 * i, 0)
                up(2 * i + 1, pair(i, 2))
                low_half(2 * i + 1, 1)
            dve.wait_ge(added, (STEPS - 1) * KD)
            add_down((STEPS - 1) * KD)
    K.pair += n_pairs
    K.fed += n_pairs - 1


def build(nc, A):
    K = Names()
    K.A = A
    with ExitStack() as top:
        def sb(stack, name, shape, dt=F32, side="left"):
            return stack.enter_context(nc.sbuf_tensor(name, shape, dt, side=side))

        K.ps = top.enter_context(nc.psum_tensor("ps", [P, 8, 512], F32))
        K.s_load = top.enter_context(nc.semaphore("s_load"))
        K.unit_in, K.hi_done, K.split_done, K.unit_used = (
            [top.enter_context(nc.semaphore(f"{x}{s}")) for s in range(2)]
            for x in ("unit_in", "hi_done", "split_done", "unit_used"))
        K.may_split, K.may_fetch = (top.enter_context(nc.semaphore(x)) for x in ("may_split", "may_fetch"))
        K.pair = K.fed = 0
        K.x = sb(top, "x", [P, KD, T])
        K.raw = sb(top, "raw", [P, 2, KD * P])
        K.w_hi, K.w_lo = (sb(top, n, [P, 2, KD * P], F32R) for n in ("w_hi", "w_lo"))
        K.vecs = sb(top, "vecs", [P, N_VEC])
        K.ident, K.ones, K.causal = (sb(top, n, [P, P]) for n in ("ident", "ones", "causal"))
        K.pages, K.part, K.page_rows = (sb(top, n, [P, DEC_B], I32) for n in ("pages", "part", "page_rows"))
        K.eps = sb(top, "eps", [P, 1])

        def halves_of_x(stack, name):
            return [sb(stack, f"{name}_{h}", [P, KD, T], F32R, "right") for h in ("hi", "lo")]

        with ExitStack() as mixed:
            with ExitStack() as mixer:
                K.qlat = sb(mixer, "qlat", [P, KC * DEC_B, HEADS * DEC_S], F32, "right")[:, :, :].rearrange(
                    "p (l b) (h s) -> p l b h s", l=KC, h=HEADS)
                K.qpe = sb(mixer, "qpe", [P, DEC_B, HEADS * DEC_S], F32, "right")[:, :, :].rearrange(
                    "p b (h s) -> p b h s", h=HEADS)
                K.wuv = sb(mixer, "wuv", [P, KC, HEADS * VH], F32, "right")
                K.kh = sb(mixer, "kh", [P, T], F32, "right")
                K.c = sb(mixer, "c", [P, KC, T], F32, "right")
                with ExitStack() as prompt:
                    with ExitStack() as conv:
                        with ExitStack() as latents:
                            K.lat = sb(latents, "lat", [P, KQ + KC + 1, T], F32, "right")
                            K.rope = sb(conv, "rope", [P, T])
                            load_stage(nc, K, A)
                            with ExitStack() as proj:
                                h = halves_of_x(proj, "h")
                                norm_stage(nc, K, "pre_mix", K.x, KD, T, "g_pre_mix", None, D_MODEL, split=h,
                                           prefetch=True)
                                linear_stage(nc, K, "latents", K.lat, KQ + KC + 1, h, last=False)
                                K.u_prompt = sb(conv, "u_prompt", [P, 2 * KU, CPAD + 512])
                                K.u_sample = sb(conv, "u_sample", [P, KU * DEC_B, CPAD + DEC_S])
                                glu_stage(nc, K, h)
                            rope_k_stage(nc, K)
                            K.qn = sb(conv, "qn", [P, KQ, T])
                            norm_stage(nc, K, "q_norm", K.lat[:, 0:KQ, :], KQ, T, "g_q_a", K.qn, Q_LORA)

                            def store_latents(sp, stored):
                                sp.dma_start(A.kv_latent_t, K.c[:, :, :]).then_inc(stored, 16)
                                return 1

                            norm_stage(nc, K, "kv_norm", K.lat[:, KQ:KQ + KC, :], KC, T, "g_kv_a", K.c, KV_LORA,
                                       store=store_latents)
                        K.cv_prompt = sb(prompt, "cv_prompt", [P, 2 * KU, 512], F32, "right")
                        K.cv_sample = sb(prompt, "cv_sample", [P, KU * DEC_B, DEC_S], F32, "right")
                        K.attn = sb(prompt, "attn", [P, HEADS // 2 * SEQ], F32, "right")
                        K.v = sb(conv, "v", [P, QT, HEADS * VH])
                        value_stage(nc, K)
                        prompt_attention_stage(nc, K)
                    K.mix = sb(mixed, "mix", [P, KD, T])
                    gather_mix_stage(nc, K)
                    norm_stage(nc, K, "conv_norm", K.mix[:, KU:, :], KU, T, "g_cln", K.mix[:, KU:, :], D_CONV,
                               center=True, bias="b_cln", func=ACT.Silu, prefetch=True)
                K.olat = sb(mixer, "olat", [P, KC, HEADS, SAMPLE], F32, "right")
                paged_attention_stage(nc, K)
                sample_value_stage(nc, K)
            m = sb(mixed, "m", [P, KD, T])
            with ExitStack() as proj:
                linear_stage(nc, K, "out", m, KD, halves_of_x(proj, "mix"), src=K.mix)
            norm_stage(nc, K, "post_mix", m, KD, T, "g_post_mix", K.x, D_MODEL, add_to=K.x, prefetch=True)
        with ExitStack() as cross:
            with ExitStack() as keys:
                mem_k = sb(keys, "mem_k", [P, KD, N_MEM], F32, "right")
                mem_v = sb(keys, "mem_v", [P, 2, D_MODEL], F32, "right")
                xq_sample = sb(keys, "xq_sample", [P, KD, SAMPLE], F32, "right")
                with ExitStack() as memory:
                    mem = sb(memory, "mem", [P, KD, N_MEM])
                    mem_halves = [sb(memory, f"mem_{x}", [P, KD, N_MEM], F32R) for x in ("hi", "lo")]
                    mem_in = memory.enter_context(nc.semaphore("mem_in"))
                    with nc.Block() as block:
                        @block.sync
                        def _(sp):
                            sp.dma_start(mem[:, :, :], A.mem_t).then_inc(mem_in, 16)
                            sp.wait_ge(mem_in, 16)
                    norm_stage(nc, K, "mem_norm", mem, KD, N_MEM, "g_mem", None, D_MODEL, split=mem_halves)
                    memory_stage(nc, K, mem_halves, mem_k, mem_v)
                with ExitStack() as proj:
                    h = halves_of_x(proj, "hx")
                    norm_stage(nc, K, "pre_x", K.x, KD, T, "g_pre_x", None, D_MODEL, split=h, prefetch=True)
                    xo = sb(cross, "xo", [P, KD, T])
                    prompt_cross_stage(nc, K, h, mem_k, mem_v, xo, xq_sample)
                sample_cross_stage(nc, K, xo, xq_sample)
            xz = sb(cross, "xz", [P, KD, T])
            with ExitStack() as proj:
                linear_stage(nc, K, "xo", xz, KD, halves_of_x(proj, "xo"), src=xo)
            norm_stage(nc, K, "post_x", xz, KD, T, "g_post_x", K.x, D_MODEL, add_to=K.x)
        with ExitStack() as ffn:
            h = halves_of_x(ffn, "hf")
            norm_stage(nc, K, "pre_ffn", K.x, KD, T, "g_pre_ffn", None, D_MODEL, split=h, prefetch=True)
            y = sb(ffn, "y", [P, KD, T])
            ffn_stage(nc, K, h, y)

            def store_y(sp, stored):
                sp.dma_start(A.y_t, K.x[:, :, :]).then_inc(stored, 16)
                return 1

            norm_stage(nc, K, "post_ffn", y, KD, T, "g_post_ffn", K.x, D_MODEL, add_to=K.x, store=store_y)


OUTS = {
    "y_t": [P, KD, T], "kv_latent_t": [P, KC, T], "k_rope_t": [ROPE, T],
    "conv_prompt_t": [KU, P, CPAD], "conv_sample_t": [KU, P, DEC_B, CPAD],
    "ffn_state_t": [P, KF, 1 + DEC_B, FPAD], "mem_k_t": [P, KD, N_MEM], "mem_v_t": [P, 2, D_MODEL],
}


def kernel(**inputs):
    import numpy as np
    import concourse.bacc as bacc
    from concourse.bass_utils import run_bass_kernel_spmd

    a = {k: np.asarray(v) for k, v in inputs.items()}
    w = {k: v[0] for k, v in a.items() if k[0:2] in ("w_", "g_", "b_")}

    def by_feature(rows):
        return rows.reshape(rows.shape[0], -1, P).transpose(2, 1, 0)

    def tiles(m):
        k, f = m.shape
        return m.reshape(k // P, P, f // P, P).transpose(2, 1, 0, 3).reshape(f // P, P, k)

    def columns(v):
        return v.reshape(-1, P, int(v.size // v.shape[0])).transpose(1, 0, 2).reshape(P, -1)

    d = {}
    d["x_t"] = by_feature(np.concatenate([a["x_prompt"][0], a["x_sample"].reshape(SAMPLE, D_MODEL)]))
    d["mem_t"] = by_feature(a["mem_prompt"][0])
    twice = np.repeat(np.arange(KU), 2)
    per_feature = dict(w, w_fdw=w["w_fdw"].T,
                       w_dw=w["w_dw"].T.reshape(KU, P, CONV_W)[twice].reshape(-1, CONV_W),
                       b_dw=w["b_dw"].reshape(KU, P)[twice].reshape(-1))
    d["vecs"] = np.concatenate([columns(per_feature[n]) for n, _ in VEC_SIZES], axis=1)

    pos = np.concatenate([np.arange(SEQ), PAST + np.tile(np.arange(DEC_S), DEC_B)]).astype(np.float32)
    half = ROPE // 2
    inv = (np.float32(10000.0) ** (-np.arange(half, dtype=np.float32) / np.float32(half))).astype(np.float32)
    ang = (pos[None, :] * inv[:, None]).astype(np.float32)
    cos, sin = np.cos(ang), np.sin(ang)
    d["rope"] = np.concatenate([cos, cos, -sin, sin]).astype(np.float32)
    d["ident"] = np.eye(P, dtype=np.float32)
    d["causal"] = np.triu(np.full((P, P), -1e30, np.float32), 1)
    same = np.eye(DEC_B, dtype=bool)[None, :, :, None] & np.tril(np.ones((DEC_S, DEC_S), bool))[:, None, None, :]
    mask = np.where(same, 0.0, -1e30).astype(np.float32)
    d["new_mask"] = np.tile(mask.reshape(DEC_S, -1), (HEADS, 1))
    d["part"] = np.tile((np.arange(P, dtype=np.int32) % PARTS)[:, None], (1, DEC_B))

    def swapped(cols):
        return np.concatenate([cols[..., half:], cols[..., :half]], axis=-1)

    cuts = np.cumsum([Q_LORA, KV_LORA, ROPE, D_CONV])
    wq, wc, wpe, wa, wb = np.split(w["w_in"], cuts, axis=1)
    glu = np.concatenate([x for k in range(KU) for x in (wb[:, k * P:(k + 1) * P], wa[:, k * P:(k + 1) * P])], axis=1)
    units = [tiles(np.concatenate([wq, wc, wpe, wpe, wpe, swapped(wpe), glu], axis=1)), tiles(w["w_out"]),
             np.stack([tiles(w["w_xk"]), tiles(w["w_xv"])], axis=1).reshape(2 * KD, P, D_MODEL),
             tiles(w["w_xq"]), tiles(w["w_xo"])]
    heads = w["w_q_b"].reshape(KQ, P, HEADS, NOPE + ROPE)
    heads = np.concatenate([heads, swapped(heads[..., NOPE:])], axis=-1).transpose(2, 1, 0, 3).reshape(HEADS, P, -1)
    uk = w["w_uk"].reshape(KC, P, HEADS, NOPE).transpose(2, 1, 0, 3).reshape(HEADS, P, -1)
    uk_t = w["w_uk"].transpose(1, 2, 0)
    d["w_head_t"] = np.concatenate([heads, uk, np.concatenate([uk_t, uk_t], axis=1)], axis=2)
    d["w_uv_t"] = w["w_uv"].reshape(KC, P, HEADS * VH).transpose(1, 0, 2)
    value, gate = np.split(w["w_up"], 2, axis=1)
    up = np.stack([tiles(gate), tiles(value)], axis=1)
    down = w["w_down"].reshape(KF // 2, 2, P, KD // DOWN_F, DOWN_F, P).transpose(0, 3, 2, 4, 1, 5)
    down = down.reshape(KF // 2, KD // DOWN_F, P, D_MODEL)
    units += [up[0], up[1]]
    for i in range(1, KF // 2):
        units += [up[2 * i], down[i - 1], up[2 * i + 1]]
    d["units"] = np.concatenate(units + [down[-1]])

    d["cache"] = np.concatenate([a["cache_kv_latent"][0].reshape(-1, PER_ROW * KV_LORA),
                                 a["cache_k_rope"][0].reshape(-1, PER_ROW * ROPE)], axis=1)
    d["pages"] = np.repeat(a["page_table"].T, PARTS, axis=0)
    d["cache_k_t"] = a["cache_mem_k"][0].reshape(DEC_B, N_MEM, KD, P).transpose(0, 3, 2, 1)
    d["cache_v_t"] = a["cache_mem_v"][0].reshape(DEC_B, 2, P, D_MODEL).transpose(0, 2, 1, 3)
    d["state_conv_t"] = a["state_conv"][0].reshape(DEC_B, CPAD, KU, P).transpose(2, 3, 0, 1)
    d["state_ffn_t"] = a["state_ffn_conv"][0].reshape(DEC_B, FPAD, KF, P).transpose(3, 2, 0, 1)

    nc = bacc.Bacc("TRN2", target_bir_lowering=False, num_devices=1)
    A, arrays = Names(), {}
    for name, arr in d.items():
        arr = np.ascontiguousarray(arr)
        arrays[f"in_{name}"] = arr
        A.__dict__[name] = nc.dram_tensor(f"in_{name}", arr.shape, mybir.dt.from_np(arr.dtype),
                                          kind="ExternalInput").ap()
    for name, shape in OUTS.items():
        A.__dict__[name] = nc.dram_tensor(f"out_{name}", shape, F32, kind="ExternalOutput").ap()
    build(nc, A)
    got = run_bass_kernel_spmd(nc, [arrays], core_ids=[0]).results[0]
    r = {name: np.asarray(got[f"out_{name}"]) for name in OUTS}

    def rows(t):
        return t.transpose(2, 1, 0).reshape(t.shape[2], -1)

    y, c, pe = rows(r["y_t"]), rows(r["kv_latent_t"]), r["k_rope_t"].T
    ffn = r["ffn_state_t"].transpose(2, 3, 1, 0).reshape(1 + DEC_B, FPAD, D_FF)
    return (
        y[None, :SEQ], y[SEQ:].reshape(DEC_B, DEC_S, D_MODEL),
        c[None, None, :SEQ], pe[None, None, :SEQ],
        r["conv_prompt_t"].transpose(2, 0, 1).reshape(1, 1, CPAD, D_CONV), ffn[None, 0:1],
        rows(r["mem_k_t"]).reshape(1, 1, N_MEM, XH, XD),
        r["mem_v_t"].transpose(1, 0, 2).reshape(1, 1, N_MEM, XH, XD),
        c[SEQ:].reshape(1, DEC_B, DEC_S, KV_LORA), pe[SEQ:].reshape(1, DEC_B, DEC_S, ROPE),
        r["conv_sample_t"].transpose(2, 3, 0, 1).reshape(1, DEC_B, CPAD, D_CONV), ffn[None, 1:],
    )
```
